# Optimizing a Trainium2 kernel written in Bass

```python
import math
import jax, jax.numpy as jnp
from jax import lax
import numpy as np

D_MODEL = 1024
BATCH = 1
SEQ = 512
DEPTH = 2

D_FF = 2816
EPS = 1e-6
FOURIER_GROUPS = 8
FOURIER_GROUP_DIM = 128
FOURIER_WIDTH = FOURIER_GROUPS * FOURIER_GROUP_DIM
DIL_PAIRS = ((128, 1), (512, 4), (2048, 16))
DIL_HEADS_PER_GROUP = 2
DIL_HEAD_DIM = 64
DIL_HEADS = DIL_HEADS_PER_GROUP * len(DIL_PAIRS)
DIL_WIDTH = DIL_HEADS * DIL_HEAD_DIM
DIL_OUT_WIDTH = DIL_HEADS_PER_GROUP * DIL_HEAD_DIM
DIFF_HEADS = 4
DIFF_HEAD_DIM = 64
DIFF_QK_WIDTH = DIFF_HEADS * 2 * DIFF_HEAD_DIM
DIFF_V_DIM = 2 * DIFF_HEAD_DIM
DIFF_V_WIDTH = DIFF_HEADS * DIFF_V_DIM
SUBLN_EPS = 1e-5
Q_BLOCK = 128
IN_WIDTH = FOURIER_WIDTH + 3 * DIL_WIDTH + 2 * DIFF_QK_WIDTH + DIFF_V_WIDTH
N_BRANCHES = 3
NUM_BUCKETS = 32
MAX_DISTANCE = 1024
N_BIAS_HEADS = DIL_HEADS + DIFF_HEADS
NEG_INF = -1e30


def rmsnorm(x, g, eps=EPS):
    xf = x.astype(jnp.float32)
    y = xf * lax.rsqrt(jnp.mean(xf * xf, axis=-1, keepdims=True) + eps)
    return (y * g.astype(jnp.float32)).astype(x.dtype)

def swiglu(h, w_gate, w_up, w_down):
    return (jax.nn.silu(h @ w_gate) * (h @ w_up)) @ w_down

def rel_bucket(rel):
    half = NUM_BUCKETS // 2
    max_exact = half // 2
    ret = jnp.where(rel > 0, half, 0)
    n = jnp.abs(rel)
    nf = jnp.maximum(n, 1).astype(jnp.float32)
    large = max_exact + (jnp.log(nf / max_exact) / math.log(MAX_DISTANCE / max_exact)
                         * (half - max_exact)).astype(jnp.int32)
    large = jnp.minimum(large, half - 1)
    return ret + jnp.where(n < max_exact, n, large)

def fourier_mix(a):
    Bsz, S, _ = a.shape
    ag = a.astype(jnp.float32).reshape(Bsz, S, FOURIER_GROUPS, FOURIER_GROUP_DIM)
    y = jnp.fft.fftn(ag, axes=(1, 3), norm="ortho").real
    return y.reshape(Bsz, S, FOURIER_WIDTH).astype(a.dtype)

def dilated_window_attention(q, k, v, bias_cols, window, dil):
    Bsz, S, H, dh = q.shape
    radius = window // (2 * dil)
    blk = radius
    L = S // dil
    nb = -(-L // blk)
    Lp = nb * blk

    def to_sub(t):
        t = t.reshape(Bsz, L, dil, H, dh).transpose(0, 2, 3, 1, 4)
        return jnp.pad(t, ((0, 0), (0, 0), (0, 0), (0, Lp - L), (0, 0)))

    def windows(t):
        tp = jnp.pad(to_sub(t), ((0, 0), (0, 0), (0, 0), (blk, blk), (0, 0)))
        tp = tp.reshape(Bsz, dil, H, nb + 2, blk, dh)
        return jnp.concatenate([tp[:, :, :, :-2], tp[:, :, :, 1:-1], tp[:, :, :, 2:]], axis=4)

    qs = to_sub(q).reshape(Bsz, dil, H, nb, blk, dh).astype(jnp.float32)
    kw = windows(k).astype(jnp.float32)
    vw = windows(v).astype(jnp.float32)

    i = jnp.arange(blk)[:, None]
    m = jnp.arange(3 * blk)[None, :]
    rel_t = m - blk - i
    bias = bias_cols[rel_bucket(rel_t * dil)].astype(jnp.float32)
    bias = jnp.transpose(bias, (2, 0, 1))
    tk = (jnp.arange(nb)[:, None, None] - 1) * blk + m[None]
    valid = (jnp.abs(rel_t) <= radius)[None] & (tk >= 0) & (tk < L)

    logits = jnp.einsum('bdhjqc,bdhjkc->bdhjqk', qs, kw) * (dh ** -0.5)
    logits = logits + bias[None, None, :, None]
    logits = jnp.where(valid, logits, NEG_INF)
    lse = jax.nn.logsumexp(logits, axis=-1)
    p = jnp.exp(logits - lse[..., None])
    o = jnp.einsum('bdhjqk,bdhjkc->bdhjqc', p, vw)

    o = o.reshape(Bsz, dil, H, Lp, dh)[:, :, :, :L].transpose(0, 3, 1, 2, 4).reshape(Bsz, S, H, dh)
    lse = lse.reshape(Bsz, dil, H, Lp)[:, :, :, :L].transpose(0, 3, 1, 2).reshape(Bsz, S, H)
    return o, lse

def dilated_mixture(qb, kb, vb, rel_bias):
    Bsz, S, _ = qb.shape
    q = qb.reshape(Bsz, S, DIL_HEADS, DIL_HEAD_DIM)
    k = kb.reshape(Bsz, S, DIL_HEADS, DIL_HEAD_DIM)
    v = vb.reshape(Bsz, S, DIL_HEADS, DIL_HEAD_DIM)
    outs, lses = [], []
    for g, (window, dil) in enumerate(DIL_PAIRS):
        hs = slice(g * DIL_HEADS_PER_GROUP, (g + 1) * DIL_HEADS_PER_GROUP)
        o, lse = dilated_window_attention(q[:, :, hs], k[:, :, hs], v[:, :, hs],
                                          rel_bias[:, hs], window, dil)
        outs.append(o)
        lses.append(lse)
    o = jnp.stack(outs, axis=0)
    w = jax.nn.softmax(jnp.stack(lses, axis=0), axis=0)
    y = jnp.sum(w[..., None] * o, axis=0)
    return y.reshape(Bsz, S, DIL_OUT_WIDTH).astype(qb.dtype)

def diff_attention(qc, kc, vc, bias_cols, lam, subln_g, lam_init):
    Bsz, S, _ = qc.shape
    H, dh = DIFF_HEADS, DIFF_HEAD_DIM
    nq = S // Q_BLOCK
    qb = qc.reshape(Bsz, nq, Q_BLOCK, H, 2, dh).transpose(1, 0, 2, 3, 4, 5).astype(jnp.float32)
    kf = kc.reshape(Bsz, S, H, 2, dh).astype(jnp.float32)
    vf = vc.reshape(Bsz, S, H, DIFF_V_DIM).astype(jnp.float32)
    kpos = jnp.arange(S)
    scale = dh ** -0.5

    def one_block(args):
        j, qj = args
        qpos = j * Q_BLOCK + jnp.arange(Q_BLOCK)
        bias = bias_cols[rel_bucket(kpos[None, :] - qpos[:, None])].astype(jnp.float32)
        bias = jnp.transpose(bias, (2, 0, 1))
        logits = jnp.einsum('bqhmc,bkhmc->bhmqk', qj, kf) * scale + bias[None, :, None]
        p = jax.nn.softmax(logits, axis=-1)
        a = p[:, :, 0] - lam * p[:, :, 1]
        return jnp.einsum('bhqk,bkhe->bqhe', a, vf)

    o = lax.map(one_block, (jnp.arange(nq), qb))
    o = o.transpose(1, 0, 2, 3, 4).reshape(Bsz, S, H, DIFF_V_DIM)
    o = rmsnorm(o, subln_g, SUBLN_EPS) * (1.0 - lam_init)
    return o.reshape(Bsz, S, DIFF_V_WIDTH).astype(qc.dtype)

def first_inputs(seed: int = 0) -> dict:
    key = jax.random.key(seed)
    ks = jax.random.split(key, 26)

    def nrm(k, shape, fan_in):
        return jax.random.normal(k, shape, jnp.float32) * (fan_in ** -0.5)

    def gain(k, shape):
        return 1.0 + 0.05 * jax.random.normal(k, shape, jnp.float32)

    L = DEPTH
    return {
        "x": jax.random.normal(ks[0], (BATCH, SEQ, D_MODEL), jnp.float32),
        "g_ffn1": gain(ks[1], (L, D_MODEL)),
        "w_ffn1_gate": nrm(ks[2], (L, D_MODEL, D_FF), D_MODEL),
        "w_ffn1_up": nrm(ks[3], (L, D_MODEL, D_FF), D_MODEL),
        "w_ffn1_down": nrm(ks[4], (L, D_FF, D_MODEL), D_FF),
        "g_mix": gain(ks[5], (L, D_MODEL)),
        "w_in": nrm(ks[6], (L, D_MODEL, IN_WIDTH), D_MODEL),
        "w_gate": nrm(ks[7], (L, D_MODEL, N_BRANCHES * D_MODEL), D_MODEL),
        "b_gate": 0.02 * jax.random.normal(ks[8], (L, N_BRANCHES * D_MODEL), jnp.float32),
        "w_br_a": nrm(ks[9], (L, FOURIER_WIDTH, D_MODEL), FOURIER_WIDTH),
        "w_br_b": nrm(ks[10], (L, DIL_OUT_WIDTH, D_MODEL), DIL_OUT_WIDTH),
        "w_br_c": nrm(ks[11], (L, DIFF_V_WIDTH, D_MODEL), DIFF_V_WIDTH),
        "w_out": nrm(ks[12], (L, D_MODEL, D_MODEL), D_MODEL),
        "lam_q1": 0.1 * jax.random.normal(ks[13], (L, DIFF_HEAD_DIM), jnp.float32),
        "lam_k1": 0.1 * jax.random.normal(ks[14], (L, DIFF_HEAD_DIM), jnp.float32),
        "lam_q2": 0.1 * jax.random.normal(ks[15], (L, DIFF_HEAD_DIM), jnp.float32),
        "lam_k2": 0.1 * jax.random.normal(ks[16], (L, DIFF_HEAD_DIM), jnp.float32),
        "subln_g": gain(ks[17], (L, DIFF_V_DIM)),
        "rel_bias": 0.5 * jax.random.normal(ks[18], (NUM_BUCKETS, N_BIAS_HEADS), jnp.float32),
        "g_ffn2": gain(ks[19], (L, D_MODEL)),
        "w_ffn2_gate": nrm(ks[20], (L, D_MODEL, D_FF), D_MODEL),
        "w_ffn2_up": nrm(ks[21], (L, D_MODEL, D_FF), D_MODEL),
        "w_ffn2_down": nrm(ks[22], (L, D_FF, D_MODEL), D_FF),
        "g_final": gain(ks[23], (D_MODEL,)),
    }

def first_block(x, g_ffn1, w_ffn1_gate, w_ffn1_up, w_ffn1_down, g_mix, w_in, w_gate, b_gate,
              w_br_a, w_br_b, w_br_c, w_out, lam_q1, lam_k1, lam_q2, lam_k2, subln_g,
              rel_bias, g_ffn2, w_ffn2_gate, w_ffn2_up, w_ffn2_down, g_final):
    Bsz, S, D = x.shape
    c0 = FOURIER_WIDTH
    c1 = c0 + DIL_WIDTH
    c2 = c1 + DIL_WIDTH
    c3 = c2 + DIL_WIDTH
    c4 = c3 + DIFF_QK_WIDTH
    c5 = c4 + DIFF_QK_WIDTH
    for l in range(DEPTH):
        x = x + 0.5 * swiglu(rmsnorm(x, g_ffn1[l]), w_ffn1_gate[l], w_ffn1_up[l], w_ffn1_down[l])

        u = rmsnorm(x, g_mix[l])
        p = u @ w_in[l]
        a_in = p[..., :c0]
        qb, kb, vb = p[..., c0:c1], p[..., c1:c2], p[..., c2:c3]
        qc, kc, vc = p[..., c3:c4], p[..., c4:c5], p[..., c5:]

        y_a = fourier_mix(a_in) @ w_br_a[l]
        y_b = dilated_mixture(qb, kb, vb, rel_bias[:, :DIL_HEADS]) @ w_br_b[l]
        lam_init = 0.8 - 0.6 * math.exp(-0.3 * l)
        lam = (jnp.exp(jnp.sum(lam_q1[l].astype(jnp.float32) * lam_k1[l].astype(jnp.float32)))
               - jnp.exp(jnp.sum(lam_q2[l].astype(jnp.float32) * lam_k2[l].astype(jnp.float32)))
               + lam_init)
        y_c = diff_attention(qc, kc, vc, rel_bias[:, DIL_HEADS:], lam, subln_g[l], lam_init) @ w_br_c[l]

        gates = jax.nn.sigmoid(u @ w_gate[l] + b_gate[l]).reshape(Bsz, S, N_BRANCHES, D)
        merged = gates[:, :, 0] * y_a + gates[:, :, 1] * y_b + gates[:, :, 2] * y_c
        x = x + merged @ w_out[l]

        x = x + 0.5 * swiglu(rmsnorm(x, g_ffn2[l]), w_ffn2_gate[l], w_ffn2_up[l], w_ffn2_down[l])
    return rmsnorm(x, g_final)


SB_HEADS = 8
SB_HEAD_DIM = D_MODEL // SB_HEADS
SB_WIDTH = SB_HEADS * SB_HEAD_DIM
SB_BLOCK = 128
S5_WIDTH = D_MODEL // 2
S5_GROUP = 16
S5_GROUPS = S5_WIDTH // S5_GROUP
S5_STATE = 64
S5_DT_MIN = 1e-3
S5_DT_MAX = 1e-1
EVEN_IN = 4 * SB_WIDTH + 2 * S5_WIDTH
EVEN_MIX = SB_WIDTH + S5_WIDTH
GLA_HEADS = 4
GLA_KEY = D_MODEL // 2
GLA_VAL = D_MODEL
GLA_DK = GLA_KEY // GLA_HEADS
GLA_DV = GLA_VAL // GLA_HEADS
GLA_RANK = 16
GLA_TAU = 16.0
GLA_CHUNK = 64
ODD_IN = 2 * GLA_KEY + 2 * GLA_VAL + GLA_RANK
N_EVEN = (DEPTH + 1) // 2
N_ODD = DEPTH // 2


def rms_norm(x, g):
    xf = x.astype(jnp.float32)
    y = xf * lax.rsqrt(jnp.mean(xf * xf, axis=-1, keepdims=True) + EPS)
    return (y * g.astype(jnp.float32)).astype(x.dtype)

def stick_breaking_attention(q, k, v):
    bsz, L, h, dh = q.shape
    qf = q.astype(jnp.float32) * (dh ** -0.5)
    kf = k.astype(jnp.float32)
    vf = v.astype(jnp.float32)
    outs = []
    for blk in range(L // SB_BLOCK):
        q0 = blk * SB_BLOCK
        kend = q0 + SB_BLOCK
        z = jnp.einsum('bthd,bshd->bhts', qf[:, q0:kend], kf[:, :kend])
        t_idx = q0 + jnp.arange(SB_BLOCK)[:, None]
        s_idx = jnp.arange(kend)[None, :]
        causal = s_idx < t_idx
        log_beta = jax.nn.log_sigmoid(z)
        log_one_minus = jnp.where(causal, log_beta - z, 0.0)
        rest = lax.cumsum(log_one_minus, axis=3, reverse=True) - log_one_minus
        w = jnp.where(causal, jnp.exp(log_beta + rest), 0.0)
        outs.append(jnp.einsum('bhts,bshd->bthd', w, vf[:, :kend]))
    return jnp.concatenate(outs, axis=1).astype(q.dtype)

def s5_mixer(u, lam_re, lam_im, log_dt, b_re, b_im, c_re, c_im, d_skip, w_glu, b_glu):
    f32 = jnp.float32
    bsz, L, _ = u.shape
    uf = u.astype(f32).reshape(bsz, L, S5_GROUPS, S5_GROUP)
    lam = lax.complex(lam_re.astype(f32), lam_im.astype(f32))
    dt = jnp.exp(log_dt.astype(f32))[:, None]
    lam_bar = jnp.exp(lam * dt)
    bmat = lax.complex(b_re.astype(f32), b_im.astype(f32))
    b_bar = ((lam_bar - 1.0) / lam)[..., None] * bmat
    bu = lax.complex(jnp.einsum('gnp,blgp->blgn', b_bar.real, uf),
                     jnp.einsum('gnp,blgp->blgn', b_bar.imag, uf))
    a = jnp.broadcast_to(lam_bar, bu.shape)

    def combine(left, right):
        a_l, x_l = left
        a_r, x_r = right
        return a_r * a_l, a_r * x_l + x_r

    _, hstate = lax.associative_scan(combine, (a, bu), axis=1)
    y = (jnp.einsum('gpn,blgn->blgp', c_re.astype(f32), hstate.real)
         - jnp.einsum('gpn,blgn->blgp', c_im.astype(f32), hstate.imag)
         + d_skip.astype(f32) * uf)
    y = jax.nn.gelu(y.reshape(bsz, L, S5_WIDTH))
    y = y * jax.nn.sigmoid(y @ w_glu.astype(f32) + b_glu.astype(f32))
    return y.astype(u.dtype)

def gla_chunked(q, k, v, log_a):
    f32 = jnp.float32
    bsz, L, h, dk = q.shape
    dv = v.shape[-1]
    c = GLA_CHUNK
    n = L // c
    qc = (q.astype(f32) * (dk ** -0.5)).reshape(bsz, n, c, h, dk)
    kc = k.astype(f32).reshape(bsz, n, c, h, dk)
    vc = v.astype(f32).reshape(bsz, n, c, h, dv)
    g = jnp.cumsum(log_a.astype(f32).reshape(bsz, n, c, h, dk), axis=2)
    g_last = g[:, :, -1]
    q_dec = qc * jnp.exp(g)
    k_inv = kc * jnp.exp(-g)
    k_dec = kc * jnp.exp(g_last[:, :, None] - g)
    scores = jnp.einsum('bnthk,bnshk->bnhts', q_dec, k_inv)
    mask = jnp.tril(jnp.ones((c, c), dtype=bool))
    scores = jnp.where(mask, scores, 0.0)
    o_intra = jnp.einsum('bnhts,bnshv->bnthv', scores, vc)

    def step(state, inp):
        qd, kd, vv, gl = inp
        o = jnp.einsum('bthk,bhkv->bthv', qd, state)
        state = jnp.exp(gl)[..., None] * state + jnp.einsum('bthk,bthv->bhkv', kd, vv)
        return state, o

    s0 = jnp.zeros((bsz, h, dk, dv), f32)
    _, o_inter = lax.scan(step, s0, (jnp.moveaxis(q_dec, 1, 0), jnp.moveaxis(k_dec, 1, 0),
                                     jnp.moveaxis(vc, 1, 0), jnp.moveaxis(g_last, 1, 0)))
    o = o_intra + jnp.moveaxis(o_inter, 0, 1)
    return o.reshape(bsz, L, h, dv)

def second_inputs(seed: int = 0) -> dict:
    key = jax.random.key(seed)
    ks = jax.random.split(key, 24)
    f32 = jnp.float32
    nrm = lambda k, shape, s: jax.random.normal(k, shape, f32) * s
    x = jax.random.normal(ks[0], (BATCH, SEQ, D_MODEL), f32)
    even_norm_g = 1.0 + nrm(ks[1], (N_EVEN, D_MODEL), 0.02)
    even_w_in = nrm(ks[2], (N_EVEN, D_MODEL, EVEN_IN), D_MODEL ** -0.5)
    sb_q_norm_g = 1.0 + nrm(ks[3], (N_EVEN, SB_HEAD_DIM), 0.02)
    sb_k_norm_g = 1.0 + nrm(ks[4], (N_EVEN, SB_HEAD_DIM), 0.02)
    s5_lambda_re = -0.5 + nrm(ks[5], (N_EVEN, S5_GROUPS, S5_STATE), 0.01)
    n_idx = jnp.arange(S5_STATE, dtype=f32)
    s5_lambda_im = math.pi * n_idx + nrm(ks[6], (N_EVEN, S5_GROUPS, S5_STATE), 0.01)
    s5_log_dt = jax.random.uniform(ks[7], (N_EVEN, S5_GROUPS), f32,
                                   math.log(S5_DT_MIN), math.log(S5_DT_MAX))
    s5_b_re = nrm(ks[8], (N_EVEN, S5_GROUPS, S5_STATE, S5_GROUP), (2 * S5_GROUP) ** -0.5)
    s5_b_im = nrm(ks[9], (N_EVEN, S5_GROUPS, S5_STATE, S5_GROUP), (2 * S5_GROUP) ** -0.5)
    s5_c_re = nrm(ks[10], (N_EVEN, S5_GROUPS, S5_GROUP, S5_STATE), S5_STATE ** -0.5)
    s5_c_im = nrm(ks[11], (N_EVEN, S5_GROUPS, S5_GROUP, S5_STATE), S5_STATE ** -0.5)
    s5_d = nrm(ks[12], (N_EVEN, S5_GROUPS, S5_GROUP), 1.0)
    s5_w_glu = nrm(ks[13], (N_EVEN, S5_WIDTH, S5_WIDTH), S5_WIDTH ** -0.5)
    s5_b_glu = nrm(ks[14], (N_EVEN, S5_WIDTH), 0.02)
    even_w_out = nrm(ks[15], (N_EVEN, EVEN_MIX, D_MODEL), EVEN_MIX ** -0.5)
    odd_norm_g = 1.0 + nrm(ks[16], (N_ODD, D_MODEL), 0.02)
    odd_w_in = nrm(ks[17], (N_ODD, D_MODEL, ODD_IN), D_MODEL ** -0.5)
    gla_w_gate = nrm(ks[18], (N_ODD, GLA_RANK, GLA_KEY), GLA_RANK ** -0.5)
    gla_b_gate = nrm(ks[19], (N_ODD, GLA_KEY), 0.1)
    gla_o_norm_g = 1.0 + nrm(ks[20], (N_ODD, GLA_DV), 0.02)
    odd_w_out = nrm(ks[21], (N_ODD, GLA_VAL, D_MODEL), GLA_VAL ** -0.5)
    return {"x": x, "even_norm_g": even_norm_g, "even_w_in": even_w_in,
            "sb_q_norm_g": sb_q_norm_g, "sb_k_norm_g": sb_k_norm_g,
            "s5_lambda_re": s5_lambda_re, "s5_lambda_im": s5_lambda_im, "s5_log_dt": s5_log_dt,
            "s5_b_re": s5_b_re, "s5_b_im": s5_b_im, "s5_c_re": s5_c_re, "s5_c_im": s5_c_im,
            "s5_d": s5_d, "s5_w_glu": s5_w_glu, "s5_b_glu": s5_b_glu, "even_w_out": even_w_out,
            "odd_norm_g": odd_norm_g, "odd_w_in": odd_w_in, "gla_w_gate": gla_w_gate,
            "gla_b_gate": gla_b_gate, "gla_o_norm_g": gla_o_norm_g, "odd_w_out": odd_w_out}

def second_block(x, even_norm_g, even_w_in, sb_q_norm_g, sb_k_norm_g, s5_lambda_re, s5_lambda_im,
              s5_log_dt, s5_b_re, s5_b_im, s5_c_re, s5_c_im, s5_d, s5_w_glu, s5_b_glu, even_w_out,
              odd_norm_g, odd_w_in, gla_w_gate, gla_b_gate, gla_o_norm_g, odd_w_out):
    bsz, L, _ = x.shape
    for layer in range(DEPTH):
        i = layer // 2
        if layer % 2 == 0:
            h = rms_norm(x, even_norm_g[i])
            proj = h @ even_w_in[i]
            q, k, v, z_a, u, z_b = jnp.split(
                proj, [SB_WIDTH, 2 * SB_WIDTH, 3 * SB_WIDTH, 4 * SB_WIDTH,
                       4 * SB_WIDTH + S5_WIDTH], axis=-1)
            q = rms_norm(q.reshape(bsz, L, SB_HEADS, SB_HEAD_DIM), sb_q_norm_g[i])
            k = rms_norm(k.reshape(bsz, L, SB_HEADS, SB_HEAD_DIM), sb_k_norm_g[i])
            v = v.reshape(bsz, L, SB_HEADS, SB_HEAD_DIM)
            o_a = stick_breaking_attention(q, k, v).reshape(bsz, L, SB_WIDTH) * jax.nn.silu(z_a)
            o_b = s5_mixer(u, s5_lambda_re[i], s5_lambda_im[i], s5_log_dt[i], s5_b_re[i],
                           s5_b_im[i], s5_c_re[i], s5_c_im[i], s5_d[i], s5_w_glu[i],
                           s5_b_glu[i]) * jax.nn.silu(z_b)
            x = x + jnp.concatenate([o_a, o_b], axis=-1) @ even_w_out[i]
        else:
            h = rms_norm(x, odd_norm_g[i])
            proj = h @ odd_w_in[i]
            q, k, v, z, r = jnp.split(
                proj, [GLA_KEY, 2 * GLA_KEY, 2 * GLA_KEY + GLA_VAL,
                       2 * GLA_KEY + 2 * GLA_VAL], axis=-1)
            log_a = jax.nn.log_sigmoid((r @ gla_w_gate[i] + gla_b_gate[i]).astype(jnp.float32)) / GLA_TAU
            o = gla_chunked(q.reshape(bsz, L, GLA_HEADS, GLA_DK),
                            k.reshape(bsz, L, GLA_HEADS, GLA_DK),
                            v.reshape(bsz, L, GLA_HEADS, GLA_DV),
                            log_a.reshape(bsz, L, GLA_HEADS, GLA_DK))
            o = rms_norm(o, gla_o_norm_g[i]).astype(x.dtype).reshape(bsz, L, GLA_VAL)
            x = x + (o * jax.nn.silu(z)) @ odd_w_out[i]
    return x


def setup_inputs(seed=0):
    out = dict(first_inputs(seed))
    for name, value in second_inputs(seed + 1).items():
        if name != "x":
            out[name + "_2"] = value
    return out


def reference(
    x, g_ffn1, w_ffn1_gate, w_ffn1_up, w_ffn1_down, g_mix, w_in, w_gate, b_gate, w_br_a, w_br_b,
    w_br_c, w_out, lam_q1, lam_k1, lam_q2, lam_k2, subln_g, rel_bias, g_ffn2, w_ffn2_gate,
    w_ffn2_up, w_ffn2_down, g_final, even_norm_g_2, even_w_in_2, sb_q_norm_g_2, sb_k_norm_g_2,
    s5_lambda_re_2, s5_lambda_im_2, s5_log_dt_2, s5_b_re_2, s5_b_im_2, s5_c_re_2, s5_c_im_2,
    s5_d_2, s5_w_glu_2, s5_b_glu_2, even_w_out_2, odd_norm_g_2, odd_w_in_2, gla_w_gate_2,
    gla_b_gate_2, gla_o_norm_g_2, odd_w_out_2,
):
    x = first_block(
        x, g_ffn1, w_ffn1_gate, w_ffn1_up, w_ffn1_down, g_mix, w_in, w_gate, b_gate, w_br_a,
        w_br_b, w_br_c, w_out, lam_q1, lam_k1, lam_q2, lam_k2, subln_g, rel_bias, g_ffn2,
        w_ffn2_gate, w_ffn2_up, w_ffn2_down, g_final,
    )
    return second_block(
        x, even_norm_g_2, even_w_in_2, sb_q_norm_g_2, sb_k_norm_g_2, s5_lambda_re_2,
        s5_lambda_im_2, s5_log_dt_2, s5_b_re_2, s5_b_im_2, s5_c_re_2, s5_c_im_2, s5_d_2,
        s5_w_glu_2, s5_b_glu_2, even_w_out_2, odd_norm_g_2, odd_w_in_2, gla_w_gate_2,
        gla_b_gate_2, gla_o_norm_g_2, odd_w_out_2,
    )


_drawn_inputs = setup_inputs


def setup_inputs(seed=0):
    import zlib

    import numpy as np

    out = dict(_drawn_inputs(seed))
    spreads = {}
    factors = {'b_gate': 7.225,
     'even_norm_g_2': 4.133,
     'sb_q_norm_g_2': 8.0,
     'sb_k_norm_g_2': 8.0,
     's5_lambda_re_2': 64.0,
     's5_lambda_im_2': 30.704,
     's5_log_dt_2': 33.632,
     's5_b_re_2': 43.08,
     's5_b_im_2': 42.648,
     's5_c_re_2': 42.616,
     's5_c_im_2': 42.384,
     's5_b_glu_2': 30.571,
     'gla_o_norm_g_2': 46.472,
     'odd_norm_g_2': 4.069,
     'gla_b_gate_2': 3.806}
    for name, (base, spread) in spreads.items():
        noise = np.random.default_rng([zlib.crc32(name.encode()), seed]).standard_normal(out[name].shape)
        drawn = base * np.exp(spread * noise) if base else spread * noise
        out[name] = __import__('jax').numpy.asarray(drawn.astype(out[name].dtype))
    for name, factor in factors.items():
        out[name] = (out[name] * factor).astype(out[name].dtype)
    return out
```

```python
import math

import numpy as np
import concourse.bass as bass
from concourse import mybir
from contextlib import ExitStack

F32 = mybir.dt.float32
F32R = mybir.dt.float32r
ACT = mybir.ActivationFunctionType
ALU = mybir.AluOpType
AX = mybir.AxisListType

P = 128
S = 512
D = 1024
KT = D // P
ST = S // P
DEPTH = 2
FF = 2816
FT = FF // P
UNIT = 8 * P
GROUPS = 8
DIL = ((128, 1), (512, 4), (2048, 16))
N_DIL = len(DIL)
N_DIFF = 4
N_MAPS = 2 * N_DIL + N_DIFF
HD = 64
BUCKETS = 32
REL = 2 * S - 1
BW = S + P * (ST - 1)
NEG = -1e30
EPS = 1e-6
SUB_EPS = 1e-5
LAM_INIT = [0.8 - 0.6 * math.exp(-0.3 * l) for l in range(DEPTH)]

PAIR_FFN1 = 0
PAIR_DOWN1 = PAIR_FFN1 + FT
PAIR_FOUR = PAIR_DOWN1 + FT // 2
PAIR_BR_A = PAIR_FOUR + GROUPS // 2
PAIR_HEADS = PAIR_BR_A + KT
PAIR_MERGE = PAIR_HEADS + 2 * (N_DIL + N_DIFF)
PAIR_OUT = PAIR_MERGE + 3 * KT // 2
PAIR_FFN2 = PAIR_OUT + KT // 2
PAIR_DOWN2 = PAIR_FFN2 + FT
PAIRS_LAYER = PAIR_DOWN2 + FT // 2
PAIR_TAIL = DEPTH * PAIRS_LAYER
N_DH = N_DIL + N_DIFF
BIAS_LOADS = 32 * (N_DIL + 1) + 16 * (N_DIFF - 1)
N_T = 8 * N_DIL + 4 * N_DIFF
N_MIX = 13
N_X = KT * (3 * DEPTH + 4)
SB_HEADS = 8
S5_W = 512
UT = S5_W // P
S5_GROUPS, S5_STATE, S5_GROUP = 32, 64, 16
NST = S5_GROUPS * S5_STATE // P
LEVELS = 9
TAU = 16.0
GLA_HEADS = 4
CH = 64
NCH = S // CH
PAIR_U = PAIR_TAIL
PAIR_S5 = PAIR_U + UT // 2
PAIR_ZB = PAIR_S5 + NST // 4
PAIR_GLU = PAIR_ZB + UT // 2
PAIR_SB = PAIR_GLU + 1
PAIR_EOUT = PAIR_SB + 2 * SB_HEADS
PAIR_R = PAIR_EOUT + KT
PAIR_GLA = PAIR_R + 1
PAIR_OOUT = PAIR_GLA + 3 * GLA_HEADS
N_PAIRS = PAIR_OOUT + KT // 2
SCAN_LEVELS = 2 * LEVELS - 1
N_SCAN = 4 * (2 + 3 * SCAN_LEVELS)
LN_EXP = "natural_log_exp_and_others"
GATED = 8
CREDIT = 2


def build_program(nc, a):
    es = ExitStack()
    with es:
        def sb(name, shape, dt=F32):
            return es.enter_context(nc.sbuf_tensor(name, shape, dt))

        def sem(name):
            return es.enter_context(nc.semaphore(name))

        ARENA = 84 * 1024

        def at(name, kb, shape, dt=F32):
            return nc.alloc_sbuf_tensor_at(name, shape, dt, offset=ARENA + int(kb * 1024))

        x = sb("x", [P, KT, S])
        xn_hi = sb("xn_hi", [P, KT, S], F32R)
        xn_lo = sb("xn_lo", [P, KT, S], F32R)
        w_raw = [sb(f"w_raw{i}", [P, UNIT]) for i in range(2)]
        w_hi = [sb(f"w_hi{i}", [P, 8, P], F32R) for i in range(2)]
        w_lo = [sb(f"w_lo{i}", [P, 8, P], F32R) for i in range(2)]
        gains = sb("gains", [P, 9 * KT])
        gate_bias = sb("gate_bias", [P, DEPTH * 3 * KT])
        ident = sb("ident", [P, P])
        ones = sb("ones", [P, P])
        after = sb("after", [P, 2 * P])
        after_r = sb("after_r", [P, P], F32R)
        ones_r = sb("ones_r", [P, P], F32R)
        keep = sb("keep", [P, P], mybir.dt.uint32)
        eps = sb("eps", [P, 2])
        lam_neg = sb("lam_neg", [P, DEPTH])
        sub_gain = sb("sub_gain", [P, DEPTH])
        nmax = sb("nmax", [P, N_DIL + 1, 8])
        rsum = sb("rsum", [P, N_DIL + 1, 8])
        mixw = sb("mixw", [P, 5, 8])
        mixr = sb("mixr", [P, N_DIL, 8])
        rinv = sb("rinv", [P, 4, 2])
        s5_in = sb("s5_in", [P, 3, NST])
        s5_t = sb("s5_t", [P, 12, NST])
        s5_pow = sb("s5_pow", [P, 3, LEVELS, NST])
        s5_now = sb("s5_now", [P, 3, LEVELS, 4])
        s5_coef = sb("s5_coef", [P, 3, NST])
        s5_cols = sb("s5_cols", [P, 2, UT])
        tail_cols = sb("tail_cols", [P, 2 + 2 + GLA_HEADS])

        sq = at("sq", 24, [P, KT, S])
        xf = at("xf", 0, [P, KT, S])
        acc = at("acc", 128, [P, S])
        rlog = at("rlog", 130, [P, S])
        rstd = at("rstd", 132, [P, S])
        h_hi = at("h_hi", 40, [P, FT, S], F32R)
        h_lo = at("h_lo", 84, [P, FT, S], F32R)
        gated = [at(f"gated{j}", 128 + 2 * j, [P, S]) for j in range(2)]
        prod = [at(f"prod{j}", 132 + 2 * j, [P, S]) for j in range(2)]
        mg = at("mg", 0, [P, KT, S])
        yb_hi = at("yb_hi", 16, [P, 1, S], F32R)
        yb_lo = at("yb_lo", 18, [P, 1, S], F32R)
        yc_hi = at("yc_hi", 20, [P, N_DIFF, S], F32R)
        yc_lo = at("yc_lo", 28, [P, N_DIFF, S], F32R)
        ya_hi = at("ya_hi", 40, [P, GROUPS, S], F32R)
        ya_lo = at("ya_lo", 56, [P, GROUPS, S], F32R)
        dft_raw = at("dft_raw", 40, [P, 8 * S + 2 * P])
        dft_hi = at("dft_hi", 72, [P, 8 * S + 2 * P], F32R)
        dft_lo = at("dft_lo", 90, [P, 8 * S + 2 * P], F32R)
        fa_hi = [at(f"fa_hi{j}", 108 + 2 * j, [P, S], F32R) for j in range(2)]
        fa_lo = [at(f"fa_lo{j}", 112 + 2 * j, [P, S], F32R) for j in range(2)]
        fp_hi = [at(f"fp_hi{j}", 116 + 4 * j, [P, ST, 2 * P], F32R) for j in range(2)]
        fp_lo = [at(f"fp_lo{j}", 124 + 4 * j, [P, ST, 2 * P], F32R) for j in range(2)]
        sig = [at(f"sig{j}", 132 + 2 * j, [P, S]) for j in range(2)]
        q_hi = at("q_hi", 40, [P, S], F32R)
        q_lo = at("q_lo", 42, [P, S], F32R)
        k_hi = at("k_hi", 44, [P, S], F32R)
        k_lo = at("k_lo", 46, [P, S], F32R)
        v_hi = at("v_hi", 48, [P, ST, P], F32R)
        v_lo = at("v_lo", 50, [P, ST, P], F32R)
        logit = [at(f"logit{j}", 52 + 2 * j, [P, S]) for j in range(2)]
        prob = at("prob", 56, [P, 8, S])
        pt_hi = [at(f"pt_hi{m}", 72 + 8 * m, [P, ST, S], F32R) for m in range(2)]
        pt_lo = [at(f"pt_lo{m}", 88 + 8 * m, [P, ST, S], F32R) for m in range(2)]
        bias = [at(f"bias{m}", 104 + 4 * m, [P, BW]) for m in range(2)]
        og = at("og", 112, [P, N_DIL, 8, HD])
        ybf = at("ybf", 118, [P, 8, HD])
        ybt = at("ybt", 120, [P, 8, HD])
        amap = [at(f"amap{j}", 122 + 2 * j, [P, S]) for j in range(2)]
        amap0 = at("amap0", 126, [P, S])
        of = at("of", 128, [P, S])
        osq = at("osq", 130, [P, S])
        olog = at("olog", 130, [P, S])
        orstd = at("orstd", 132, [P, S])
        onorm = at("onorm", 134, [P, S])
        vf = at("vf", 136, [P, S])
        m_hi = at("m_hi", 40, [P, KT, S], F32R)
        m_lo = at("m_lo", 56, [P, KT, S], F32R)
        sigb = [at(f"sigb{j}", 72 + 2 * j, [P, S]) for j in range(2)]
        sigc = [at(f"sigc{j}", 76 + 2 * j, [P, S]) for j in range(2)]
        tmpb = [at(f"tmpb{j}", 80 + 2 * j, [P, S]) for j in range(2)]
        tmpc = [at(f"tmpc{j}", 84 + 2 * j, [P, S]) for j in range(2)]
        uf = at("uf", 0, [P, UT, S])
        u_hi = at("u_hi", 8, [P, UT, S], F32R)
        u_lo = at("u_lo", 16, [P, UT, S], F32R)
        bx = [at(f"bx{j}", 24 + 4 * j, [P, 2, S]) for j in range(2)]
        sc = [at(f"sc{j}", kb, [P, 2, S]) for j, kb in enumerate((32, 36, 124, 128))]
        st_hi = [at(f"st_hi{j}", kb, [P, 2, S], F32R) for j, kb in enumerate((40, 44, 84, 88))]
        st_lo = [at(f"st_lo{j}", kb, [P, 2, S], F32R) for j, kb in enumerate((48, 52, 92, 96))]
        yf = [at(f"yf{j}", 56 + 2 * j, [P, S]) for j in range(2)]
        ge = at("ge", 60, [P, UT, S])
        ge_hi = at("ge_hi", 68, [P, UT, S], F32R)
        ge_lo = at("ge_lo", 76, [P, UT, S], F32R)
        zb = at("zb", 84, [P, UT, S])
        glu = [at(f"glu{j}", 92 + 2 * j, [P, S]) for j in range(2)]
        ob_f = [at(f"ob_f{j}", 96 + 2 * j, [P, S]) for j in range(2)]
        eo_hi = at("eo_hi", 100, [P, SB_HEADS + UT, S], F32R)
        eo_lo = at("eo_lo", 0, [P, SB_HEADS + UT, S], F32R)
        sbq = [at(f"sbq{j}", 24 + 2 * j, [P, S]) for j in range(2)]
        sbs = [at(f"sbs{j}", 28 + 2 * j, [P, S]) for j in range(2)]
        sbl = [at(f"sbl{j}", 32 + 2 * j, [P, S]) for j in range(2)]
        sbn_hi = [at(f"sbn_hi{j}", 36 + 2 * j, [P, S], F32R) for j in range(2)]
        sbn_lo = [at(f"sbn_lo{j}", 40 + 2 * j, [P, S], F32R) for j in range(2)]
        sv_hi = at("sv_hi", 44, [P, ST, P], F32R)
        sv_lo = at("sv_lo", 46, [P, ST, P], F32R)
        svf = at("svf", 48, [P, S])
        za = [at(f"za{j}", 50 + 2 * j, [P, S]) for j in range(2)]
        zm = [at(f"zm{j}", 54 + 2 * j, [P, S]) for j in range(2)]
        ze = [at(f"ze{j}", 58 + 2 * j, [P, S]) for j in range(2)]
        lom = [at(f"lom{j}", 62 + 2 * j, [P, S]) for j in range(2)]
        lom_hi = at("lom_hi", 66, [P, ST, S], F32R)
        lom_lo = at("lom_lo", 74, [P, ST, S], F32R)
        ww = [at(f"ww{j}", 82 + 2 * j, [P, S]) for j in range(2)]
        w_hi_t = at("w_hi_t", 86, [P, ST, S], F32R)
        w_lo_t = at("w_lo_t", 124, [P, ST, S], F32R)
        eo = at("eo", 100, [P, SB_HEADS, S])
        ez = at("ez", 0, [P, SB_HEADS, S])
        r_hi = at("r_hi", 0, [P, S], F32R)
        r_lo = at("r_lo", 2, [P, S], F32R)
        gx = [at(f"gx{j}", 4 + 2 * j, [P, S]) for j in range(2)]
        ga = [at(f"ga{j}", 8 + 2 * j, [P, S]) for j in range(2)]
        gl = [at(f"gl{j}", 12 + 2 * j, [P, S]) for j in range(2)]
        gcum = at("gcum", 16, [P, GLA_HEADS, S])
        restart = at("restart", 24, [P, S])
        gexp = [at(f"gexp{j}", 28 + 2 * j, [P, S]) for j in range(3)]
        gdiff = at("gdiff", 34, [P, S])
        gend = at("gend", 36, [P, NCH])
        gq = [at(f"gq{j}", 38 + 2 * j, [P, S]) for j in range(3)]
        gq_hi = [at(f"gq_hi{j}", 44 + 2 * j, [P, S], F32R) for j in range(2)]
        gq_lo = [at(f"gq_lo{j}", 48 + 2 * j, [P, S], F32R) for j in range(2)]
        kd_hi = at("kd_hi", 52, [P, ST, P], F32R)
        kd_lo = at("kd_lo", 54, [P, ST, P], F32R)
        gv_hi = at("gv_hi", 56, [P, ST, 2 * P], F32R)
        gv_lo = at("gv_lo", 60, [P, ST, 2 * P], F32R)
        score = at("score", 64, [P, ST, P])
        score_hi = at("score_hi", 66, [P, ST, P], F32R)
        score_lo = at("score_lo", 68, [P, ST, P], F32R)
        state = [at(f"state{j}", 70 + j, [P, 2 * P]) for j in range(2)]
        state_hi = [at(f"state_hi{j}", j, [P, 2 * P], F32R) for j in range(NCH)]
        state_lo = [at(f"state_lo{j}", NCH + j, [P, 2 * P], F32R) for j in range(NCH)]
        gvf = [at(f"gvf{j}", 84 + 2 * j, [P, S]) for j in range(2)]
        gsq = [at(f"gsq{j}", 76 + 2 * j, [P, S]) for j in range(2)]
        grs = [at(f"grs{j}", 80 + 2 * j, [P, S]) for j in range(2)]
        go_hi = at("go_hi", 96, [P, KT, S], F32R)
        go_lo = at("go_lo", 112, [P, KT, S], F32R)
        go = at("go", 96, [P, KT, S])
        gz = at("gz", 112, [P, KT, S])
        gate = [at(f"gate{j}", 88 + 2 * j, [P, S]) for j in range(2)]
        gated_o = [at(f"gated_o{j}", 92 + 2 * j, [P, S]) for j in range(2)]
        onehot = at("onehot", 40, [BUCKETS + N_DIL, REL])
        relt = at("relt", 48, [BUCKETS + N_DIL, N_MAPS])
        table = at("table", 49, [N_MAPS, REL])
        lamv = at("lamv", 54, [P, 4 * DEPTH * HD])
        lamp = at("lamp", 56, [P, 2 * DEPTH * HD])
        lams = at("lams", 57, [P, 2 * DEPTH])
        lame = at("lame", 57.25, [P, 2 * DEPTH])
        lamd = at("lamd", 57.5, [P, DEPTH])

        ps = [es.enter_context(nc.psum_tensor(f"ps{i}", [P, S], F32)) for i in range(8)]

        bu_banks = ((0, 1), (2, 3), (5, 6), (7, 4))

        def kv_bank(c):
            return ps[4 + 2 * (c % 2) + c // 4][:, (c // 2 % 2) * 2 * P:(c // 2 % 2 + 1) * 2 * P]

        unit_loaded = [sem(f"unit_loaded{i}") for i in range(2)]
        unit_hi = sem("unit_hi")
        unit_lo = sem("unit_lo")
        unit_used = sem("unit_used")
        small_in = sem("small_in")
        consts_ready = sem("consts_ready")
        setup_step = sem("setup_step")
        table_ready = sem("table_ready")
        table_copied = sem("table_copied")
        table_out = sem("table_out")
        lam_exp = sem("lam_exp")
        x_ready = sem("x_ready")
        x_out = sem("x_out")
        sq_done = sem("sq_done")
        sum_step = sem("sum_step")
        ms_done = sem("ms_done")
        rlog_done = sem("rlog_done")
        rstd_done = sem("rstd_done")
        xf_done = sem("xf_done")
        xh_done = sem("xh_done")
        xn_done = sem("xn_done")
        gate_done = sem("gate_done")
        prod_done = sem("prod_done")
        hid_hi = sem("hid_hi")
        hid_lo = sem("hid_lo")
        dft_in = sem("dft_in")
        dft_hi_done = sem("dft_hi_done")
        dft_lo_done = sem("dft_lo_done")
        fa_hi_done = sem("fa_hi_done")
        fa_lo_done = sem("fa_lo_done")
        fp_mm = sem("fp_mm")
        fp_hi_done = sem("fp_hi_done")
        fp_lo_done = sem("fp_lo_done")
        fy_mm = sem("fy_mm")
        fy_hi_done = sem("fy_hi_done")
        fy_lo_done = sem("fy_lo_done")
        siga_done = sem("siga_done")
        mga_done = sem("mga_done")
        bias_in = sem("bias_in")
        vf_done = sem("vf_done")
        vt_done = sem("vt_done")
        qkv_hi = sem("qkv_hi")
        qkv_lo = sem("qkv_lo")
        s_done = sem("s_done")
        logit_done = sem("logit_done")
        nmax_done = sem("nmax_done")
        exp_done = sem("exp_done")
        amap_step = sem("amap_step")
        t_done = sem("t_done")
        pt_hi_done = sem("pt_hi_done")
        pt_lo_done = sem("pt_lo_done")
        o_done = sem("o_done")
        od_done = sem("od_done")
        ot_done = sem("ot_done")
        og_done = sem("og_done")
        mix_step = sem("mix_step")
        mix_exp = sem("mix_exp")
        ybt_done = sem("ybt_done")
        yb_hi_done = sem("yb_hi_done")
        yb_lo_done = sem("yb_lo_done")
        ov_done = sem("ov_done")
        osq_done = sem("osq_done")
        oms_done = sem("oms_done")
        olog_done = sem("olog_done")
        orstd_done = sem("orstd_done")
        onorm_done = sem("onorm_done")
        yc_hi_done = sem("yc_hi_done")
        yc_lo_done = sem("yc_lo_done")
        sigbc_done = sem("sigbc_done")
        merge_step = sem("merge_step")
        merged = sem("merged")
        m_hi_done = sem("m_hi_done")
        m_lo_done = sem("m_lo_done")

        s5_step = sem("s5_step")
        s5_dt = sem("s5_dt")
        s5_tables = sem("s5_tables")
        u_hi_done = sem("u_hi_done")
        u_lo_done = sem("u_lo_done")
        bu_mm = sem("bu_mm")
        bx_done = sem("bx_done")
        s5_now_set = sem("s5_now_set")
        scan_step = sem("scan_step")
        st_hi_done = sem("st_hi_done")
        st_lo_done = sem("st_lo_done")
        yf_done = sem("yf_done")
        ge_done = sem("ge_done")
        ge_hi_done = sem("ge_hi_done")
        ge_lo_done = sem("ge_lo_done")
        zb_done = sem("zb_done")
        glu_done = sem("glu_done")
        ob_step = sem("ob_step")
        ob_hi_done = sem("ob_hi_done")
        ob_lo_done = sem("ob_lo_done")
        masks_r = sem("masks_r")
        sbq_done = sem("sbq_done")
        sbms_done = sem("sbms_done")
        sblog_done = sem("sblog_done")
        sbr_done = sem("sbr_done")
        sbn_done = sem("sbn_done")
        sb_hi_done = sem("sb_hi_done")
        sb_lo_done = sem("sb_lo_done")
        sz_done = sem("sz_done")
        svf_done = sem("svf_done")
        svt_done = sem("svt_done")
        raw_done = sem("raw_done")
        gate_made = sem("gate_made")
        gated_f = sem("gated_f")
        gated_hi = sem("gated_hi")
        gated_lo = sem("gated_lo")
        z_done = sem("z_done")
        za_done = sem("za_done")
        ze_done = sem("ze_done")
        zl_done = sem("zl_done")
        zm_step = sem("zm_step")
        lom_done = sem("lom_done")
        lom_hi_done = sem("lom_hi_done")
        lom_lo_done = sem("lom_lo_done")
        rest_done = sem("rest_done")
        wlog_done = sem("wlog_done")
        w_exp_done = sem("w_exp_done")
        w_masked = sem("w_masked")
        wt_hi_done = sem("wt_hi_done")
        wt_lo_done = sem("wt_lo_done")
        sbo_done = sem("sbo_done")
        r_hi_done = sem("r_hi_done")
        r_lo_done = sem("r_lo_done")
        gx_step = sem("gx_step")
        ga_step = sem("ga_step")
        gcum_set = sem("gcum_set")
        gcum_done = sem("gcum_done")
        gd_done = sem("gd_done")
        gexp_done = sem("gexp_done")
        gq_done = sem("gq_done")
        gq_hi_done = sem("gq_hi_done")
        gq_lo_done = sem("gq_lo_done")
        kdt_done = sem("kdt_done")
        kd_hi_done = sem("kd_hi_done")
        kd_lo_done = sem("kd_lo_done")
        gvf_done = sem("gvf_done")
        gvt_done = sem("gvt_done")
        gv_hi_done = sem("gv_hi_done")
        gv_lo_done = sem("gv_lo_done")
        sc_mm = sem("sc_mm")
        score_done = sem("score_done")
        score_hi_done = sem("score_hi_done")
        score_lo_done = sem("score_lo_done")
        kv_done = sem("kv_done")
        state_done = sem("state_done")
        state_hi_done = sem("state_hi_done")
        state_lo_done = sem("state_lo_done")
        go_mm = sem("go_mm")
        gsq_done = sem("gsq_done")
        gms_done = sem("gms_done")
        grs_step = sem("grs_step")
        gz_done = sem("gz_done")

        block = es.enter_context(nc.Block())

        SMALL = 13

        @block.sync
        def _(sp):
            sp.dma_start(x[:, :, :], a["x"]).then_inc(small_in, 16)
            for dst, name in ((gains, "gains"), (gate_bias, "gate_bias"), (ident, "ident"),
                              (sub_gain, "sub_gain"), (after, "after"), (keep, "keep"), (onehot, "onehot"), (relt, "relt")):
                sp.dma_start(dst[:, :], a[name]).then_inc(small_in, 16)
            sp.dma_start(lamv[:, :], a["lam"].to_broadcast([P, 4 * DEPTH * HD])).then_inc(small_in, 16)
            sp.dma_start(s5_in[:, :, :], a["s5_in"]).then_inc(small_in, 16)
            sp.dma_start(s5_cols[:, :, :], a["s5_cols"]).then_inc(small_in, 16)
            sp.dma_start(tail_cols[:, :], a["tail_cols"]).then_inc(small_in, 16)
            for j in range(2):
                sp.dma_start(w_raw[j][:, :], a["weights"][j]).then_inc(unit_loaded[j], 16)
            with sp.Fori(1, N_PAIRS) as p:
                for j in range(2):
                    sp.wait_ge(unit_lo, 2 * p + j - 1)
                    sp.dma_start(w_raw[j][:, :], a["weights"][2 * p + j]).then_inc(unit_loaded[j], 16)
            sp.wait_ge(x_ready, N_X)
            sp.dma_start(a["out"], x[:, :, :]).then_inc(x_out, 16)
            sp.wait_ge(x_out, 16)

        @block.gpsimd
        def _(pool):
            with pool.Fori(0, N_PAIRS) as p:
                for j in range(2):
                    pool.wait_ge(unit_hi, 2 * p + j + 1)
                    pool.tensor_tensor(w_lo[j][:, :, :], w_raw[j][:, :].rearrange("p (k m) -> p k m", k=8),
                                       w_hi[j][:, :, :].bitcast(F32), ALU.subtract).then_inc(unit_lo, 1)

        @block.tensor
        def _(pe):
            def three(out, lh, ll, rh, rl, first, last):
                pe.matmul(out, lh, rh, start=first, stop=False)
                pe.matmul(out, lh, rl, start=False, stop=False)
                return pe.matmul(out, ll, rh, start=False, stop=last)

            def unit_arrived(pair, j):
                pe.wait_ge(unit_lo, 2 * pair + j + 1)

            def project(pair, j, out, in_hi, in_lo):
                unit_arrived(pair, j)
                for k in range(KT):
                    last = three(out, w_hi[j][:, k, :], w_lo[j][:, k, :], in_hi[:, k, :], in_lo[:, k, :],
                                 k == 0, k == KT - 1)
                last.then_inc(unit_used, 1)

            def norm(n):
                pe.wait_ge(sum_step, 7 * n + 7)
                pe.matmul(ps[7][:, :], ones[:, :], acc[:, :], start=True, stop=True).then_inc(ms_done, 1)

            def ffn_up(r, pair0, n):
                with pe.Fori(0, FT // 2) as i:
                    pe.wait_ge(xn_done, KT * (n + 1))
                    for j in range(2):
                        pe.wait_ge(prod_done, r * FT + 2 * i + j + 1)
                        project(pair0 + 2 * i + j, 0, ps[2 * j][:, :], xn_hi, xn_lo)
                        project(pair0 + 2 * i + j, 1, ps[2 * j + 1][:, :], xn_hi, xn_lo)

            def ffn_down(r, pair0):
                def tile(pair, j, f, first, last):
                    pe.wait_ge(hid_lo, CREDIT + r * FT + f + 1)
                    unit_arrived(pair, j)
                    for m in range(KT):
                        mm = three(ps[m][:, :], w_hi[j][:, m, :], w_lo[j][:, m, :],
                                   h_hi[:, f, :], h_lo[:, f, :], first, last)
                    mm.then_inc(unit_used, 1)
                pe.wait_ge(prod_done, CREDIT + (r + 1) * FT)
                tile(pair0, 0, 0, True, False)
                tile(pair0, 1, 1, False, False)
                with pe.Fori(1, FT // 2 - 1) as i:
                    for j in range(2):
                        tile(pair0 + i, j, 2 * i + j, False, False)
                tile(pair0 + FT // 2 - 1, 0, FT - 2, False, False)
                tile(pair0 + FT // 2 - 1, 1, FT - 1, False, True)

            def fourier(l):
                COS, SIN, CH = 0, 4 * S, 8 * S
                with pe.Fori(0, GROUPS // 2) as i:
                    pe.wait_ge(xn_done, KT * (3 * l + 2))
                    g0 = l * GROUPS + 2 * i
                    for j in range(2):
                        pe.wait_ge(fy_lo_done, g0 + j + 1)
                        project(l * PAIRS_LAYER + PAIR_FOUR + i, j, ps[j][:, :], xn_hi, xn_lo)
                    pe.wait_ge(dft_lo_done, l + 1)
                    for j in range(2):
                        pe.wait_ge(fa_lo_done, g0 + j + 1)
                        for t in range(ST):
                            out = ps[2 + 2 * j + t // 2][:, (t % 2) * 2 * P:(t % 2 + 1) * 2 * P]
                            last = three(out, fa_hi[j][:, t * P:(t + 1) * P], fa_lo[j][:, t * P:(t + 1) * P],
                                         dft_hi[:, CH:CH + 2 * P], dft_lo[:, CH:CH + 2 * P], True, True)
                        last.then_inc(fp_mm, 1)
                    for j in range(2):
                        pe.wait_ge(fp_lo_done, 2 * (g0 + j + 1))
                        for c in range(2):
                            for t in range(ST):
                                o = (COS, SIN)[c] + t * S
                                last = three(ps[j][:, :], fp_hi[j][:, t, c * P:(c + 1) * P],
                                             fp_lo[j][:, t, c * P:(c + 1) * P],
                                             dft_hi[:, o:o + S], dft_lo[:, o:o + S],
                                             c == 0 and t == 0, c == 1 and t == ST - 1)
                        last.then_inc(fy_mm, 1)

            def branch_a(l):
                with pe.Fori(0, KT // 2) as i:
                    pe.wait_ge(fy_lo_done, CREDIT + (l + 1) * GROUPS)
                    for j in range(2):
                        c = 2 * i + j
                        pair = l * PAIRS_LAYER + PAIR_BR_A + c
                        pe.wait_ge(mga_done, l * KT + c + 1)
                        project(pair, 0, ps[2 * j][:, :], xn_hi, xn_lo)
                        project(pair, 1, ps[2 * j + 1][:, :], ya_hi, ya_lo)

            def qkv(pair, n):
                u, k = divmod(n, KT)
                slot, tile = (u, k) if u < 2 else divmod(k, KT // 2)
                if tile == 0:
                    unit_arrived(pair + u // 2, slot)
                last = three(ps[u][:, :], w_hi[slot][:, tile, :], w_lo[slot][:, tile, :],
                             xn_hi[:, k, :], xn_lo[:, k, :], k == 0, k == KT - 1)
                if tile == (KT - 1 if u < 2 else KT // 2 - 1):
                    last.then_inc(unit_used, 1)

            def v_transposed(q):
                pe.wait_ge(vf_done, q + 1)
                for t in range(ST):
                    last = pe.transpose(ps[2][:, t * P:(t + 1) * P], vf[:, t * P:(t + 1) * P], ident[:, :])
                last.then_inc(vt_done, 1)

            def double_head(q, tile_of, transposed_ready, next_pair):
                for step in range(10):
                    if step < 8:
                        m, t = tile_of(step)
                        r = slice(HD * m, HD * m + HD)
                        if step == 0:
                            pe.wait_ge(qkv_lo, 3 * q + 2)
                        pe.wait_ge(logit_done, 8 * q + step + 1)
                        three(ps[3 + step % 2][:, :], q_hi[r, t * P:(t + 1) * P], q_lo[r, t * P:(t + 1) * P],
                              k_hi[r, :], k_lo[r, :], True, True).then_inc(s_done, 1)
                        if next_pair is not None:
                            for n in range(3 * step, 3 * step + 3):
                                if n == 2 * KT:
                                    pe.wait_ge(qkv_lo, 3 * q + 3)
                                qkv(next_pair, n)
                    if step >= 2:
                        transposed_ready(step - 2)

            def first_head(l):
                pe.wait_ge(mga_done, CREDIT + (l + 1) * KT)
                for n in range(3 * KT):
                    qkv(l * PAIRS_LAYER + PAIR_HEADS, n)
                v_transposed(l * N_DH)

            def dilated(l):
                with pe.Fori(0, N_DIL) as g:
                    q = l * N_DH + g
                    tq = l * N_T + 8 * g

                    def transposed(i):
                        pe.wait_ge(exp_done, CREDIT + 8 * q + i + 1)
                        pe.wait_ge(pt_lo_done, tq + i + 1)
                        for kb in range(ST):
                            last = pe.transpose(ps[5 + i % 2][:, kb * P:(kb + 1) * P],
                                                prob[:, i, kb * P:(kb + 1) * P], ident[:, :])
                        last.then_inc(t_done, 1)

                    double_head(q, lambda s: divmod(s, ST), transposed, l * PAIRS_LAYER + PAIR_HEADS + 2 * g + 2)
                    pe.wait_ge(qkv_lo, 3 * q + 3)
                    for m in range(2):
                        pe.wait_ge(pt_lo_done, CREDIT + tq + 4 * m + 4)
                        for kb in range(ST):
                            last = three(ps[(7, 3)[m]][:, :], v_hi[:, kb, :], v_lo[:, kb, :],
                                         pt_hi[m][:, kb, :], pt_lo[m][:, kb, :], kb == 0, kb == ST - 1)
                    last.then_inc(o_done, 1)
                    v_transposed(q + 1)
                    pe.wait_ge(od_done, 2 * (l * N_DIL + g) + 2)
                    for t in range(ST):
                        last = pe.transpose(ps[7][:, t * P:(t + 1) * P], of[:, t * P:(t + 1) * P], ident[:, :])
                    last.then_inc(ot_done, 1)

            def diff(l):
                def head(h, has_next):
                    q = l * N_DH + N_DIL + h
                    dq = l * N_DIFF + h
                    tq = l * N_T + 8 * N_DIL + 4 * h

                    def transposed(i):
                        if i % 2 == 0:
                            return
                        t = i // 2
                        pe.wait_ge(amap_step, 4 * (4 * dq + t + 1))
                        pe.wait_ge(pt_lo_done, tq + t + 1)
                        for kb in range(ST):
                            last = pe.transpose(ps[5 + t % 2][:, kb * P:(kb + 1) * P],
                                                amap[t % 2][:, kb * P:(kb + 1) * P], ident[:, :])
                        last.then_inc(t_done, 1)

                    double_head(q, lambda s: (s % 2, s // 2), transposed,
                                l * PAIRS_LAYER + PAIR_HEADS + 2 * N_DIL + 2 * h + 2 if has_next else None)
                    pe.wait_ge(qkv_lo, 3 * q + 3)
                    pe.wait_ge(pt_lo_done, CREDIT + tq + 4)
                    for kb in range(ST):
                        last = three(ps[7][:, :], v_hi[:, kb, :], v_lo[:, kb, :],
                                     pt_hi[0][:, kb, :], pt_lo[0][:, kb, :], kb == 0, kb == ST - 1)
                    last.then_inc(ov_done, 1)
                    if has_next:
                        v_transposed(q + 1)
                    pe.wait_ge(osq_done, dq + 1)
                    pe.matmul(ps[5][:, :], ones[:, :], osq[:, :], start=True, stop=True).then_inc(oms_done, 1)

                with pe.Fori(0, N_DIFF - 1) as h:
                    head(h, True)
                head(N_DIFF - 1, False)
                pe.wait_ge(mix_step, N_MIX * (l + 1))
                for t in range(ST):
                    src = ybf[:, 2 * t:2 * t + 2, :].rearrange("p m e -> p (m e)")
                    last = pe.transpose(ps[7][:, t * P:(t + 1) * P], src, ident[:, :])
                last.then_inc(ybt_done, 1)

            def merge(l):
                with pe.Fori(0, KT // 2) as i:
                    for j in range(2):
                        pair = l * PAIRS_LAYER + PAIR_MERGE + 3 * i
                        b = 4 * j
                        pe.wait_ge(merged, l * KT + 2 * i + j + 1)
                        u = 3 * j
                        project(pair + u // 2, u % 2, ps[b][:, :], xn_hi, xn_lo)
                        u = 3 * j + 1
                        project(pair + u // 2, u % 2, ps[b + 1][:, :], xn_hi, xn_lo)
                        u = 3 * j + 2
                        s = u % 2
                        unit_arrived(pair + u // 2, s)
                        pe.wait_ge(yc_lo_done, (l + 1) * N_DIFF)
                        pe.wait_ge(yb_lo_done, l + 1)
                        three(ps[b + 2][:, :], w_hi[s][:, 4, :], w_lo[s][:, 4, :], yb_hi[:, 0, :], yb_lo[:, 0, :],
                              True, True)
                        for k in range(N_DIFF):
                            last = three(ps[b + 3][:, :], w_hi[s][:, k, :], w_lo[s][:, k, :],
                                         yc_hi[:, k, :], yc_lo[:, k, :], k == 0, k == N_DIFF - 1)
                        last.then_inc(unit_used, 1)

            def out_projection(l):
                with pe.Fori(0, KT // 2) as i:
                    pe.wait_ge(m_lo_done, (l + 1) * KT)
                    for j in range(2):
                        pe.wait_ge(x_ready, KT * (3 * l + 2) + 2 * i + j - 1)
                        project(l * PAIRS_LAYER + PAIR_OUT + i, j, ps[j][:, :], m_hi, m_lo)

            def single(out, w, rh, rl, first, last):
                pe.matmul(out, w, rh, start=first, stop=False)
                return pe.matmul(out, w, rl, start=False, stop=last)

            def s5():
                with pe.Fori(0, UT // 2) as i:
                    pe.wait_ge(xn_done, KT * (3 * DEPTH + 1))
                    for j in range(2):
                        pe.wait_ge(u_lo_done, 2 * i + j + 1)
                        project(PAIR_U + i, j, ps[2 * j][:, :], xn_hi, xn_lo)
                with pe.Fori(0, UT) as c:
                    pe.wait_ge(u_lo_done, CREDIT + UT)
                    pe.wait_ge(yf_done, c + 1)
                    for s in range(4):
                        if s % 2 == 0:
                            unit_arrived(PAIR_S5 + c, s // 2)
                        for b in range(2):
                            w = 4 * (s % 2) + b
                            last = three(ps[bu_banks[s][b]][:, :], w_hi[s // 2][:, w, :], w_lo[s // 2][:, w, :],
                                         u_hi[:, c, :], u_lo[:, c, :], True, True)
                        last.then_inc(bu_mm, 1)
                    for s in range(4):
                        pe.wait_ge(st_lo_done, 4 * c + s + 1)
                        for b in range(2):
                            w = 4 * (s % 2) + 2 + b
                            last = three(ps[4][:, :], w_hi[s // 2][:, w, :], w_lo[s // 2][:, w, :],
                                         st_hi[s][:, b, :], st_lo[s][:, b, :],
                                         s == 0 and b == 0, s == 3 and b == 1)
                        if s % 2:
                            last.then_inc(unit_used, 1)
                with pe.Fori(0, UT // 2) as i:
                    for j in range(2):
                        pe.wait_ge(zb_done, 2 * i + j + 1)
                        project(PAIR_ZB + i, j, ps[2 * j][:, :], xn_hi, xn_lo)
                for c in range(UT):
                    if c % 2 == 0:
                        unit_arrived(PAIR_GLU, c // 2)
                    if c == 0:
                        pe.wait_ge(ge_lo_done, UT)
                    for k in range(UT):
                        w = UT * (c % 2) + k
                        last = three(ps[4 + c][:, :], w_hi[c // 2][:, w, :], w_lo[c // 2][:, w, :],
                                     ge_hi[:, k, :], ge_lo[:, k, :], k == 0, k == UT - 1)
                    if c % 2:
                        last.then_inc(unit_used, 1)

            def stick_breaking():
                def mean_square(h, j):
                    pe.wait_ge(sbq_done, 2 * (2 * h + j + 1))
                    pe.matmul(ps[j][:, :], ones[:, :], sbs[j][:, :], start=True, stop=True).then_inc(sbms_done, 1)

                def gate_argument(h, pair):
                    pe.wait_ge(sblog_done, 2 * h + 1)
                    project(pair + 1, 1, ps[0][:, :], xn_hi, xn_lo)

                def v_transposed(h):
                    pe.wait_ge(svf_done, h + 1)
                    for t in range(ST):
                        last = pe.transpose(ps[2][:, t * P:(t + 1) * P], svf[:, t * P:(t + 1) * P], ident[:, :])
                    last.then_inc(svt_done, 1)

                def logits(h, n):
                    b = ST - 1 - n
                    if n >= 2:
                        pe.wait_ge(lom_done, ST * h + n - 1)
                    three(ps[5 + n % 2][:, 0:S - b * P], sbn_hi[1][:, b * P:(b + 1) * P],
                          sbn_lo[1][:, b * P:(b + 1) * P], sbn_hi[0][:, b * P:S], sbn_lo[0][:, b * P:S],
                          True, True).then_inc(z_done, 1)

                def rest(h, n):
                    b = ST - 1 - n
                    pe.wait_ge(lom_lo_done, ST * h + n + 1)
                    if n >= 2:
                        pe.wait_ge(wlog_done, ST * h + n - 1)
                    out = ps[3 + n % 2]
                    last = single(out[:, 0:S - b * P], after_r[:, :], lom_hi[:, b, b * P:S], lom_lo[:, b, b * P:S],
                                  True, b == ST - 1)
                    for e in range(b + 1, ST):
                        last = single(out[:, (e - b) * P:S - b * P], ones_r[:, :], lom_hi[:, e, e * P:S],
                                      lom_lo[:, e, e * P:S], False, e == ST - 1)
                    last.then_inc(rest_done, 1)

                def head(h, has_next):
                    pair = PAIR_SB + 2 * h + 2
                    pe.wait_ge(sb_lo_done, 3 * h + 2)
                    logits(h, 0)
                    logits(h, 1)
                    if has_next:
                        pe.wait_ge(sz_done, h + 1)
                        project(pair, 0, ps[0][:, :], xn_hi, xn_lo)
                    rest(h, 0)
                    logits(h, 2)
                    if has_next:
                        project(pair, 1, ps[1][:, :], xn_hi, xn_lo)
                    rest(h, 1)
                    logits(h, 3)
                    pe.wait_ge(sb_lo_done, 3 * h + 3)
                    if has_next:
                        mean_square(h + 1, 0)
                        project(pair + 1, 0, ps[2][:, :], xn_hi, xn_lo)
                    rest(h, 2)
                    if has_next:
                        mean_square(h + 1, 1)
                        gate_argument(h + 1, pair)
                    rest(h, 3)
                    pe.wait_ge(wt_lo_done, ST * (h + 1))
                    for b in range(ST):
                        last = three(ps[7][:, b * P:S], sv_hi[:, b, :], sv_lo[:, b, :],
                                     w_hi_t[:, b, b * P:S], w_lo_t[:, b, b * P:S], b == 0, b == ST - 1)
                    last.then_inc(sbo_done, 1)
                    if has_next:
                        v_transposed(h + 1)

                pe.wait_ge(ob_lo_done, UT)
                for j in range(2):
                    project(PAIR_SB, j, ps[j][:, :], xn_hi, xn_lo)
                for j in range(2):
                    mean_square(0, j)
                project(PAIR_SB + 1, 0, ps[2][:, :], xn_hi, xn_lo)
                gate_argument(0, PAIR_SB)
                v_transposed(0)
                with pe.Fori(0, SB_HEADS - 1) as h:
                    head(h, True)
                head(SB_HEADS - 1, False)
                with pe.Fori(0, KT // 2) as i:
                    pe.wait_ge(gated_lo, CREDIT + SB_HEADS)
                    for j in range(2):
                        pe.wait_ge(x_ready, KT * (3 * DEPTH + 2) + 2 * i + j - 1)
                        for b in range(2):
                            unit_arrived(PAIR_EOUT + 2 * i + j, b)
                            for k in range(6):
                                last = three(ps[j][:, :], w_hi[b][:, k, :], w_lo[b][:, k, :], eo_hi[:, 6 * b + k, :],
                                             eo_lo[:, 6 * b + k, :], b == 0 and k == 0, b == 1 and k == 5)
                            last.then_inc(unit_used, 1)

            def gla():
                pe.wait_ge(xn_done, KT * (3 * DEPTH + 2))
                unit_arrived(PAIR_R, 0)
                for k in range(KT):
                    last = three(ps[0][:, :], w_hi[0][:, k, :], w_lo[0][:, k, :], xn_hi[:, k, :], xn_lo[:, k, :],
                                 k == 0, k == KT - 1)
                last.then_inc(unit_used, 1)
                unit_arrived(PAIR_R, 1)
                pe.wait_ge(r_lo_done, 1)
                for h in range(GLA_HEADS):
                    last = three(ps[1 + h][:, :], w_hi[1][:, h, :], w_lo[1][:, h, :], r_hi[:, :], r_lo[:, :],
                                 True, True)
                last.then_inc(unit_used, 1)
                with pe.Fori(0, GLA_HEADS) as h:
                    pair = PAIR_GLA + 3 * h
                    pe.wait_ge(gcum_done, GLA_HEADS)
                    project(pair, 0, ps[0][:, :], xn_hi, xn_lo)
                    project(pair, 1, ps[1][:, :], xn_hi, xn_lo)
                    pe.wait_ge(raw_done, SB_HEADS + 2 * h)
                    for j in range(2):
                        project(pair + 1, j, ps[2 + j][:, :], xn_hi, xn_lo)
                    pe.wait_ge(gq_done, 3 * h + 3)
                    for t in range(ST):
                        last = pe.transpose(ps[0][:, t * P:(t + 1) * P], gq[2][:, t * P:(t + 1) * P], ident[:, :])
                    last.then_inc(kdt_done, 1)
                    pe.wait_ge(gq_lo_done, 2 * h + 2)
                    for t in range(ST):
                        r = slice(t * P, (t + 1) * P)
                        last = three(ps[1][:, r], gq_hi[1][:, r], gq_lo[1][:, r], gq_hi[0][:, r], gq_lo[0][:, r],
                                     True, True)
                    last.then_inc(sc_mm, 1)
                    for j in range(2):
                        pe.wait_ge(gvf_done, 2 * h + j + 1)
                        for t in range(ST):
                            last = pe.transpose(ps[2 + j][:, t * P:(t + 1) * P], gvf[j][:, t * P:(t + 1) * P],
                                                ident[:, :])
                        last.then_inc(gvt_done, 1)
                    pe.wait_ge(kd_lo_done, h + 1)
                    pe.wait_ge(gv_lo_done, 2 * h + 2)
                    for c in range(NCH - 1):
                        r = slice(CH * (c % 2), CH * (c % 2) + CH)
                        last = three(kv_bank(c),
                                     kd_hi[r, c // 2, :], kd_lo[r, c // 2, :], gv_hi[r, c // 2, :], gv_lo[r, c // 2, :],
                                     True, True)
                    last.then_inc(kv_done, 1)
                    for j in range(2):
                        project(pair + 2, j, ps[j][:, :], xn_hi, xn_lo)
                    pe.wait_ge(score_lo_done, h + 1)
                    for d in range(2):
                        for t in range(ST):
                            three(ps[2 + d][:, t * P:(t + 1) * P], gv_hi[:, t, d * P:(d + 1) * P],
                                  gv_lo[:, t, d * P:(d + 1) * P], score_hi[:, t, :], score_lo[:, t, :],
                                  t == 0, False)
                    for c in range(1, NCH):
                        pe.wait_ge(state_lo_done, (NCH - 1) * h + c)
                        for d in range(2):
                            last = three(ps[2 + d][:, CH * c:CH * c + CH], state_hi[c][:, d * P:(d + 1) * P],
                                         state_lo[c][:, d * P:(d + 1) * P], gq_hi[0][:, CH * c:CH * c + CH],
                                         gq_lo[0][:, CH * c:CH * c + CH], False, c == NCH - 1)
                    last.then_inc(go_mm, 1)
                    pe.wait_ge(gz_done, 2 * h + 2)
                    pe.wait_ge(gsq_done, 2 * h + 2)
                    pe.matmul(ps[4][:, :], ones[:, :], gsq[0][:, :], start=True, stop=False)
                    pe.matmul(ps[4][:, :], ones[:, :], gsq[1][:, :], start=False, stop=True).then_inc(gms_done, 1)
                with pe.Fori(0, KT // 2) as i:
                    pe.wait_ge(gated_lo, CREDIT + SB_HEADS + KT)
                    for j in range(2):
                        pe.wait_ge(x_ready, KT * (3 * DEPTH + 3) + 2 * i + j - 1)
                        project(PAIR_OOUT + i, j, ps[j][:, :], go_hi, go_lo)

            pe.wait_ge(consts_ready, 1)
            pe.wait_ge(small_in, 16 * SMALL)
            for c, w in ((0, 512), (512, REL - 512)):
                last = pe.matmul(ps[c // 512][0:N_MAPS, 0:w], relt[:, :], onehot[:, c:c + w], start=True, stop=True)
            last.then_inc(table_ready, 1)
            with pe.Fori(0, DEPTH) as l:
                norm(3 * l)
                ffn_up(2 * l, l * PAIRS_LAYER + PAIR_FFN1, 3 * l)
                ffn_down(2 * l, l * PAIRS_LAYER + PAIR_DOWN1)
                norm(3 * l + 1)
                fourier(l)
                branch_a(l)
                first_head(l)
                dilated(l)
                diff(l)
                merge(l)
                out_projection(l)
                norm(3 * l + 2)
                ffn_up(2 * l + 1, l * PAIRS_LAYER + PAIR_FFN2, 3 * l + 2)
                ffn_down(2 * l + 1, l * PAIRS_LAYER + PAIR_DOWN2)
            norm(3 * DEPTH)
            norm(3 * DEPTH + 1)
            s5()
            stick_breaking()
            norm(3 * DEPTH + 2)
            gla()

        @block.scalar
        def _(act):
            def split(pair, j):
                act.wait_ge(unit_loaded[j], 16 * (pair + 1))
                act.wait_ge(unit_used, 2 * pair + j + 1)
                act.activation(w_hi[j][:, :, :], w_raw[j][:, :].rearrange("p (k m) -> p k m", k=8), ACT.Copy)\
                   .then_inc(unit_hi, 1)

            def used(pair, j):
                act.wait_ge(unit_used, CREDIT + 2 * pair + j + 1)

            def norm(n, r, final=False):
                act.preload_act_table_set(LN_EXP)
                with act.Fori(0, KT) as k:
                    act.wait_ge(x_ready, KT * n + k + 1)
                    act.activation(sq[:, k, :], x[:, k, :], ACT.Square).then_inc(sq_done, 1)
                act.wait_ge(ms_done, n + 1)
                act.activation(rlog[:, :], ps[7][:, :], ACT.Ln, bias=eps[:, 0:1], scale=1.0 / D).then_inc(rlog_done, 1)
                act.wait_ge(rlog_done, n + 1)
                act.activation(rstd[:, :], rlog[:, :], ACT.Exp, scale=-0.5).then_inc(rstd_done, 1)
                if final:
                    return
                with act.Fori(0, KT) as k:
                    act.wait_ge(xf_done, KT * r + k + 1)
                    act.activation(xn_hi[:, k, :], xf[:, k, :], ACT.Copy).then_inc(xh_done, 1)

            def ffn_up(r, pair0):
                act.preload_act_table(ACT.Silu)
                with act.Fori(0, FT // 2) as i:
                    for j in range(2):
                        f = r * FT + 2 * i + j
                        pair = pair0 + 2 * i + j
                        split(pair, 1)
                        used(pair, 0)
                        act.wait_ge(prod_done, f + 1)
                        act.activation(gated[j][:, :], ps[2 * j][:, :], ACT.Silu).then_inc(gate_done, 1)
                        split(pair + 1, 0)
                        act.wait_ge(prod_done, CREDIT + f + 1)
                        act.activation(h_hi[:, 2 * i + j, :], prod[j][:, :], ACT.Copy).then_inc(hid_hi, 1)

            def split_ahead(pair0, pairs):
                with act.Fori(0, pairs) as i:
                    split(pair0 + i, 1)
                    split(pair0 + i + 1, 0)

            def fourier(l):
                for half in range(2):
                    w = 4 * S + P
                    act.dma_start(dft_raw[:, half * w:(half + 1) * w], a["dft"][:, half * w:(half + 1) * w])\
                       .then_inc(dft_in, 16)
                act.wait_ge(dft_in, 32 * (l + 1))
                act.activation(dft_hi[:, :], dft_raw[:, :], ACT.Copy).then_inc(dft_hi_done, 1)
                with act.Fori(0, GROUPS // 2) as i:
                    g0 = l * GROUPS + 2 * i
                    pair = l * PAIRS_LAYER + PAIR_FOUR + i
                    split(pair, 1)
                    for j in range(2):
                        used(pair, j)
                        act.activation(fa_hi[j][:, :], ps[j][:, :], ACT.Copy).then_inc(fa_hi_done, 1)
                        if j == 0:
                            split(pair + 1, 0)
                    for j in range(2):
                        act.wait_ge(fp_mm, g0 + j + 1)
                        for b in range(2):
                            act.activation(fp_hi[j][:, 2 * b:2 * b + 2, :],
                                           ps[2 + 2 * j + b][:, :].rearrange("p (t c) -> p t c", t=2), ACT.Copy)\
                               .then_inc(fp_hi_done, 1)
                    for j in range(2):
                        act.wait_ge(fy_mm, g0 + j + 1)
                        act.activation(ya_hi[:, 2 * i + j, :], ps[j][:, :], ACT.Copy).then_inc(fy_hi_done, 1)

            def branch_a(l):
                act.preload_act_table(ACT.Sigmoid)
                with act.Fori(0, KT // 2) as i:
                    for j in range(2):
                        c = 2 * i + j
                        pair = l * PAIRS_LAYER + PAIR_BR_A + c
                        split(pair, 1)
                        used(pair, 0)
                        act.wait_ge(mga_done, l * KT + c + 1)
                        act.activation(sig[j][:, :], ps[2 * j][:, :], ACT.Sigmoid,
                                       bias=gate_bias[:, bass.ds(l * 3 * KT + c, 1)]).then_inc(siga_done, 1)
                        split(pair + 1, 0)

            def load_bias(*maps):
                for m, n in enumerate(maps):
                    act.dma_start(bias[m][:, :], a["toeplitz"](n)).then_inc(bias_in, 16)

            def queries_keys(pair):
                used(pair, 0)
                act.activation(q_hi[:, :], ps[0][:, :], ACT.Copy).then_inc(qkv_hi, 1)
                used(pair, 1)
                act.activation(k_hi[:, :], ps[1][:, :], ACT.Copy).then_inc(qkv_hi, 1)
                used(pair + 1, 1)
                act.activation(vf[:, :], ps[2][:, :], ACT.Copy).then_inc(vf_done, 1)

            def values(q):
                act.wait_ge(vt_done, q + 1)
                act.activation(v_hi[:, :, :], ps[2][:, :].rearrange("p (t m) -> p t m", t=ST), ACT.Copy)\
                   .then_inc(qkv_hi, 1)

            def first_head(l):
                pair = l * PAIRS_LAYER + PAIR_HEADS
                load_bias(0, 1)
                split(pair, 1)
                split(pair + 1, 0)
                split(pair + 1, 1)
                split(pair + 2, 0)
                queries_keys(pair)
                values(l * N_DH)

            def double_head(q, stat, transposed, next_pair, *next_maps):
                if next_pair is not None:
                    split(next_pair, 1)
                for step in range(10):
                    if step < 8:
                        act.wait_ge(nmax_done, 8 * q + step + 1)
                        act.activation(prob[:, step, :], logit[step % 2][:, :], ACT.Exp,
                                       bias=nmax[:, stat, step:step + 1],
                                       accum_out=rsum[:, stat, step:step + 1]).then_inc(exp_done, 1)
                    if next_pair is not None:
                        if step in (3, 5, 7):
                            ahead, slot = {3: (1, 0), 5: (1, 1), 7: (2, 0)}[step]
                            split(next_pair + ahead, slot)
                        if step == 8:
                            load_bias(*next_maps)
                            act.wait_ge(s_done, 8 * q + 8)
                            queries_keys(next_pair)
                    if step >= 2:
                        transposed(step - 2)

            def dilated(l):
                act.preload_act_table_set(LN_EXP)
                with act.Fori(0, N_DIL) as g:
                    q = l * N_DH + g
                    tq = l * N_T + 8 * g

                    def transposed(i):
                        m, t = divmod(i, ST)
                        act.wait_ge(t_done, tq + i + 1)
                        act.activation(pt_hi[m][:, :, t * P:(t + 1) * P],
                                       ps[5 + i % 2][:, :].rearrange("p (b q) -> p b q", b=ST), ACT.Copy)\
                           .then_inc(pt_hi_done, 1)

                    double_head(q, g, transposed, l * PAIRS_LAYER + PAIR_HEADS + 2 * g + 2, 2 * g + 2, 2 * g + 3)
                    act.wait_ge(o_done, l * N_DIL + g + 1)
                    act.activation(of[0:HD, :], ps[7][0:HD, :], ACT.Copy).then_inc(od_done, 1)
                    act.activation(of[HD:P, :], ps[3][HD:P, :], ACT.Copy).then_inc(od_done, 1)
                    values(q + 1)
                    act.wait_ge(ot_done, l * N_DIL + g + 1)
                    act.activation(og[:, g, :, :].rearrange("p (m t) e -> p t m e", m=2),
                                   ps[7][:, :].rearrange("p (t m e) -> p t m e", t=ST, m=2), ACT.Copy)\
                       .then_inc(og_done, 1)
                act.wait_ge(mix_step, N_MIX * l + 3)
                act.activation(mixw[:, 1:4, :], mixw[:, 1:4, :], ACT.Exp).then_inc(mix_exp, 1)

            def diff(l):
                def head(h, has_next):
                    q = l * N_DH + N_DIL + h
                    dq = l * N_DIFF + h
                    tq = l * N_T + 8 * N_DIL + 4 * h

                    def transposed(i):
                        if i % 2 == 0:
                            return
                        t = i // 2
                        act.wait_ge(t_done, tq + t + 1)
                        act.activation(pt_hi[0][:, :, t * P:(t + 1) * P],
                                       ps[5 + t % 2][:, :].rearrange("p (b q) -> p b q", b=ST), ACT.Copy)\
                           .then_inc(pt_hi_done, 1)

                    double_head(q, N_DIL, transposed,
                                l * PAIRS_LAYER + PAIR_HEADS + 2 * N_DIL + 2 * h + 2 if has_next else None,
                                2 * N_DIL + h + 1)
                    act.wait_ge(ov_done, dq + 1)
                    act.activation(of[:, :], ps[7][:, :], ACT.Copy)
                    act.activation(osq[:, :], ps[7][:, :], ACT.Square).then_inc(osq_done, 1)
                    if has_next:
                        values(q + 1)
                    act.wait_ge(oms_done, dq + 1)
                    act.activation(olog[:, :], ps[5][:, :], ACT.Ln, bias=eps[:, 1:2], scale=1.0 / P)\
                       .then_inc(olog_done, 1)
                    act.wait_ge(olog_done, dq + 1)
                    act.activation(orstd[:, :], olog[:, :], ACT.Exp, scale=-0.5).then_inc(orstd_done, 1)
                    act.wait_ge(onorm_done, dq + 1)
                    act.activation(yc_hi[:, h, :], onorm[:, :], ACT.Copy).then_inc(yc_hi_done, 1)

                with act.Fori(0, N_DIFF - 1) as h:
                    head(h, True)
                head(N_DIFF - 1, False)
                act.wait_ge(ybt_done, l + 1)
                act.activation(yb_hi[:, 0, :], ps[7][:, :], ACT.Copy).then_inc(yb_hi_done, 1)

            def merge(l):
                act.preload_act_table(ACT.Sigmoid)
                with act.Fori(0, KT // 2) as i:
                    for j in range(2):
                        c = 2 * i + j
                        pair = l * PAIRS_LAYER + PAIR_MERGE + 3 * i
                        u = 3 * j
                        split(pair + (u + 1) // 2, (u + 1) % 2)
                        used(pair + u // 2, u % 2)
                        act.wait_ge(merged, l * KT + c + 1)
                        act.activation(sigb[j][:, :], ps[4 * j][:, :], ACT.Sigmoid,
                                       bias=gate_bias[:, bass.ds(l * 3 * KT + KT + c, 1)]).then_inc(sigbc_done, 1)
                        split(pair + (u + 2) // 2, (u + 2) % 2)
                        used(pair + (u + 1) // 2, (u + 1) % 2)
                        act.activation(sigc[j][:, :], ps[4 * j + 1][:, :], ACT.Sigmoid,
                                       bias=gate_bias[:, bass.ds(l * 3 * KT + 2 * KT + c, 1)]).then_inc(sigbc_done, 1)
                        split(pair + (u + 3) // 2, (u + 3) % 2)
                        act.wait_ge(merged, CREDIT + l * KT + c + 1)
                        act.activation(m_hi[:, c, :], mg[:, c, :], ACT.Copy).then_inc(m_hi_done, 1)

            def s5():
                act.preload_act_table(ACT.Gelu_apprx_tanh)
                with act.Fori(0, UT // 2) as i:
                    for j in range(2):
                        split(PAIR_U + i + j, 1 - j)
                        used(PAIR_U + i, j)
                        act.activation(uf[:, 2 * i + j, :], ps[2 * j][:, :], ACT.Copy)
                        act.activation(u_hi[:, 2 * i + j, :], ps[2 * j][:, :], ACT.Copy).then_inc(u_hi_done, 1)
                with act.Fori(0, UT) as c:
                    split(PAIR_S5 + c, 1)
                    for s in range(4):
                        act.wait_ge(bu_mm, 4 * c + s + 1)
                        if s >= 2:
                            act.wait_ge(scan_step, N_SCAN * c + 2 * (s - 1))
                        for b in range(2):
                            act.activation(bx[s % 2][:, b, :], ps[bu_banks[s][b]][:, :], ACT.Copy,
                                           scale=s5_coef[:, 0, bass.ds(4 * c + s, 1)]).then_inc(bx_done, 1)
                    for s in range(4):
                        act.wait_ge(scan_step, N_SCAN * (c + 1) - 2 * (3 - s))
                        act.activation(st_hi[s][:, 0, :], sc[s][:, 0, :], ACT.Copy).then_inc(st_hi_done, 1)
                        act.activation(st_hi[s][:, 1, :], sc[s][:, 1, :], ACT.Copy, scale=-1.0)\
                           .then_inc(st_hi_done, 1)
                    split(PAIR_S5 + c + 1, 0)
                    act.wait_ge(yf_done, c + 2)
                    act.activation(ge[:, c, :], yf[0][:, :], ACT.Gelu_apprx_tanh).then_inc(ge_done, 1)
                    act.wait_ge(ge_done, c + 1)
                    act.activation(ge_hi[:, c, :], ge[:, c, :], ACT.Copy).then_inc(ge_hi_done, 1)
                act.preload_act_table(ACT.Silu)
                with act.Fori(0, UT // 2) as i:
                    for j in range(2):
                        split(PAIR_ZB + i + j, 1 - j)
                        used(PAIR_ZB + i, j)
                        act.activation(zb[:, 2 * i + j, :], ps[2 * j][:, :], ACT.Silu).then_inc(zb_done, 1)
                split(PAIR_GLU, 1)
                for c in range(UT):
                    if c % 2 == 0:
                        used(PAIR_GLU, c // 2)
                        split(PAIR_SB, 0) if c == 0 else None
                    act.wait_ge(ob_step, 2 * (c - 1)) if c >= 2 else None
                    act.activation(glu[c % 2][:, :], ps[4 + c][:, :], ACT.Sigmoid, bias=s5_cols[:, 1, c:c + 1])\
                       .then_inc(glu_done, 1)
                for c in range(UT):
                    act.wait_ge(ob_step, 2 * (c + 1))
                    act.activation(eo_hi[:, SB_HEADS + c, :], ob_f[c % 2][:, :], ACT.Copy).then_inc(ob_hi_done, 1)

            def stick_breaking():
                def query_key(h, pair, j):
                    used(pair, j)
                    act.activation(sbq[j][:, :], ps[j][:, :], ACT.Copy).then_inc(sbq_done, 1)
                    act.activation(sbs[j][:, :], ps[j][:, :], ACT.Square).then_inc(sbq_done, 1)

                def log_mean(h, j):
                    act.wait_ge(sbms_done, 2 * h + j + 1)
                    act.activation(sbl[j][:, :], ps[j][:, :], ACT.Ln, bias=eps[:, 0:1], scale=1.0 / P)\
                       .then_inc(sblog_done, 1)

                def root(h, j):
                    act.wait_ge(sblog_done, 2 * h + j + 1)
                    act.activation(sbs[j][:, :], sbl[j][:, :], ACT.Exp, scale=-0.5).then_inc(sbr_done, 1)

                def value(pair):
                    used(pair + 1, 0)
                    act.activation(svf[:, :], ps[2][:, :], ACT.Copy).then_inc(svf_done, 1)
                    split(pair + 2, 0)

                def finish(h, pair):
                    used(pair + 1, 1)
                    act.activation(ez[:, h, :], ps[0][:, :], ACT.Copy).then_inc(sz_done, 1)
                    for j in range(2):
                        act.wait_ge(sbn_done, 2 * h + j + 1)
                        act.activation(sbn_hi[j][:, :], sbq[j][:, :], ACT.Copy).then_inc(sb_hi_done, 1)
                    act.wait_ge(svt_done, h + 1)
                    act.activation(sv_hi[:, :, :], ps[2][:, :].rearrange("p (t m) -> p t m", t=ST), ACT.Copy)\
                       .then_inc(sb_hi_done, 1)

                def log_rest(h, n):
                    b = ST - 1 - n
                    w = S - b * P
                    k = ST * h + n
                    act.wait_ge(z_done, k + 1)
                    act.activation(za[n % 2][:, 0:w], ps[5 + n % 2][:, 0:w], ACT.Abs, scale=P ** -0.5)\
                       .then_inc(za_done, 1)
                    act.wait_ge(za_done, k + 1)
                    act.activation(ze[n % 2][:, 0:w], za[n % 2][:, 0:w], ACT.Exp, scale=-1.0).then_inc(ze_done, 1)
                    act.wait_ge(ze_done, k + 1)
                    act.activation(za[n % 2][:, 0:w], ze[n % 2][:, 0:w], ACT.Ln, bias=ones[:, 0:1])\
                       .then_inc(zl_done, 1)
                    act.wait_ge(lom_done, k + 1)
                    act.activation(lom_hi[:, b, b * P:S], lom[n % 2][:, 0:w], ACT.Copy).then_inc(lom_hi_done, 1)

                def weights(h, n):
                    b = ST - 1 - n
                    w = S - b * P
                    k = ST * h + n
                    act.wait_ge(wlog_done, k + 1)
                    act.activation(ww[n % 2][:, 0:w], zm[n % 2][:, 0:w], ACT.Exp).then_inc(w_exp_done, 1)
                    act.wait_ge(w_masked, k + 1)
                    act.activation(w_hi_t[:, b, b * P:S], ww[n % 2][:, 0:w], ACT.Copy).then_inc(wt_hi_done, 1)

                def head(h, has_next):
                    pair = PAIR_SB + 2 * h + 2
                    if has_next:
                        split(pair, 1)
                    log_rest(h, 0)
                    log_rest(h, 1)
                    if has_next:
                        split(pair + 1, 0)
                        query_key(h + 1, pair, 0)
                    weights(h, 0)
                    log_rest(h, 2)
                    if has_next:
                        split(pair + 1, 1)
                        query_key(h + 1, pair, 1)
                    weights(h, 1)
                    log_rest(h, 3)
                    if has_next:
                        log_mean(h + 1, 0)
                        value(pair)
                    weights(h, 2)
                    if has_next:
                        log_mean(h + 1, 1)
                        for j in range(2):
                            root(h + 1, j)
                    weights(h, 3)
                    if has_next:
                        finish(h + 1, pair)

                act.preload_act_table_set(LN_EXP)
                split(PAIR_SB, 1)
                for j in range(2):
                    query_key(0, PAIR_SB, j)
                    split(PAIR_SB + 1, j)
                log_mean(0, 0)
                value(PAIR_SB)
                log_mean(0, 1)
                for j in range(2):
                    root(0, j)
                finish(0, PAIR_SB)
                with act.Fori(0, SB_HEADS - 1) as h:
                    head(h, True)
                head(SB_HEADS - 1, False)
                gate_outputs(0, eo_hi, ez)
                split_ahead(PAIR_EOUT, KT)

            def gate_outputs(n0, out_hi, z):
                act.preload_act_table(ACT.Silu)
                with act.Fori(0, GATED // 2) as i:
                    for j in range(3):
                        n = n0 + 2 * i + j
                        if j < 2:
                            act.wait_ge(raw_done, n0 + GATED)
                            act.wait_ge(gated_f, n + 1)
                            act.activation(gate[j][:, :], z[:, 2 * i + j, :], ACT.Silu).then_inc(gate_made, 1)
                        if j:
                            act.wait_ge(gated_f, CREDIT + n)
                            act.activation(out_hi[:, 2 * i + j - 1, :], gated_o[j - 1][:, :], ACT.Copy)\
                               .then_inc(gated_hi, 1)

            def gla():
                act.preload_act_table_set(LN_EXP)
                split(PAIR_R, 1)
                used(PAIR_R, 0)
                act.activation(r_hi[:, :], ps[0][:, :], ACT.Copy).then_inc(r_hi_done, 1)
                split(PAIR_GLA, 0)
                for h in range(GLA_HEADS):
                    act.wait_ge(gx_step, h + 1)
                    act.activation(ga[h % 2][:, :], gx[h % 2][:, :], ACT.Abs).then_inc(ga_step, 1)
                    act.wait_ge(ga_step, 3 * h + 1)
                    act.activation(ga[h % 2][:, :], ga[h % 2][:, :], ACT.Exp, scale=-1.0).then_inc(ga_step, 1)
                    act.wait_ge(ga_step, 3 * h + 2)
                    if h >= 2:
                        act.wait_ge(gcum_done, h - 1)
                    act.activation(gl[h % 2][:, :], ga[h % 2][:, :], ACT.Ln, bias=ones[:, 0:1]).then_inc(ga_step, 1)
                with act.Fori(0, GLA_HEADS) as h:
                    pair = PAIR_GLA + 3 * h
                    split(pair, 1)
                    act.wait_ge(gd_done, h + 1)
                    for n, (src, scale) in enumerate(((gcum[:, h, :], 1 / TAU), (gcum[:, h, :], -1 / TAU),
                                                      (gdiff[:, :], 1 / TAU))):
                        act.activation(gexp[n][:, :], src, ACT.Exp, scale=scale).then_inc(gexp_done, 1)
                    act.activation(gend[:, :], gcum[:, h, CH - 1::CH], ACT.Exp, scale=1 / TAU).then_inc(gexp_done, 1)
                    split(pair + 1, 0)
                    for j in range(2):
                        act.wait_ge(gq_done, 3 * h + j + 1)
                        act.activation(gq_hi[j][:, :], gq[j][:, :], ACT.Copy).then_inc(gq_hi_done, 1)
                        if j == 0:
                            split(pair + 1, 1)
                    for j in range(2):
                        used(pair + 1, j)
                        act.activation(gvf[j][:, :], ps[2 + j][:, :], ACT.Copy).then_inc(gvf_done, 1)
                        split(pair + 2, j)
                    act.wait_ge(kdt_done, h + 1)
                    act.activation(kd_hi[:, :, :], ps[0][:, :].rearrange("p (t m) -> p t m", t=ST), ACT.Copy)\
                       .then_inc(kd_hi_done, 1)
                    act.wait_ge(score_done, h + 2)
                    act.activation(score_hi[:, :, :], score[:, :, :], ACT.Copy).then_inc(score_hi_done, 1)
                    for j in range(2):
                        act.wait_ge(gvt_done, 2 * h + j + 1)
                        act.activation(gv_hi[:, :, j * P:(j + 1) * P], ps[2 + j][:, :].rearrange("p (t m) -> p t m", t=ST),
                                       ACT.Copy).then_inc(gv_hi_done, 1)
                    for c in range(1, NCH):
                        act.wait_ge(state_done, (NCH - 1) * h + c)
                        act.activation(state_hi[c][:, :], state[c % 2][:, :], ACT.Copy).then_inc(state_hi_done, 1)
                    act.wait_ge(go_mm, h + 1)
                    for d in range(2):
                        act.activation(gsq[d][:, :], ps[2 + d][:, :], ACT.Square).then_inc(gsq_done, 1)
                    for d in range(2):
                        used(pair + 2, d)
                        act.activation(gz[:, 2 * h + d, :], ps[d][:, :], ACT.Copy).then_inc(gz_done, 1)
                        if d == 0:
                            split(pair + 3, 0)
                    act.wait_ge(gms_done, h + 1)
                    act.activation(grs[0][:, :], ps[4][:, :], ACT.Ln, bias=eps[:, 0:1], scale=0.5 / P).then_inc(grs_step, 1)
                    act.wait_ge(grs_step, 2 * h + 1)
                    act.activation(grs[1][:, :], grs[0][:, :], ACT.Exp, scale=-0.5).then_inc(grs_step, 1)
                gate_outputs(SB_HEADS, go_hi, gz)
                split_ahead(PAIR_OOUT, KT // 2 - 1)
                split(N_PAIRS - 1, 1)

            def s5_setup():
                lre, lim, ldt = (s5_in[:, n, :] for n in range(3))
                act.activation(s5_t[:, 0, :], ldt, ACT.Exp).then_inc(s5_dt, 1)
                act.wait_ge(s5_step, 2)
                act.activation(s5_t[:, 3, :], s5_t[:, 1, :], ACT.Exp).then_inc(s5_tables, 1)
                act.wait_ge(s5_step, 12)
                act.activation(s5_t[:, 5, :], s5_t[:, 5, :], ACT.Sin).then_inc(s5_tables, 1)
                act.activation(s5_t[:, 6, :], s5_t[:, 6, :], ACT.Sin).then_inc(s5_tables, 1)

            act.wait_ge(consts_ready, 1)
            act.wait_ge(small_in, 16 * SMALL)
            act.activation(after_r[:, :], after[:, 0:P], ACT.Copy).then_inc(masks_r, 1)
            act.activation(ones_r[:, :], ones[:, :], ACT.Copy).then_inc(masks_r, 1)
            s5_setup()
            act.wait_ge(setup_step, 2)
            act.activation(lame[:, :], lams[:, :], ACT.Exp).then_inc(lam_exp, 1)
            act.wait_ge(table_copied, 2)
            act.dma_start(a["table"], table[:, :].unsqueeze(1).to_broadcast([N_MAPS, P, REL])).then_inc(table_out, 16)
            act.wait_ge(table_out, 16)
            split(0, 0)
            with act.Fori(0, DEPTH) as l:
                norm(3 * l, 3 * l)
                ffn_up(2 * l, l * PAIRS_LAYER + PAIR_FFN1)
                split_ahead(l * PAIRS_LAYER + PAIR_DOWN1, FT // 2)
                norm(3 * l + 1, 3 * l + 1)
                fourier(l)
                branch_a(l)
                first_head(l)
                dilated(l)
                diff(l)
                merge(l)
                split_ahead(l * PAIRS_LAYER + PAIR_OUT, KT // 2)
                norm(3 * l + 2, 3 * l + 2)
                ffn_up(2 * l + 1, l * PAIRS_LAYER + PAIR_FFN2)
                split_ahead(l * PAIRS_LAYER + PAIR_DOWN2, FT // 2)
            norm(3 * DEPTH, 0, final=True)
            norm(3 * DEPTH + 1, 3 * DEPTH)
            s5()
            stick_breaking()
            norm(3 * DEPTH + 2, 3 * DEPTH + 1)
            gla()

        @block.vector
        def _(dve):
            def used(pair, j):
                dve.wait_ge(unit_used, CREDIT + 2 * pair + j + 1)

            def low(out, full, hi):
                return dve.tensor_tensor(out, full, hi.bitcast(F32), ALU.subtract)

            def norm(n, r, final=False):
                dve.wait_ge(sq_done, KT * n + 2)
                dve.tensor_tensor(acc[:, :], sq[:, 0, :], sq[:, 1, :], ALU.add).then_inc(sum_step, 1)
                for k in range(2, KT):
                    dve.wait_ge(sq_done, KT * n + k + 1)
                    dve.wait_ge(sum_step, 7 * n + k - 1)
                    dve.tensor_tensor(acc[:, :], acc[:, :], sq[:, k, :], ALU.add).then_inc(sum_step, 1)
                dve.wait_ge(rstd_done, n + 1)
                for k in range(KT):
                    g = gains[:, bass.ds(n * KT + k, 1)]
                    if final:
                        dve.scalar_tensor_tensor(x[:, k, :], x[:, k, :], g, rstd[:, :], ALU.mult, ALU.mult)\
                           .then_inc(x_ready, 1)
                        continue
                    dve.scalar_tensor_tensor(xf[:, k, :], x[:, k, :], g, rstd[:, :], ALU.mult, ALU.mult)\
                       .then_inc(xf_done, 1)
                    if k:
                        dve.wait_ge(xh_done, KT * r + k)
                        low(xn_lo[:, k - 1, :], xf[:, k - 1, :], xn_hi[:, k - 1, :]).then_inc(xn_done, 1)
                if not final:
                    dve.wait_ge(xh_done, KT * r + KT)
                    low(xn_lo[:, KT - 1, :], xf[:, KT - 1, :], xn_hi[:, KT - 1, :]).then_inc(xn_done, 1)

            def ffn_up(r, pair0):
                with dve.Fori(0, FT // 2) as i:
                    for j in range(2):
                        f = r * FT + 2 * i + j
                        dve.wait_ge(gate_done, f + 1)
                        used(pair0 + 2 * i + j, 1)
                        dve.wait_ge(hid_lo, f + 1)
                        dve.tensor_tensor(prod[j][:, :], gated[j][:, :], ps[2 * j + 1][:, :], ALU.mult)\
                           .then_inc(prod_done, 1)
                        dve.wait_ge(hid_hi, f + 1)
                        low(h_lo[:, 2 * i + j, :], prod[j][:, :], h_hi[:, 2 * i + j, :]).then_inc(hid_lo, 1)

            def ffn_down(pair0):
                used(pair0 + FT // 2 - 1, 1)
                for m in range(KT):
                    dve.scalar_tensor_tensor(x[:, m, :], ps[m][:, :], 0.5, x[:, m, :], ALU.mult, ALU.add)\
                       .then_inc(x_ready, 1)

            def fourier(l):
                dve.wait_ge(dft_hi_done, l + 1)
                low(dft_lo[:, :], dft_raw[:, :], dft_hi[:, :]).then_inc(dft_lo_done, 1)
                with dve.Fori(0, GROUPS // 2) as i:
                    g0 = l * GROUPS + 2 * i
                    for j in range(2):
                        dve.wait_ge(fa_hi_done, g0 + j + 1)
                        low(fa_lo[j][:, :], ps[j][:, :], fa_hi[j][:, :]).then_inc(fa_lo_done, 1)
                    for j in range(2):
                        for b in range(2):
                            dve.wait_ge(fp_hi_done, 2 * (g0 + j) + b + 1)
                            low(fp_lo[j][:, 2 * b:2 * b + 2, :], ps[2 + 2 * j + b][:, :].rearrange("p (t c) -> p t c", t=2),
                                fp_hi[j][:, 2 * b:2 * b + 2, :]).then_inc(fp_lo_done, 1)
                    for j in range(2):
                        dve.wait_ge(fy_hi_done, g0 + j + 1)
                        low(ya_lo[:, 2 * i + j, :], ps[j][:, :], ya_hi[:, 2 * i + j, :]).then_inc(fy_lo_done, 1)

            def branch_a(l):
                with dve.Fori(0, KT // 2) as i:
                    for j in range(2):
                        c = 2 * i + j
                        dve.wait_ge(siga_done, l * KT + c + 1)
                        used(l * PAIRS_LAYER + PAIR_BR_A + c, 1)
                        dve.tensor_tensor(mg[:, c, :], sig[j][:, :], ps[2 * j + 1][:, :], ALU.mult).then_inc(mga_done, 1)

            def queries_keys(q):
                for n, (hi, lo) in enumerate(((q_hi, q_lo), (k_hi, k_lo))):
                    dve.wait_ge(qkv_hi, 3 * q + n + 1)
                    low(lo[:, :], ps[n][:, :], hi[:, :]).then_inc(qkv_lo, 1)

            def values(q):
                dve.wait_ge(qkv_hi, 3 * q + 3)
                low(v_lo[:, :, :], ps[2][:, :].rearrange("p (t m) -> p t m", t=ST), v_hi[:, :, :]).then_inc(qkv_lo, 1)

            def first_head(l):
                queries_keys(l * N_DH)
                values(l * N_DH)

            def double_head(q, stat, tile_of, bias_of, transposed, has_next):
                for step in range(10):
                    if step < 8:
                        m, t = tile_of(step)
                        dve.wait_ge(s_done, 8 * q + step + 1)
                        dve.wait_ge(exp_done, 8 * q + step + 1)
                        o = P * (ST - 1 - t)
                        dve.scalar_tensor_tensor(logit[step % 2][:, :], ps[3 + step % 2][:, :], HD ** -0.5,
                                                 bias_of(m)[:, o:o + S], ALU.mult, ALU.add).then_inc(logit_done, 1)
                        dve.wait_ge(logit_done, CREDIT + 8 * q + step + 1)
                        dve.tensor_reduce(nmax[:, stat, step:step + 1], logit[step % 2][:, :], AX.X, ALU.max,
                                          negate=True).then_inc(nmax_done, 1)
                    if step == 8 and has_next:
                        queries_keys(q + 1)
                    if step >= 2:
                        transposed(step - 2)

            def transposed_low(n, m, t, bank):
                dve.wait_ge(pt_hi_done, n + 1)
                low(pt_lo[m][:, :, t * P:(t + 1) * P], ps[bank][:, :].rearrange("p (b q) -> p b q", b=ST),
                    pt_hi[m][:, :, t * P:(t + 1) * P]).then_inc(pt_lo_done, 1)

            def dilated(l):
                with dve.Fori(0, N_DIL) as g:
                    tq = l * N_T + 8 * g

                    def transposed(i):
                        transposed_low(tq + i, i // ST, i % ST, 5 + i % 2)

                    q = l * N_DH + g
                    dve.wait_ge(bias_in, l * BIAS_LOADS + 32 * (g + 1))
                    double_head(q, g, lambda s: divmod(s, ST), lambda m: bias[m], transposed, True)
                    values(q + 1)
                step = [0]

                def link(ins):
                    step[0] += 1
                    ins.then_inc(mix_step, 1)
                    if step[0] < N_MIX:
                        dve.wait_ge(mix_step, N_MIX * l + step[0])

                def wide(w):
                    return w.unsqueeze(2).to_broadcast([P, 8, HD])

                dve.wait_ge(og_done, (l + 1) * N_DIL)
                link(dve.tensor_tensor(mixw[:, 0, :], nmax[:, 0, :], nmax[:, 1, :], ALU.min))
                link(dve.tensor_tensor(mixw[:, 0, :], mixw[:, 0, :], nmax[:, 2, :], ALU.min))
                link(dve.tensor_tensor(mixw[:, 1:4, :], mixw[:, 0:1, :].to_broadcast([P, N_DIL, 8]), nmax[:, 0:N_DIL, :],
                                       ALU.subtract))
                dve.wait_ge(mix_exp, l + 1)
                link(dve.tensor_tensor(mixr[:, :, :], mixw[:, 1:4, :], rsum[:, 0:N_DIL, :], ALU.mult))
                link(dve.tensor_tensor(mixw[:, 4, :], mixr[:, 0, :], mixr[:, 1, :], ALU.add))
                link(dve.tensor_tensor(mixw[:, 4, :], mixw[:, 4, :], mixr[:, 2, :], ALU.add))
                link(dve.reciprocal(mixw[:, 0, :], mixw[:, 4, :]))
                link(dve.tensor_tensor(mixr[:, :, :], mixw[:, 1:4, :], mixw[:, 0:1, :].to_broadcast([P, N_DIL, 8]),
                                       ALU.mult))
                out = ybf[:, :, :].rearrange("p (t m) e -> p m t e", m=2)
                tmp = ybt[:, :, :].rearrange("p (m t) e -> p m t e", m=2)

                def part(g):
                    return (og[:, g, :, :].rearrange("p (m t) e -> p m t e", m=2),
                            wide(mixr[:, g, :]).rearrange("p (m t) e -> p m t e", m=2))

                link(dve.tensor_tensor(out, *part(0), ALU.mult))
                link(dve.tensor_tensor(tmp, *part(1), ALU.mult))
                link(dve.tensor_tensor(out, out, tmp, ALU.add))
                link(dve.tensor_tensor(tmp, *part(2), ALU.mult))
                link(dve.tensor_tensor(out, out, tmp, ALU.add))

            def diff(l):
                def head(h, has_next):
                    q = l * N_DH + N_DIL + h
                    dq = l * N_DIFF + h
                    tq = l * N_T + 8 * N_DIL + 4 * h

                    def transposed(i):
                        if i % 2 == 0:
                            return
                        t = i // 2
                        n = 4 * (4 * dq + t)
                        dve.wait_ge(exp_done, CREDIT + 8 * q + i + 1)
                        if t:
                            dve.wait_ge(amap_step, n)
                        dve.reciprocal(rinv[:, t, :], rsum[:, N_DIL, 2 * t:2 * t + 2]).then_inc(amap_step, 1)
                        dve.wait_ge(amap_step, n + 1)
                        dve.tensor_scalar(rinv[:, t, 1:2], rinv[:, t, 1:2], lam_neg[:, bass.ds(l, 1)], None, ALU.mult)\
                           .then_inc(amap_step, 1)
                        dve.tensor_scalar(amap0[:, :], prob[:, i - 1, :], rinv[:, t, 0:1], None, ALU.mult)\
                           .then_inc(amap_step, 1)
                        dve.wait_ge(amap_step, n + 3)
                        dve.wait_ge(t_done, tq + t - 1)
                        dve.scalar_tensor_tensor(amap[t % 2][:, :], prob[:, i, :], rinv[:, t, 1:2], amap0[:, :],
                                                 ALU.mult, ALU.add).then_inc(amap_step, 1)
                        if t:
                            transposed_low(tq + t - 1, 0, t - 1, 5 + (t - 1) % 2)

                    dve.wait_ge(bias_in, l * BIAS_LOADS + 32 * (N_DIL + 1) + 16 * h)
                    double_head(q, N_DIL, lambda s: (s % 2, s // 2), lambda m: bias[0], transposed, has_next)
                    transposed_low(tq + 3, 0, 3, 6)
                    if has_next:
                        values(q + 1)
                    dve.wait_ge(orstd_done, dq + 1)
                    dve.scalar_tensor_tensor(onorm[:, :], of[:, :], sub_gain[:, bass.ds(l, 1)], orstd[:, :],
                                             ALU.mult, ALU.mult).then_inc(onorm_done, 1)
                    dve.wait_ge(yc_hi_done, dq + 1)
                    low(yc_lo[:, h, :], onorm[:, :], yc_hi[:, h, :]).then_inc(yc_lo_done, 1)

                with dve.Fori(0, N_DIFF - 1) as h:
                    head(h, True)
                head(N_DIFF - 1, False)
                dve.wait_ge(yb_hi_done, l + 1)
                low(yb_lo[:, 0, :], ps[7][:, :], yb_hi[:, 0, :]).then_inc(yb_lo_done, 1)

            def merge(l):
                with dve.Fori(0, KT // 2) as i:
                    for j in range(2):
                        c = 2 * i + j
                        n = l * KT + c
                        u = 3 * j + 2
                        used(l * PAIRS_LAYER + PAIR_MERGE + 3 * i + u // 2, u % 2)
                        dve.wait_ge(sigbc_done, 2 * (n + 1))
                        dve.tensor_tensor(tmpb[j][:, :], sigb[j][:, :], ps[4 * j + 2][:, :], ALU.mult)\
                           .then_inc(merge_step, 1)
                        dve.tensor_tensor(tmpc[j][:, :], sigc[j][:, :], ps[4 * j + 3][:, :], ALU.mult)\
                           .then_inc(merge_step, 1)
                        dve.wait_ge(merge_step, 3 * n + 1)
                        dve.tensor_tensor(mg[:, c, :], mg[:, c, :], tmpb[j][:, :], ALU.add).then_inc(merge_step, 1)
                        dve.wait_ge(merge_step, 3 * n + 3)
                        dve.tensor_tensor(mg[:, c, :], mg[:, c, :], tmpc[j][:, :], ALU.add).then_inc(merged, 1)
                        dve.wait_ge(m_hi_done, n + 1)
                        low(m_lo[:, c, :], mg[:, c, :], m_hi[:, c, :]).then_inc(m_lo_done, 1)

            def out_projection(l):
                with dve.Fori(0, KT // 2) as i:
                    for j in range(2):
                        used(l * PAIRS_LAYER + PAIR_OUT + i, j)
                        dve.tensor_tensor(x[:, 2 * i + j, :], x[:, 2 * i + j, :], ps[j][:, :], ALU.add)\
                           .then_inc(x_ready, 1)

            def s5_setup():
                count = [0]

                def link(ins):
                    count[0] += 1
                    ins.then_inc(s5_step, 1)
                    dve.wait_ge(s5_step, count[0])

                def tt(out, x0, x1, op):
                    link(dve.tensor_tensor(out, x0, x1, op))

                def stt(out, x0, c, x1, op0=ALU.mult, op1=ALU.add):
                    link(dve.scalar_tensor_tensor(out, x0, c, x1, op0, op1))

                def ts(out, x0, c0, c1, op0, op1):
                    link(dve.tensor_scalar(out, x0, c0, c1, op0, op1))

                t = [s5_t[:, n, :] for n in range(12)]
                lre, lim = s5_in[:, 0, :], s5_in[:, 1, :]
                dve.wait_ge(s5_dt, 1)
                tt(t[1], lre, t[0], ALU.mult)
                tt(t[2], lim, t[0], ALU.mult)
                big = 1.5 * 2.0 ** 23
                ts(t[4], t[2], 1 / (2 * math.pi), big, ALU.mult, ALU.add)
                ts(t[4], t[4], -big, None, ALU.add, ALU.bypass)
                c1, c2 = 6.28125, 0.0019350051879882812
                stt(t[5], t[4], -c1, t[2])
                stt(t[5], t[4], -c2, t[5])
                stt(t[5], t[4], -(2 * math.pi - c1 - c2), t[5])
                limit = 3.1415925
                ts(t[6], t[5], math.pi / 2, None, ALU.add, ALU.bypass)
                ts(t[7], t[6], math.pi, -2 * math.pi, ALU.is_gt, ALU.mult)
                tt(t[6], t[6], t[7], ALU.add)
                ts(t[6], t[6], limit, -limit, ALU.min, ALU.max)
                ts(t[5], t[5], limit, -limit, ALU.min, ALU.max)
                assert count[0] == 12, count
                dve.wait_ge(s5_tables, 3)
                re, im, neg = (s5_pow[:, n, :, :] for n in range(3))
                tt(re[:, 0, :], t[3], t[6], ALU.mult)
                tt(im[:, 0, :], t[3], t[5], ALU.mult)
                ts(t[4], re[:, 0, :], -1.0, None, ALU.add, ALU.bypass)
                tt(t[7], lre, lre, ALU.mult)
                tt(t[8], lim, lim, ALU.mult)
                tt(t[7], t[7], t[8], ALU.add)
                link(dve.reciprocal(t[7], t[7]))
                tt(t[8], t[4], lre, ALU.mult)
                tt(t[9], im[:, 0, :], lim, ALU.mult)
                tt(t[8], t[8], t[9], ALU.add)
                tt(s5_coef[:, 0, :], t[8], t[7], ALU.mult)
                tt(t[9], im[:, 0, :], lre, ALU.mult)
                tt(t[10], t[4], lim, ALU.mult)
                tt(t[9], t[9], t[10], ALU.subtract)
                tt(s5_coef[:, 1, :], t[9], t[7], ALU.mult)
                ts(s5_coef[:, 2, :], s5_coef[:, 1, :], -1.0, None, ALU.mult, ALU.bypass)
                for n in range(LEVELS):
                    ts(neg[:, n, :], im[:, n, :], -1.0, None, ALU.mult, ALU.bypass)
                    if n + 1 < LEVELS:
                        tt(t[8], re[:, n, :], re[:, n, :], ALU.mult)
                        tt(t[9], im[:, n, :], im[:, n, :], ALU.mult)
                        tt(re[:, n + 1, :], t[8], t[9], ALU.subtract)
                        stt(im[:, n + 1, :], re[:, n, :], 2.0, im[:, n, :], ALU.mult, ALU.mult)

            def s5():
                with dve.Fori(0, UT // 2) as i:
                    for j in range(2):
                        dve.wait_ge(u_hi_done, 2 * i + j + 1)
                        low(u_lo[:, 2 * i + j, :], ps[2 * j][:, :], u_hi[:, 2 * i + j, :]).then_inc(u_lo_done, 1)
                with dve.Fori(0, UT) as c:
                    base = N_SCAN * c
                    dve.tensor_copy(s5_now[:, :, :, :], s5_pow[:, :, :, bass.ds(4 * c, 4)]).then_inc(s5_now_set, 1)
                    for s in range(4):
                        coef = [s5_coef[:, n, bass.ds(4 * c + s, 1)] for n in range(3)]
                        dve.wait_ge(bx_done, 2 * (4 * c + s) + 2)
                        re, im = (ps[b][:, :] for b in bu_banks[s])
                        dve.scalar_tensor_tensor(sc[s][:, 0, :], im, coef[2], bx[s % 2][:, 0, :], ALU.mult, ALU.add)\
                           .then_inc(scan_step, 1)
                        dve.scalar_tensor_tensor(sc[s][:, 1, :], re, coef[1], bx[s % 2][:, 1, :], ALU.mult, ALU.add)\
                           .then_inc(scan_step, 1)
                    steps = [(n, 2 * (1 << n) - 1) for n in range(LEVELS)]
                    steps += [(n, 3 * (1 << n) - 1) for n in reversed(range(LEVELS - 1))]
                    dve.wait_ge(s5_now_set, c + 1)
                    for m, (n, first) in enumerate(steps):
                        to, fro = slice(first, S, 2 << n), slice(first - (1 << n), S - (1 << n), 2 << n)
                        start = base + 8 + 12 * m
                        p_re, p_im, p_neg = ([s5_now[:, part, n, s:s + 1] for s in range(4)] for part in range(3))
                        for s in range(4):
                            dve.wait_ge(scan_step, start - 6 + 2 * s if m else base + 2 * (s + 1))
                            dve.scalar_tensor_tensor(sc[s][:, :, to], sc[s][:, :, fro], p_re[s], sc[s][:, :, to],
                                                     ALU.mult, ALU.add).then_inc(scan_step, 1)
                        for s in range(4):
                            dve.wait_ge(scan_step, start + s + 1)
                            dve.scalar_tensor_tensor(sc[s][:, 0, to], sc[s][:, 1, fro], p_neg[s], sc[s][:, 0, to],
                                                     ALU.mult, ALU.add).then_inc(scan_step, 1)
                            dve.scalar_tensor_tensor(sc[s][:, 1, to], sc[s][:, 0, fro], p_im[s], sc[s][:, 1, to],
                                                     ALU.mult, ALU.add).then_inc(scan_step, 1)
                    for s in range(4):
                        dve.wait_ge(st_hi_done, 2 * (4 * c + s) + 2)
                        low(st_lo[s][:, 0, :], sc[s][:, 0, :], st_hi[s][:, 0, :])
                        dve.scalar_tensor_tensor(st_lo[s][:, 1, :], sc[s][:, 1, :], -1.0,
                                                 st_hi[s][:, 1, :].bitcast(F32), ALU.mult, ALU.subtract)\
                           .then_inc(st_lo_done, 1)
                    dve.wait_ge(unit_used, CREDIT + 2 * (PAIR_S5 + c) + 2)
                    dve.scalar_tensor_tensor(yf[0][:, :], uf[:, c, :], s5_cols[:, 0, bass.ds(c, 1)], ps[4][:, :],
                                             ALU.mult, ALU.add).then_inc(yf_done, 1)
                    dve.wait_ge(ge_hi_done, c + 1)
                    low(ge_lo[:, c, :], ge[:, c, :], ge_hi[:, c, :]).then_inc(ge_lo_done, 1)
                for c in range(UT):
                    dve.wait_ge(glu_done, c + 1)
                    if c >= 2:
                        dve.wait_ge(ob_lo_done, c - 1)
                    if c == 0:
                        dve.wait_ge(zb_done, CREDIT + UT)
                    dve.tensor_tensor(ob_f[c % 2][:, :], glu[c % 2][:, :], ge[:, c, :], ALU.mult).then_inc(ob_step, 1)
                    dve.wait_ge(ob_step, 2 * c + 1)
                    dve.tensor_tensor(ob_f[c % 2][:, :], ob_f[c % 2][:, :], zb[:, c, :], ALU.mult).then_inc(ob_step, 1)
                    if c >= 1:
                        dve.wait_ge(ob_hi_done, c)
                        low(eo_lo[:, SB_HEADS + c - 1, :], ob_f[(c - 1) % 2][:, :], eo_hi[:, SB_HEADS + c - 1, :])\
                            .then_inc(ob_lo_done, 1)
                dve.wait_ge(ob_hi_done, UT)
                low(eo_lo[:, SB_HEADS + UT - 1, :], ob_f[(UT - 1) % 2][:, :], eo_hi[:, SB_HEADS + UT - 1, :])\
                    .then_inc(ob_lo_done, 1)

            def stick_breaking():
                scale = P ** -0.5

                def normed(h):
                    for j in range(2):
                        dve.wait_ge(sbr_done, 2 * h + j + 1)
                        dve.scalar_tensor_tensor(sbq[j][:, :], sbq[j][:, :], tail_cols[:, j:j + 1], sbs[j][:, :],
                                                 ALU.mult, ALU.mult).then_inc(sbn_done, 1)

                def normed_low(h):
                    for j in range(2):
                        dve.wait_ge(sb_hi_done, 3 * h + 1 + j)
                        low(sbn_lo[j][:, :], sbq[j][:, :], sbn_hi[j][:, :]).then_inc(sb_lo_done, 1)

                def value_low(h):
                    dve.wait_ge(sb_hi_done, 3 * h + 3)
                    low(sv_lo[:, :, :], ps[2][:, :].rearrange("p (t m) -> p t m", t=ST), sv_hi[:, :, :])\
                        .then_inc(sb_lo_done, 1)

                def log_rest(h, n):
                    b = ST - 1 - n
                    w = S - b * P
                    k = ST * h + n
                    z = ps[5 + n % 2][:, 0:w]
                    dve.wait_ge(za_done, k + 1)
                    if n >= 2:
                        dve.wait_ge(w_exp_done, k - 1)
                    dve.tensor_scalar(zm[n % 2][:, 0:w], z, scale, 0.0, ALU.mult, ALU.min).then_inc(zm_step, 1)
                    dve.wait_ge(zl_done, k + 1)
                    dve.wait_ge(zm_step, 3 * k + 1)
                    dve.tensor_tensor(zm[n % 2][:, 0:w], zm[n % 2][:, 0:w], za[n % 2][:, 0:w], ALU.subtract)\
                       .then_inc(zm_step, 1)
                    dve.wait_ge(zm_step, 3 * k + 2)
                    dve.scalar_tensor_tensor(lom[n % 2][:, 0:w], z, -scale, zm[n % 2][:, 0:w], ALU.mult, ALU.add)\
                       .then_inc(zm_step, 1)
                    dve.wait_ge(zm_step, 3 * k + 3)
                    dve.tensor_tensor(lom[n % 2][:, 0:P], lom[n % 2][:, 0:P], after[:, P:2 * P], ALU.mult)\
                       .then_inc(lom_done, 1)
                    dve.wait_ge(lom_hi_done, k + 1)
                    low(lom_lo[:, b, b * P:S], lom[n % 2][:, 0:w], lom_hi[:, b, b * P:S]).then_inc(lom_lo_done, 1)

                def weights(h, n):
                    m = n % 2
                    b = ST - 1 - n
                    w = S - b * P
                    k = ST * h + n
                    dve.wait_ge(rest_done, k + 1)
                    dve.tensor_tensor(zm[m][:, 0:w], zm[m][:, 0:w], ps[3 + m][:, 0:w], ALU.add).then_inc(wlog_done, 1)
                    dve.wait_ge(w_exp_done, k + 1)
                    dve.tensor_tensor(ww[m][:, 0:P], ww[m][:, 0:P], after[:, P:2 * P], ALU.mult).then_inc(w_masked, 1)
                    dve.wait_ge(wt_hi_done, k + 1)
                    low(w_lo_t[:, b, b * P:S], ww[m][:, 0:w], w_hi_t[:, b, b * P:S]).then_inc(wt_lo_done, 1)

                def head(h, has_next):
                    log_rest(h, 0)
                    for n in range(1, ST):
                        log_rest(h, n)
                        weights(h, n - 1)
                    if has_next:
                        normed(h + 1)
                    weights(h, 3)
                    if has_next:
                        normed_low(h + 1)
                    dve.wait_ge(sbo_done, h + 1)
                    dve.tensor_copy(eo[:, h, :], ps[7][:, :]).then_inc(raw_done, 1)
                    if has_next:
                        value_low(h + 1)

                dve.wait_ge(masks_r, 2)
                normed(0)
                normed_low(0)
                value_low(0)
                with dve.Fori(0, SB_HEADS - 1) as h:
                    head(h, True)
                head(SB_HEADS - 1, False)
                gate_outputs(0, eo, eo_hi, eo_lo)
                with dve.Fori(0, KT // 2) as i:
                    for j in range(2):
                        used(PAIR_EOUT + 2 * i + j, 1)
                        dve.tensor_tensor(x[:, 2 * i + j, :], x[:, 2 * i + j, :], ps[j][:, :], ALU.add)\
                           .then_inc(x_ready, 1)

            def gate_outputs(n0, raw, out_hi, out_lo):
                with dve.Fori(0, GATED // 2) as i:
                    for j in range(3):
                        n = n0 + 2 * i + j
                        if j < 2:
                            dve.wait_ge(gate_made, n + 1)
                            dve.wait_ge(gated_lo, n + 1)
                            dve.tensor_tensor(gated_o[j][:, :], raw[:, 2 * i + j, :], gate[j][:, :], ALU.mult)\
                               .then_inc(gated_f, 1)
                        if j:
                            dve.wait_ge(gated_hi, n)
                            low(out_lo[:, 2 * i + j - 1, :], gated_o[j - 1][:, :], out_hi[:, 2 * i + j - 1, :])\
                                .then_inc(gated_lo, 1)

            def gla():
                dve.memset(restart[:, :], 1.0).then_inc(gcum_set, 1)
                dve.wait_ge(gcum_set, 1)
                dve.memset(restart[:, 0:S:CH], 0.0).then_inc(gcum_set, 1)
                dve.memset(score[:, :, :], 0.0).then_inc(score_done, 1)
                dve.wait_ge(r_hi_done, 1)
                low(r_lo[:, :], ps[0][:, :], r_hi[:, :]).then_inc(r_lo_done, 1)
                used(PAIR_R, 1)
                for h in range(GLA_HEADS):
                    j = h % 2
                    if h >= 2:
                        dve.wait_ge(gcum_set, h + 1)
                    dve.tensor_scalar(gx[j][:, :], ps[1 + h][:, :], tail_cols[:, 4 + h:5 + h], None, ALU.add)\
                       .then_inc(gx_step, 1)
                    dve.wait_ge(ga_step, 3 * h + 3)
                    dve.scalar_tensor_tensor(gl[j][:, :], gx[j][:, :], 0.0, gl[j][:, :], ALU.min, ALU.subtract)\
                       .then_inc(gcum_set, 1)
                    dve.wait_ge(gcum_set, h + 3)
                    dve.tensor_tensor_scan(gcum[:, h, :], restart[:, :], gl[j][:, :], 0.0, ALU.mult, ALU.add)\
                       .then_inc(gcum_done, 1)
                dve.wait_ge(gcum_done, GLA_HEADS)
                with dve.Fori(0, GLA_HEADS) as h:
                    pair = PAIR_GLA + 3 * h
                    g = gcum[:, h, :].rearrange("p (c t) -> p c t", t=CH)
                    dve.wait_ge(gcum_done, GLA_HEADS)
                    dve.tensor_tensor(gdiff[:, :].rearrange("p (c t) -> p c t", t=CH),
                                      g[:, :, CH - 1:CH].to_broadcast([P, NCH, CH]), g, ALU.subtract).then_inc(gd_done, 1)
                    dve.wait_ge(gexp_done, 4 * h + 4)
                    used(pair, 0)
                    dve.scalar_tensor_tensor(gq[0][:, :], ps[0][:, :], P ** -0.5, gexp[0][:, :], ALU.mult, ALU.mult)\
                       .then_inc(gq_done, 1)
                    used(pair, 1)
                    dve.tensor_tensor(gq[1][:, :], gexp[1][:, :], ps[1][:, :], ALU.mult).then_inc(gq_done, 1)
                    dve.tensor_tensor(gq[2][:, :], gexp[2][:, :], ps[1][:, :], ALU.mult).then_inc(gq_done, 1)
                    for j in range(2):
                        dve.wait_ge(gq_hi_done, 2 * h + j + 1)
                        low(gq_lo[j][:, :], gq[j][:, :], gq_hi[j][:, :]).then_inc(gq_lo_done, 1)
                    dve.wait_ge(kd_hi_done, h + 1)
                    low(kd_lo[:, :, :], ps[0][:, :].rearrange("p (t m) -> p t m", t=ST), kd_hi[:, :, :])\
                        .then_inc(kd_lo_done, 1)
                    dve.wait_ge(small_in, 16 * SMALL)
                    dve.wait_ge(sc_mm, h + 1)
                    dve.copy_predicated(score[:, :, :], keep[:, :].unsqueeze(1).to_broadcast([P, ST, P]),
                                        ps[1][:, :].rearrange("p (t m) -> p t m", t=ST)).then_inc(score_done, 1)
                    dve.wait_ge(score_hi_done, h + 1)
                    low(score_lo[:, :, :], score[:, :, :], score_hi[:, :, :]).then_inc(score_lo_done, 1)
                    for j in range(2):
                        dve.wait_ge(gv_hi_done, 2 * h + j + 1)
                        low(gv_lo[:, :, j * P:(j + 1) * P], ps[2 + j][:, :].rearrange("p (t m) -> p t m", t=ST),
                            gv_hi[:, :, j * P:(j + 1) * P]).then_inc(gv_lo_done, 1)
                    dve.wait_ge(kv_done, h + 1)
                    for c in range(NCH - 1):
                        n = (NCH - 1) * h + c
                        kv = kv_bank(c)
                        new, old = (c + 1) % 2, c % 2
                        if c == 0:
                            dve.tensor_copy(state[new][:, :], kv).then_inc(state_done, 1)
                        else:
                            dve.scalar_tensor_tensor(state[new][:, :], state[old][:, :], gend[:, c:c + 1], kv,
                                                     ALU.mult, ALU.add).then_inc(state_done, 1)
                        dve.wait_ge(state_hi_done, n + 1)
                        low(state_lo[c + 1][:, :], state[new][:, :], state_hi[c + 1][:, :]).then_inc(state_lo_done, 1)
                        dve.wait_ge(state_done, n + 1)
                    dve.wait_ge(grs_step, 2 * h + 2)
                    for d in range(2):
                        dve.scalar_tensor_tensor(go[:, 2 * h + d, :], ps[2 + d][:, :], tail_cols[:, 2 + d:3 + d],
                                                 grs[1][:, :], ALU.mult, ALU.mult).then_inc(raw_done, 1)
                gate_outputs(SB_HEADS, go, go_hi, go_lo)
                with dve.Fori(0, KT // 2) as i:
                    for j in range(2):
                        used(PAIR_OOUT + i, j)
                        dve.tensor_tensor(x[:, 2 * i + j, :], x[:, 2 * i + j, :], ps[j][:, :], ALU.add)\
                           .then_inc(x_ready, 1)

            for s in (unit_used, prod_done, hid_lo, fy_lo_done, mga_done, logit_done, exp_done, pt_lo_done, merged,
                      u_lo_done, zb_done, gated_f, gated_lo):
                dve.sem_inc(s, CREDIT)
            dve.sem_inc(yf_done, 1)
            dve.memset(eps[:, 0:1], EPS)
            dve.memset(eps[:, 1:2], SUB_EPS)
            dve.memset(ones[:, :], 1.0).then_inc(consts_ready, 1)
            dve.wait_ge(small_in, 16 * SMALL)
            dve.sem_inc(x_ready, KT)
            s5_setup()
            half = 2 * DEPTH * HD
            dve.tensor_tensor(lamp[:, :], lamv[:, 0:half], lamv[:, half:2 * half], ALU.mult).then_inc(setup_step, 1)
            dve.wait_ge(setup_step, 1)
            dve.tensor_reduce(lams[:, :], lamp[:, :].rearrange("p (n c) -> p n c", c=HD), AX.X, ALU.add)\
               .then_inc(setup_step, 1)
            for l in range(DEPTH):
                dve.tensor_scalar(sub_gain[:, l:l + 1], sub_gain[:, l:l + 1], 1.0 - LAM_INIT[l], None, ALU.mult)\
                   .then_inc(setup_step, 1)
            dve.wait_ge(lam_exp, 1)
            dve.tensor_tensor(lamd[:, :], lame[:, DEPTH:2 * DEPTH], lame[:, 0:DEPTH], ALU.subtract)\
               .then_inc(setup_step, 1)
            dve.wait_ge(setup_step, 3 + DEPTH)
            for l in range(DEPTH):
                dve.tensor_scalar(lam_neg[:, l:l + 1], lamd[:, l:l + 1], -LAM_INIT[l], None, ALU.add)\
                   .then_inc(setup_step, 1)
            dve.wait_ge(table_ready, 1)
            dve.tensor_copy(table[:, 0:512], ps[0][0:N_MAPS, :]).then_inc(table_copied, 1)
            dve.tensor_copy(table[:, 512:REL], ps[1][0:N_MAPS, 0:REL - 512]).then_inc(table_copied, 1)
            dve.wait_ge(setup_step, 3 + 2 * DEPTH)
            with dve.Fori(0, DEPTH) as l:
                norm(3 * l, 3 * l)
                ffn_up(2 * l, l * PAIRS_LAYER + PAIR_FFN1)
                ffn_down(l * PAIRS_LAYER + PAIR_DOWN1)
                norm(3 * l + 1, 3 * l + 1)
                fourier(l)
                branch_a(l)
                first_head(l)
                dilated(l)
                diff(l)
                merge(l)
                out_projection(l)
                norm(3 * l + 2, 3 * l + 2)
                ffn_up(2 * l + 1, l * PAIRS_LAYER + PAIR_FFN2)
                ffn_down(l * PAIRS_LAYER + PAIR_DOWN2)
            norm(3 * DEPTH, 0, final=True)
            norm(3 * DEPTH + 1, 3 * DEPTH)
            s5()
            stick_breaking()
            norm(3 * DEPTH + 2, 3 * DEPTH + 1)
            gla()


def tiles(w, c0, c1, k0=0, k1=None):
    return w[128 * k0:None if k1 is None else 128 * k1, c0:c1].reshape(-1, P, c1 - c0).transpose(1, 0, 2)


def weight_units(inp):
    units = []

    def unit(*parts):
        u = np.zeros((P, 8, P), np.float32)
        k = 0
        for t in parts:
            u[:, k:k + t.shape[1], :t.shape[2]] = t
            k += t.shape[1]
        units.append(u.reshape(P, UNIT))

    def col(w, c):
        unit(tiles(w, P * c, P * c + P))

    def ffn(gate, up, down):
        for f in range(FT):
            col(gate, f)
            col(up, f)
        for f in range(FT):
            units.append(down[P * f:P * f + P])

    for l in range(DEPTH):
        w_in, w_gate = inp["w_in"][l], inp["w_gate"][l]
        ffn(inp["w_ffn1_gate"][l], inp["w_ffn1_up"][l], inp["w_ffn1_down"][l])
        for g in range(GROUPS):
            col(w_in, g)
        for c in range(KT):
            col(w_gate, c)
            col(inp["w_br_a"][l], c)
        for n in range(N_DH):
            q, k, v = ((GROUPS + n, GROUPS + N_DIL + n, GROUPS + 2 * N_DIL + n) if n < N_DIL else
                       (14 + n, 18 + n, 22 + n))
            col(w_in, q)
            col(w_in, k)
            unit(tiles(w_in, P * v, P * v + P, 0, 4))
            unit(tiles(w_in, P * v, P * v + P, 4, 8))
        for c in range(KT):
            col(w_gate, KT + c)
            col(w_gate, 2 * KT + c)
            unit(tiles(inp["w_br_c"][l], P * c, P * c + P), tiles(inp["w_br_b"][l], P * c, P * c + P))
        for c in range(KT):
            col(inp["w_out"][l], c)
        ffn(inp["w_ffn2_gate"][l], inp["w_ffn2_up"][l], inp["w_ffn2_down"][l])
    even = inp["even_w_in_2"][0]
    q0, k0, v0, z0, u0, zb0 = (n // P for n in (0, D, 2 * D, 3 * D, 4 * D, 4 * D + S5_W))
    for c in range(UT):
        col(even, u0 + c)
    units += s5_tiles(inp)
    for c in range(UT):
        col(even, zb0 + c)
    glu = inp["s5_w_glu_2"][0]
    for c in range(0, UT, 2):
        unit(tiles(glu, P * c, P * c + P), tiles(glu, P * c + P, P * c + 2 * P))
    for h in range(SB_HEADS):
        for c in (q0, k0, v0, z0):
            col(even, c + h)
    for c in range(KT):
        for half in range(2):
            unit(tiles(inp["even_w_out_2"][0], P * c, P * c + P, 6 * half, 6 * half + 6))
    odd = inp["odd_w_in_2"][0]
    key = D // 2
    q0, k0, v0, z0, r0 = (n // P for n in (0, key, 2 * key, 2 * key + D, 2 * key + 2 * D))
    unit(tiles(odd, P * r0, odd.shape[1]))
    wg = np.zeros((P, 8, P), np.float32)
    w = inp["gla_w_gate_2"][0]
    wg[:w.shape[0], :GLA_HEADS] = w.reshape(w.shape[0], GLA_HEADS, P)
    units.append(wg.reshape(P, UNIT))
    for h in range(GLA_HEADS):
        for c in (q0 + h, k0 + h, v0 + 2 * h, v0 + 2 * h + 1, z0 + 2 * h, z0 + 2 * h + 1):
            col(odd, c)
    for c in range(KT):
        col(inp["odd_w_out_2"][0], c)
    return units


def s5_tiles(inp):
    b = [inp[k][0].transpose(0, 2, 1) for k in ("s5_b_re_2", "s5_b_im_2")]
    c = [inp[k][0].transpose(0, 2, 1) for k in ("s5_c_re_2", "s5_c_im_2")]
    out = []
    for i in range(0, NST, 2):
        u = np.zeros((P, 8, P), np.float32)
        for s in range(2):
            for g in range(2):
                group = 2 * (i + s) + g
                ch = slice(S5_GROUP * (group % 8), S5_GROUP * (group % 8) + S5_GROUP)
                st = slice(S5_STATE * g, S5_STATE * g + S5_STATE)
                for n in range(2):
                    u[ch, 4 * s + n, st] = b[n][group]
                    u[st, 4 * s + 2 + n, ch] = c[n][group]
        out.append(u.reshape(P, UNIT))
    return out


def rel_bucket(rel):
    half, exact = BUCKETS // 2, BUCKETS // 4
    n = np.abs(rel)
    large = exact + (np.log(np.maximum(n, 1) / exact) / math.log(1024 / exact) * (half - exact)).astype(int)
    return np.where(rel > 0, half, 0) + np.where(n < exact, n, np.minimum(large, half - 1))


def shape_constants():
    rel = np.arange(REL) - (S - 1)
    onehot = np.zeros((BUCKETS + N_DIL, REL), np.float32)
    onehot[rel_bucket(rel), np.arange(REL)] = 1.0
    flags = np.zeros((N_DIL, N_MAPS), np.float32)
    for g, (window, dil) in enumerate(DIL):
        onehot[BUCKETS + g] = (np.abs(rel) > window // 2) | (rel % dil != 0)
        flags[g, 2 * g:2 * g + 2] = NEG
    tok = 2 * np.pi * (np.outer(np.arange(S), np.arange(S)) % S) / S
    chan = 2 * np.pi * (np.outer(np.arange(P), np.arange(P)) % P) / P
    cols = [np.cos(tok).reshape(ST, P, S).transpose(1, 0, 2).reshape(P, -1),
            np.sin(tok).reshape(ST, P, S).transpose(1, 0, 2).reshape(P, -1), np.cos(chan), -np.sin(chan)]
    return onehot, flags, (np.concatenate(cols, axis=1) / 16).astype(np.float32)


def same_chunk():
    s, t = np.arange(P)[:, None], np.arange(P)[None]
    return ((s // CH == t // CH) & (s <= t)).astype(np.uint32)


def feature_columns(v):
    return np.ascontiguousarray(v.reshape(-1, P).T)


def kernel(**inputs):
    import concourse.bacc as bacc
    from concourse.bass_utils import run_bass_kernel_spmd

    inp = {k: np.asarray(v) for k, v in inputs.items()}
    units = weight_units(inp)
    assert len(units) == 2 * N_PAIRS, (len(units), N_PAIRS)
    onehot, flags, dft = shape_constants()
    gain_rows = [inp[k][l] for l in range(DEPTH) for k in ("g_ffn1", "g_mix", "g_ffn2")]
    gain_rows += [inp["g_final"], inp["even_norm_g_2"][0], inp["odd_norm_g_2"][0]]
    arrays = {
        "x": np.ascontiguousarray(inp["x"][0].T.reshape(KT, P, S).transpose(1, 0, 2)),
        "weights": np.stack(units),
        "gains": feature_columns(np.concatenate(gain_rows)),
        "gate_bias": feature_columns(inp["b_gate"]),
        "ident": np.eye(P, dtype=np.float32),
        "sub_gain": np.ascontiguousarray(inp["subln_g"].T),
        "onehot": onehot,
        "relt": np.concatenate([inp["rel_bias"], flags]),
        "lam": np.concatenate([inp[k].reshape(1, -1) for k in ("lam_q1", "lam_q2", "lam_k1", "lam_k2")], axis=1),
        "dft": dft,
        "s5_in": np.stack([inp["s5_lambda_re_2"][0].reshape(NST, P).T, inp["s5_lambda_im_2"][0].reshape(NST, P).T,
                           np.repeat(inp["s5_log_dt_2"][0], S5_STATE).reshape(NST, P).T], axis=1),
        "s5_cols": np.stack([inp["s5_d_2"][0].reshape(UT, P).T, inp["s5_b_glu_2"][0].reshape(UT, P).T], axis=1),
        "tail_cols": feature_columns(np.concatenate([inp[k][0] for k in (
            "sb_q_norm_g_2", "sb_k_norm_g_2", "gla_o_norm_g_2", "gla_b_gate_2")])),
        "after": np.concatenate([np.tril(np.ones((P, P)), -1), np.triu(np.ones((P, P)), 1)], axis=1).astype(np.float32),
        "keep": same_chunk(),
    }
    nc = bacc.Bacc("TRN2", target_bir_lowering=False, num_devices=1, dynamic_dma_scratch_size=1024)
    a = {n: nc.dram_tensor("in_" + n, v.shape, mybir.dt.from_np(v.dtype), kind="ExternalInput").ap() for n, v in arrays.items()}
    a["out"] = nc.dram_tensor("out", (P, KT, S), F32, kind="ExternalOutput").ap()
    table = nc.dram_tensor("bias_table", (N_MAPS, P, REL), F32, kind="Internal").ap()
    a["table"] = table
    a["toeplitz"] = lambda m: bass.AP(table.tensor, m * (P * REL) + P - 1, [[REL - 1, P], [1, BW]])
    build_program(nc, a)
    r = run_bass_kernel_spmd(nc, [{"in_" + n: v for n, v in arrays.items()}], core_ids=[0])
    out = r.results[0]["out"]
    return np.ascontiguousarray(out.transpose(1, 0, 2).reshape(D, S).T)[None]
```

```python
import math

import numpy as np
import concourse.bass as bass
from concourse import mybir
from contextlib import ExitStack

F32 = mybir.dt.float32
F32R = mybir.dt.float32r
ACT = mybir.ActivationFunctionType
ALU = mybir.AluOpType
AX = mybir.AxisListType

P = 128
S = 512
D = 1024
KT = D // P
ST = S // P
DEPTH = 2
FF = 2816
FT = FF // P
UNIT = 8 * P
GROUPS = 8
DIL = ((128, 1), (512, 4), (2048, 16))
N_DIL = len(DIL)
N_DIFF = 4
N_MAPS = 2 * N_DIL + N_DIFF
HD = 64
BUCKETS = 32
REL = 2 * S - 1
BW = S + P * (ST - 1)
NEG = -1e30
EPS = 1e-6
SUB_EPS = 1e-5
LAM_INIT = [0.8 - 0.6 * math.exp(-0.3 * l) for l in range(DEPTH)]

PAIR_FFN1 = 0
PAIR_DOWN1 = PAIR_FFN1 + FT
PAIR_FOUR = PAIR_DOWN1 + FT // 2
PAIR_BR_A = PAIR_FOUR + GROUPS // 2
PAIR_HEADS = PAIR_BR_A + KT
PAIR_MERGE = PAIR_HEADS + 2 * (N_DIL + N_DIFF)
PAIR_OUT = PAIR_MERGE + 3 * KT // 2
PAIR_FFN2 = PAIR_OUT + KT // 2
PAIR_DOWN2 = PAIR_FFN2 + FT
PAIRS_LAYER = PAIR_DOWN2 + FT // 2
PAIR_TAIL = DEPTH * PAIRS_LAYER
N_DH = N_DIL + N_DIFF
BIAS_LOADS = 16 * (N_DIL + 1)
STEPS = 15
FILL = (0, 2, 4, 6, 8, 10, 12, 14, 16, 18, 20, 22, 24, 24, 24, 24)
N_T = 8 * N_DIL + 4 * N_DIFF
N_MIX = 13
N_X = KT * (3 * DEPTH + 4)
SB_HEADS = 8
S5_W = 512
UT = S5_W // P
S5_GROUPS, S5_STATE, S5_GROUP = 32, 64, 16
NST = S5_GROUPS * S5_STATE // P
LEVELS = 9
TAU = 16.0
GLA_HEADS = 4
CH = 64
NCH = S // CH
PAIR_U = PAIR_TAIL
PAIR_S5 = PAIR_U + UT // 2
PAIR_ZB = PAIR_S5 + NST // 4
PAIR_GLU = PAIR_ZB + UT // 2
PAIR_SB = PAIR_GLU + 1
PAIR_EOUT = PAIR_SB + 2 * SB_HEADS
PAIR_R = PAIR_EOUT + KT
PAIR_GLA = PAIR_R + 1
PAIR_OOUT = PAIR_GLA + 3 * GLA_HEADS
N_PAIRS = PAIR_OOUT + KT // 2
SCAN_LEVELS = 2 * LEVELS - 1
N_SCAN = 4 * (2 + 3 * SCAN_LEVELS)
LN_EXP = "natural_log_exp_and_others"
GATED = 8
CREDIT = 2


def build_program(nc, a):
    es = ExitStack()
    with es:
        def sb(name, shape, dt=F32):
            return es.enter_context(nc.sbuf_tensor(name, shape, dt))

        def sem(name):
            return es.enter_context(nc.semaphore(name))

        ARENA = 84 * 1024

        def at(name, kb, shape, dt=F32):
            return nc.alloc_sbuf_tensor_at(name, shape, dt, offset=ARENA + int(kb * 1024))

        x = sb("x", [P, KT, S])
        xn_hi = sb("xn_hi", [P, KT, S], F32R)
        xn_lo = sb("xn_lo", [P, KT, S], F32R)
        w_raw = [sb(f"w_raw{i}", [P, UNIT]) for i in range(2)]
        w_hi = [sb(f"w_hi{i}", [P, 8, P], F32R) for i in range(2)]
        w_lo = [sb(f"w_lo{i}", [P, 8, P], F32R) for i in range(2)]
        gains = sb("gains", [P, 9 * KT])
        gate_bias = sb("gate_bias", [P, DEPTH * 3 * KT])
        ident = sb("ident", [P, P])
        ones = sb("ones", [P, P])
        after = sb("after", [P, 2 * P])
        after_r = sb("after_r", [P, P], F32R)
        ones_r = sb("ones_r", [P, P], F32R)
        keep = sb("keep", [P, P], mybir.dt.uint32)
        eps = sb("eps", [P, 2])
        lam_neg = sb("lam_neg", [P, DEPTH])
        sub_gain = sb("sub_gain", [P, DEPTH])
        nmax = sb("nmax", [P, N_DIL + 1, 8])
        rsum = sb("rsum", [P, N_DIL + 1, 8])
        mixw = sb("mixw", [P, 5, 8])
        mixr = sb("mixr", [P, N_DIL, 8])
        rinv = sb("rinv", [P, 4, 2])
        s5_in = sb("s5_in", [P, 3, NST])
        s5_t = sb("s5_t", [P, 12, NST])
        s5_pow = sb("s5_pow", [P, 3, LEVELS, NST])
        s5_now = sb("s5_now", [P, 3, LEVELS, 4])
        s5_coef = sb("s5_coef", [P, 3, NST])
        s5_cols = sb("s5_cols", [P, 2, UT])
        tail_cols = sb("tail_cols", [P, 2 + 2 + GLA_HEADS])

        sq = at("sq", 24, [P, KT, S])
        xf = at("xf", 0, [P, KT, S])
        rlog = at("rlog", 130, [P, S])
        rstd = at("rstd", 132, [P, S])
        h_hi = at("h_hi", 40, [P, FT, S], F32R)
        h_lo = at("h_lo", 84, [P, FT, S], F32R)
        gated = [at(f"gated{j}", 128 + 2 * j, [P, S]) for j in range(2)]
        prod = [at(f"prod{j}", 132 + 2 * j, [P, S]) for j in range(2)]
        mg = at("mg", 0, [P, KT, S])
        yb_hi = at("yb_hi", 16, [P, 1, S], F32R)
        yb_lo = at("yb_lo", 18, [P, 1, S], F32R)
        yc_hi = at("yc_hi", 20, [P, N_DIFF, S], F32R)
        yc_lo = at("yc_lo", 28, [P, N_DIFF, S], F32R)
        ya_hi = at("ya_hi", 40, [P, GROUPS, S], F32R)
        ya_lo = at("ya_lo", 56, [P, GROUPS, S], F32R)
        dft_raw = at("dft_raw", 40, [P, 8 * S + 2 * P])
        dft_hi = at("dft_hi", 72, [P, 8 * S + 2 * P], F32R)
        dft_lo = at("dft_lo", 90, [P, 8 * S + 2 * P], F32R)
        fa_hi = [at(f"fa_hi{j}", 108 + 2 * j, [P, S], F32R) for j in range(2)]
        fa_lo = [at(f"fa_lo{j}", 112 + 2 * j, [P, S], F32R) for j in range(2)]
        fp_hi = [at(f"fp_hi{j}", 116 + 4 * j, [P, ST, 2 * P], F32R) for j in range(2)]
        fp_lo = [at(f"fp_lo{j}", 124 + 4 * j, [P, ST, 2 * P], F32R) for j in range(2)]
        sig = [at(f"sig{j}", 132 + 2 * j, [P, S]) for j in range(2)]
        q_hi = at("q_hi", 40, [P, S], F32R)
        q_lo = at("q_lo", 42, [P, S], F32R)
        k_hi = at("k_hi", 44, [P, S], F32R)
        k_lo = at("k_lo", 46, [P, S], F32R)
        v_hi = at("v_hi", 48, [P, ST, P], F32R)
        v_lo = at("v_lo", 50, [P, ST, P], F32R)
        logit = [at(f"logit{j}", 52 + 2 * j, [P, S]) for j in range(2)]
        prob = at("prob", 56, [P, 8, S])
        pt_hi = [at(f"pt_hi{m}", 72 + 24 * m, [P, ST, S], F32R) for m in range(2)]
        pt_lo = [at(f"pt_lo{m}", 80 + 24 * m, [P, ST, S], F32R) for m in range(2)]
        bias = at("bias", 88, [P, N_DIFF, 2 * S])
        og = at("og", 112, [P, N_DIL, 8, HD])
        ybf = at("ybf", 118, [P, 8, HD])
        ybt = at("ybt", 120, [P, 8, HD])
        amap = [at(f"amap{j}", 122 + 2 * j, [P, S]) for j in range(2)]
        amap0 = at("amap0", 126, [P, S])
        of = at("of", 128, [P, S])
        osq = at("osq", 130, [P, S])
        olog = at("olog", 130, [P, S])
        orstd = at("orstd", 132, [P, S])
        onorm = at("onorm", 134, [P, S])
        vf = at("vf", 136, [P, S])
        m_hi = at("m_hi", 40, [P, KT, S], F32R)
        m_lo = at("m_lo", 56, [P, KT, S], F32R)
        sigb = [at(f"sigb{j}", 72 + 2 * j, [P, S]) for j in range(2)]
        sigc = [at(f"sigc{j}", 76 + 2 * j, [P, S]) for j in range(2)]
        tmpb = [at(f"tmpb{j}", 80 + 2 * j, [P, S]) for j in range(2)]
        tmpc = [at(f"tmpc{j}", 84 + 2 * j, [P, S]) for j in range(2)]
        uf = at("uf", 0, [P, UT, S])
        u_hi = at("u_hi", 8, [P, UT, S], F32R)
        u_lo = at("u_lo", 16, [P, UT, S], F32R)
        bx = [at(f"bx{j}", 24 + 4 * j, [P, 2, S]) for j in range(2)]
        sc = [at(f"sc{j}", kb, [P, 2, S]) for j, kb in enumerate((32, 36, 124, 128))]
        st_hi = [at(f"st_hi{j}", kb, [P, 2, S], F32R) for j, kb in enumerate((40, 44, 84, 88))]
        st_lo = [at(f"st_lo{j}", kb, [P, 2, S], F32R) for j, kb in enumerate((48, 52, 92, 96))]
        yf = [at(f"yf{j}", 56 + 2 * j, [P, S]) for j in range(2)]
        ge = at("ge", 60, [P, UT, S])
        ge_hi = at("ge_hi", 68, [P, UT, S], F32R)
        ge_lo = at("ge_lo", 76, [P, UT, S], F32R)
        zb = at("zb", 84, [P, UT, S])
        glu = [at(f"glu{j}", 92 + 2 * j, [P, S]) for j in range(2)]
        ob_f = [at(f"ob_f{j}", 96 + 2 * j, [P, S]) for j in range(2)]
        eo_hi = at("eo_hi", 100, [P, SB_HEADS + UT, S], F32R)
        eo_lo = at("eo_lo", 0, [P, SB_HEADS + UT, S], F32R)
        sbq = [at(f"sbq{j}", 24 + 2 * j, [P, S]) for j in range(2)]
        sbs = [at(f"sbs{j}", 28 + 2 * j, [P, S]) for j in range(2)]
        sbl = [at(f"sbl{j}", 32 + 2 * j, [P, S]) for j in range(2)]
        sbn_hi = [at(f"sbn_hi{j}", 36 + 2 * j, [P, S], F32R) for j in range(2)]
        sbn_lo = [at(f"sbn_lo{j}", 40 + 2 * j, [P, S], F32R) for j in range(2)]
        sv_hi = at("sv_hi", 44, [P, ST, P], F32R)
        sv_lo = at("sv_lo", 46, [P, ST, P], F32R)
        svf = at("svf", 48, [P, S])
        za = [at(f"za{j}", 50 + 2 * j, [P, S]) for j in range(2)]
        zm = [at(f"zm{j}", 54 + 2 * j, [P, S]) for j in range(2)]
        ze = [at(f"ze{j}", 58 + 2 * j, [P, S]) for j in range(2)]
        lom = [at(f"lom{j}", 62 + 2 * j, [P, S]) for j in range(2)]
        lom_hi = at("lom_hi", 66, [P, ST, S], F32R)
        lom_lo = at("lom_lo", 74, [P, ST, S], F32R)
        ww = [at(f"ww{j}", 82 + 2 * j, [P, S]) for j in range(2)]
        w_hi_t = at("w_hi_t", 86, [P, ST, S], F32R)
        w_lo_t = at("w_lo_t", 124, [P, ST, S], F32R)
        eo = at("eo", 100, [P, SB_HEADS, S])
        ez = at("ez", 0, [P, SB_HEADS, S])
        r_hi = at("r_hi", 0, [P, S], F32R)
        r_lo = at("r_lo", 2, [P, S], F32R)
        gx = [at(f"gx{j}", 4 + 2 * j, [P, S]) for j in range(2)]
        ga = [at(f"ga{j}", 8 + 2 * j, [P, S]) for j in range(2)]
        gl = [at(f"gl{j}", 12 + 2 * j, [P, S]) for j in range(2)]
        gcum = at("gcum", 16, [P, GLA_HEADS, S])
        restart = at("restart", 24, [P, S])
        gexp = [at(f"gexp{j}", 28 + 2 * j, [P, S]) for j in range(3)]
        gdiff = at("gdiff", 34, [P, S])
        gend = at("gend", 36, [P, NCH])
        gq = [at(f"gq{j}", 38 + 2 * j, [P, S]) for j in range(3)]
        gq_hi = [at(f"gq_hi{j}", 44 + 2 * j, [P, S], F32R) for j in range(2)]
        gq_lo = [at(f"gq_lo{j}", 48 + 2 * j, [P, S], F32R) for j in range(2)]
        kd_hi = at("kd_hi", 52, [P, ST, P], F32R)
        kd_lo = at("kd_lo", 54, [P, ST, P], F32R)
        gv_hi = at("gv_hi", 56, [P, ST, 2 * P], F32R)
        gv_lo = at("gv_lo", 60, [P, ST, 2 * P], F32R)
        score = at("score", 64, [P, ST, P])
        score_hi = at("score_hi", 66, [P, ST, P], F32R)
        score_lo = at("score_lo", 68, [P, ST, P], F32R)
        state = [at(f"state{j}", 70 + j, [P, 2 * P]) for j in range(2)]
        state_hi = [at(f"state_hi{j}", j, [P, 2 * P], F32R) for j in range(NCH)]
        state_lo = [at(f"state_lo{j}", NCH + j, [P, 2 * P], F32R) for j in range(NCH)]
        gvf = [at(f"gvf{j}", 84 + 2 * j, [P, S]) for j in range(2)]
        gsq = [at(f"gsq{j}", 76 + 2 * j, [P, S]) for j in range(2)]
        grs = [at(f"grs{j}", 80 + 2 * j, [P, S]) for j in range(2)]
        go_hi = at("go_hi", 96, [P, KT, S], F32R)
        go_lo = at("go_lo", 112, [P, KT, S], F32R)
        go = at("go", 96, [P, KT, S])
        gz = at("gz", 112, [P, KT, S])
        gate = [at(f"gate{j}", 88 + 2 * j, [P, S]) for j in range(2)]
        gated_o = [at(f"gated_o{j}", 92 + 2 * j, [P, S]) for j in range(2)]
        onehot = at("onehot", 40, [BUCKETS + N_DIL, REL])
        relt = at("relt", 48, [BUCKETS + N_DIL, N_MAPS])
        table = at("table", 17, [N_MAPS, REL])
        lamv = at("lamv", 54, [P, 4 * DEPTH * HD])
        lamp = at("lamp", 56, [P, 2 * DEPTH * HD])
        lams = at("lams", 57, [P, 2 * DEPTH])
        lame = at("lame", 57.25, [P, 2 * DEPTH])
        lamd = at("lamd", 57.5, [P, DEPTH])

        ps = [es.enter_context(nc.psum_tensor(f"ps{i}", [P, S], F32)) for i in range(8)]

        bu_banks = ((0, 1), (2, 3), (5, 6), (7, 4))

        def kv_bank(c):
            return ps[4 + 2 * (c % 2) + c // 4][:, (c // 2 % 2) * 2 * P:(c // 2 % 2 + 1) * 2 * P]

        unit_loaded = [sem(f"unit_loaded{i}") for i in range(2)]
        unit_hi = sem("unit_hi")
        unit_lo = sem("unit_lo")
        unit_used = sem("unit_used")
        small_in = sem("small_in")
        x_in = sem("x_in")
        consts_ready = sem("consts_ready")
        setup_step = sem("setup_step")
        table_ready = sem("table_ready")
        table_copied = sem("table_copied")
        table_out = sem("table_out")
        x_ready = sem("x_ready")
        x_out = sem("x_out")
        sq_done = sem("sq_done")
        ms_done = sem("ms_done")
        rlog_done = sem("rlog_done")
        rstd_done = sem("rstd_done")
        xf_done = sem("xf_done")
        xh_done = sem("xh_done")
        xn_done = sem("xn_done")
        gate_done = sem("gate_done")
        prod_done = sem("prod_done")
        hid_hi = sem("hid_hi")
        hid_lo = sem("hid_lo")
        dft_in = sem("dft_in")
        dft_hi_done = sem("dft_hi_done")
        dft_lo_done = sem("dft_lo_done")
        fa_hi_done = sem("fa_hi_done")
        fa_lo_done = sem("fa_lo_done")
        fp_mm = sem("fp_mm")
        fp_hi_done = sem("fp_hi_done")
        fp_lo_done = sem("fp_lo_done")
        fy_mm = sem("fy_mm")
        fy_hi_done = sem("fy_hi_done")
        fy_lo_done = sem("fy_lo_done")
        siga_done = sem("siga_done")
        mga_done = sem("mga_done")
        bias_in = [sem(f"bias_in{m}") for m in range(2)]
        head_bias_in = sem("head_bias_in")
        vf_done = sem("vf_done")
        vt_done = sem("vt_done")
        qkv_hi = sem("qkv_hi")
        qkv_lo = sem("qkv_lo")
        s_done = sem("s_done")
        logit_done = sem("logit_done")
        nmax_done = sem("nmax_done")
        exp_done = sem("exp_done")
        amap_step = sem("amap_step")
        amap0_done = sem("amap0_done")
        t_done = sem("t_done")
        pt_hi_done = sem("pt_hi_done")
        pt_lo_done = sem("pt_lo_done")
        o_done = sem("o_done")
        ot_done = sem("ot_done")
        og_done = sem("og_done")
        mix_step = sem("mix_step")
        mix_exp = sem("mix_exp")
        ybt_done = sem("ybt_done")
        yb_hi_done = sem("yb_hi_done")
        yb_lo_done = sem("yb_lo_done")
        ov_done = sem("ov_done")
        osq_done = sem("osq_done")
        oms_done = sem("oms_done")
        olog_done = sem("olog_done")
        orstd_done = sem("orstd_done")
        onorm_done = sem("onorm_done")
        yc_hi_done = sem("yc_hi_done")
        yc_lo_done = sem("yc_lo_done")
        sigbc_done = sem("sigbc_done")
        merge_step = sem("merge_step")
        merged = sem("merged")
        m_hi_done = sem("m_hi_done")
        m_lo_done = sem("m_lo_done")

        s5_step = sem("s5_step")
        s5_tables = sem("s5_tables")
        u_hi_done = sem("u_hi_done")
        u_lo_done = sem("u_lo_done")
        bu_mm = sem("bu_mm")
        bx_done = sem("bx_done")
        s5_now_set = sem("s5_now_set")
        scan_step = sem("scan_step")
        st_hi_done = sem("st_hi_done")
        st_lo_done = sem("st_lo_done")
        yf_done = sem("yf_done")
        ge_done = sem("ge_done")
        ge_hi_done = sem("ge_hi_done")
        ge_lo_done = sem("ge_lo_done")
        zb_done = sem("zb_done")
        glu_done = sem("glu_done")
        ob_step = sem("ob_step")
        ob_hi_done = sem("ob_hi_done")
        ob_lo_done = sem("ob_lo_done")
        masks_r = sem("masks_r")
        sbq_done = sem("sbq_done")
        sbms_done = sem("sbms_done")
        sblog_done = sem("sblog_done")
        sbr_done = sem("sbr_done")
        sbn_done = sem("sbn_done")
        sb_hi_done = sem("sb_hi_done")
        sb_lo_done = sem("sb_lo_done")
        sz_done = sem("sz_done")
        svf_done = sem("svf_done")
        svt_done = sem("svt_done")
        raw_done = sem("raw_done")
        gate_made = sem("gate_made")
        gated_f = sem("gated_f")
        gated_hi = sem("gated_hi")
        gated_lo = sem("gated_lo")
        z_done = sem("z_done")
        za_done = sem("za_done")
        ze_done = sem("ze_done")
        zl_done = sem("zl_done")
        zm_step = sem("zm_step")
        lom_done = sem("lom_done")
        lom_hi_done = sem("lom_hi_done")
        lom_lo_done = sem("lom_lo_done")
        rest_done = sem("rest_done")
        wlog_done = sem("wlog_done")
        w_exp_done = sem("w_exp_done")
        w_masked = sem("w_masked")
        wt_hi_done = sem("wt_hi_done")
        wt_lo_done = sem("wt_lo_done")
        sbo_done = sem("sbo_done")
        r_hi_done = sem("r_hi_done")
        r_lo_done = sem("r_lo_done")
        gx_step = sem("gx_step")
        ga_step = sem("ga_step")
        gcum_set = sem("gcum_set")
        gcum_done = sem("gcum_done")
        gd_done = sem("gd_done")
        gexp_done = sem("gexp_done")
        gq_done = sem("gq_done")
        gq_hi_done = sem("gq_hi_done")
        gq_lo_done = sem("gq_lo_done")
        kdt_done = sem("kdt_done")
        kd_hi_done = sem("kd_hi_done")
        kd_lo_done = sem("kd_lo_done")
        gvf_done = sem("gvf_done")
        gvt_done = sem("gvt_done")
        gv_hi_done = sem("gv_hi_done")
        gv_lo_done = sem("gv_lo_done")
        sc_mm = sem("sc_mm")
        score_done = sem("score_done")
        score_hi_done = sem("score_hi_done")
        score_lo_done = sem("score_lo_done")
        kv_done = sem("kv_done")
        state_done = sem("state_done")
        state_hi_done = sem("state_hi_done")
        state_lo_done = sem("state_lo_done")
        go_mm = sem("go_mm")
        gsq_done = sem("gsq_done")
        gms_done = sem("gms_done")
        grs_step = sem("grs_step")
        gz_done = sem("gz_done")

        block = es.enter_context(nc.Block())

        SMALL = 12

        @block.sync
        def _(sp):
            for dst, name in ((gains, "gains"), (gate_bias, "gate_bias"), (ident, "ident"),
                              (sub_gain, "sub_gain"), (after, "after"), (keep, "keep"), (onehot, "onehot"), (relt, "relt")):
                sp.dma_start(dst[:, :], a[name]).then_inc(small_in, 16)
            sp.dma_start(lamv[:, :], a["lam"].to_broadcast([P, 4 * DEPTH * HD])).then_inc(small_in, 16)
            sp.dma_start(s5_in[:, :, :], a["s5_in"]).then_inc(small_in, 16)
            sp.dma_start(s5_cols[:, :, :], a["s5_cols"]).then_inc(small_in, 16)
            sp.dma_start(tail_cols[:, :], a["tail_cols"]).then_inc(small_in, 16)
            sp.dma_start(x[:, :, :], a["x"]).then_inc(x_in, 16)
            for j in range(2):
                sp.dma_start(w_raw[j][:, :], a["weights"][j]).then_inc(unit_loaded[j], 16)
            with sp.Fori(1, N_PAIRS) as p:
                for j in range(2):
                    sp.wait_ge(unit_lo, 2 * p + j - 1)
                    sp.dma_start(w_raw[j][:, :], a["weights"][2 * p + j]).then_inc(unit_loaded[j], 16)
            sp.wait_ge(x_ready, N_X)
            sp.dma_start(a["out"], x[:, :, :]).then_inc(x_out, 16)
            sp.wait_ge(x_out, 16)

        @block.gpsimd
        def _(pool):
            with pool.Fori(0, N_PAIRS) as p:
                for j in range(2):
                    pool.wait_ge(unit_hi, 2 * p + j + 1)
                    pool.tensor_tensor(w_lo[j][:, :, :], w_raw[j][:, :].rearrange("p (k m) -> p k m", k=8),
                                       w_hi[j][:, :, :].bitcast(F32), ALU.subtract).then_inc(unit_lo, 1)

        @block.tensor
        def _(pe):
            def three(out, lh, ll, rh, rl, first, last):
                pe.matmul(out, lh, rh, start=first, stop=False)
                pe.matmul(out, lh, rl, start=False, stop=False)
                return pe.matmul(out, ll, rh, start=False, stop=last)

            def unit_arrived(pair, j):
                pe.wait_ge(unit_lo, 2 * pair + j + 1)

            def project(pair, j, out, in_hi, in_lo, norms=None, arrived=None):
                unit_arrived(pair, j)
                for k in range(KT):
                    if norms is not None:
                        pe.wait_ge(xn_done, KT * (norms - 1) + k + 1)
                    if arrived:
                        arrived(k)
                    last = three(out, w_hi[j][:, k, :], w_lo[j][:, k, :], in_hi[:, k, :], in_lo[:, k, :],
                                 k == 0, k == KT - 1)
                last.then_inc(unit_used, 1)

            def norm(n, bank):
                for k in range(KT):
                    pe.wait_ge(sq_done, KT * n + k + 1)
                    last = pe.matmul(ps[bank][:, :], ones[:, :], sq[:, k, :], start=k == 0, stop=k == KT - 1)
                last.then_inc(ms_done, 1)

            def ffn_up(r, pair0, n):
                with pe.Fori(0, FT // 2) as i:
                    for j in range(2):
                        pe.wait_ge(prod_done, r * FT + 2 * i + j + 1)
                        project(pair0 + 2 * i + j, 0, ps[2 * j][:, :], xn_hi, xn_lo, norms=None if j else n + 1)
                        project(pair0 + 2 * i + j, 1, ps[2 * j + 1][:, :], xn_hi, xn_lo)

            def ffn_down(r, pair0):
                def tile(pair, j, f, first, last):
                    pe.wait_ge(hid_lo, CREDIT + r * FT + f + 1)
                    unit_arrived(pair, j)
                    for m in range(KT):
                        mm = three(ps[m][:, :], w_hi[j][:, m, :], w_lo[j][:, m, :],
                                   h_hi[:, f, :], h_lo[:, f, :], first, last)
                    mm.then_inc(unit_used, 1)
                pe.wait_ge(prod_done, CREDIT + (r + 1) * FT)
                tile(pair0, 0, 0, True, False)
                tile(pair0, 1, 1, False, False)
                with pe.Fori(1, FT // 2 - 1) as i:
                    for j in range(2):
                        tile(pair0 + i, j, 2 * i + j, False, False)
                tile(pair0 + FT // 2 - 1, 0, FT - 2, False, False)
                tile(pair0 + FT // 2 - 1, 1, FT - 1, False, True)

            def fourier(l):
                COS, SIN, CH = 0, 4 * S, 8 * S
                with pe.Fori(0, GROUPS // 2) as i:
                    g0 = l * GROUPS + 2 * i
                    for j in range(2):
                        pe.wait_ge(fy_lo_done, g0 + j + 1)
                        project(l * PAIRS_LAYER + PAIR_FOUR + i, j, ps[j][:, :], xn_hi, xn_lo,
                                norms=None if j else 3 * l + 2)
                    pe.wait_ge(dft_lo_done, l + 1)
                    for j in range(2):
                        pe.wait_ge(fa_lo_done, g0 + j + 1)
                        for t in range(ST):
                            out = ps[2 + 2 * j + t // 2][:, (t % 2) * 2 * P:(t % 2 + 1) * 2 * P]
                            last = three(out, fa_hi[j][:, t * P:(t + 1) * P], fa_lo[j][:, t * P:(t + 1) * P],
                                         dft_hi[:, CH:CH + 2 * P], dft_lo[:, CH:CH + 2 * P], True, True)
                        last.then_inc(fp_mm, 1)
                    for j in range(2):
                        pe.wait_ge(fp_lo_done, 2 * (g0 + j + 1))
                        for c in range(2):
                            for t in range(ST):
                                o = (COS, SIN)[c] + t * S
                                last = three(ps[j][:, :], fp_hi[j][:, t, c * P:(c + 1) * P],
                                             fp_lo[j][:, t, c * P:(c + 1) * P],
                                             dft_hi[:, o:o + S], dft_lo[:, o:o + S],
                                             c == 0 and t == 0, c == 1 and t == ST - 1)
                        last.then_inc(fy_mm, 1)

            def branch_a(l):
                with pe.Fori(0, KT // 2) as i:
                    pe.wait_ge(fy_lo_done, CREDIT + (l + 1) * GROUPS)
                    for j in range(2):
                        c = 2 * i + j
                        pair = l * PAIRS_LAYER + PAIR_BR_A + c
                        pe.wait_ge(mga_done, l * KT + c + 1)
                        project(pair, 0, ps[2 * j][:, :], xn_hi, xn_lo)
                        project(pair, 1, ps[2 * j + 1][:, :], ya_hi, ya_lo)

            def qkv(pair, n):
                half, tile = divmod(n, KT + KT // 2)
                slot, tile = divmod(tile, KT)
                bank, k = (2, KT // 2 * half + tile) if slot else ((0, 1)[half], tile)
                if tile == 0:
                    unit_arrived(pair + half, slot)
                last = three(ps[bank][:, :], w_hi[slot][:, tile, :], w_lo[slot][:, tile, :],
                             xn_hi[:, k, :], xn_lo[:, k, :], k == 0, k == KT - 1)
                if tile == (KT // 2 - 1 if slot else KT - 1):
                    last.then_inc(unit_used, 1)

            def v_transposed(q):
                pe.wait_ge(vf_done, q + 1)
                for t in range(ST):
                    last = pe.transpose(ps[2][:, t * P:(t + 1) * P], vf[:, t * P:(t + 1) * P], ident[:, :])
                last.then_inc(vt_done, 1)

            def double_head(q, tile_of, transposed_ready, next_pair, last_head=None):
                for step in range(STEPS):
                    if step < 8:
                        m, t = tile_of(step)
                        r = slice(HD * m, HD * m + HD)
                        if step == 0:
                            pe.wait_ge(qkv_lo, 3 * q + 2)
                        pe.wait_ge(logit_done, 8 * q + step + 1)
                        three(ps[3 + step % 2][:, :], q_hi[r, t * P:(t + 1) * P], q_lo[r, t * P:(t + 1) * P],
                              k_hi[r, :], k_lo[r, :], True, True).then_inc(s_done, 1)
                        if step == 1:
                            v_transposed(q)
                            if last_head:
                                last_head()
                    if step >= 8:
                        transposed_ready(step)
                    if next_pair is not None:
                        if step == 4:
                            pe.wait_ge(qkv_lo, 3 * q + 3)
                        for n in range(FILL[step], FILL[step + 1]):
                            qkv(next_pair, n)
                    if step < 8:
                        transposed_ready(step)

            def first_head(l):
                pe.wait_ge(mga_done, CREDIT + (l + 1) * KT)
                for n in range(3 * KT):
                    qkv(l * PAIRS_LAYER + PAIR_HEADS, n)

            def dilated(l):
                with pe.Fori(0, N_DIL) as g:
                    q = l * N_DH + g
                    tq = l * N_T + 8 * g

                    def transposed(step):
                        i = step - 2
                        if not 0 <= i < 8:
                            return
                        pe.wait_ge(exp_done, CREDIT + 8 * q + i + 1)
                        pe.wait_ge(pt_lo_done, tq + i + 1)
                        for kb in range(ST):
                            last = pe.transpose(ps[5 + i % 2][:, kb * P:(kb + 1) * P],
                                                prob[:, i, kb * P:(kb + 1) * P], ident[:, :])
                        last.then_inc(t_done, 1)

                    double_head(q, lambda s: divmod(s, ST), transposed, l * PAIRS_LAYER + PAIR_HEADS + 2 * g + 2)
                    pe.wait_ge(qkv_lo, 3 * q + 3)
                    for m in range(2):
                        pe.wait_ge(pt_lo_done, CREDIT + tq + 4 * m + 4)
                        for kb in range(ST):
                            last = three(ps[(7, 3)[m]][:, :], v_hi[:, kb, :], v_lo[:, kb, :],
                                         pt_hi[m][:, kb, :], pt_lo[m][:, kb, :], kb == 0, kb == ST - 1)
                    last.then_inc(o_done, 1)
                    pe.wait_ge(og_done, 3 * (l * N_DIL + g) + 2)
                    for t in range(ST):
                        last = pe.transpose(ps[7][:, t * P:(t + 1) * P], of[:, t * P:(t + 1) * P], ident[:, :])
                    last.then_inc(ot_done, 1)

            def diff(l):
                def mean_square(dq):
                    pe.wait_ge(osq_done, dq + 1)
                    pe.matmul(ps[5][:, :], ones[:, :], osq[:, :], start=True, stop=True).then_inc(oms_done, 1)

                def head(h, has_last, has_next):
                    q = l * N_DH + N_DIL + h
                    dq = l * N_DIFF + h
                    tq = l * N_T + 8 * N_DIL + 4 * h

                    def transposed(step):
                        t, odd = divmod(step - 5, 2)
                        if odd or not 0 <= t < ST:
                            return
                        pe.wait_ge(amap_step, 3 * (4 * dq + t + 1))
                        pe.wait_ge(pt_lo_done, tq + t + 1)
                        for kb in range(ST):
                            last = pe.transpose(ps[5 + t % 2][:, kb * P:(kb + 1) * P],
                                                amap[t % 2][:, kb * P:(kb + 1) * P], ident[:, :])
                        last.then_inc(t_done, 1)

                    double_head(q, lambda s: (s % 2, s // 2), transposed,
                                l * PAIRS_LAYER + PAIR_HEADS + 2 * N_DIL + 2 * h + 2 if has_next else None,
                                (lambda: mean_square(dq - 1)) if has_last else None)
                    pe.wait_ge(qkv_lo, 3 * q + 3)
                    pe.wait_ge(pt_lo_done, CREDIT + tq + 4)
                    for kb in range(ST):
                        last = three(ps[7][:, :], v_hi[:, kb, :], v_lo[:, kb, :],
                                     pt_hi[0][:, kb, :], pt_lo[0][:, kb, :], kb == 0, kb == ST - 1)
                    last.then_inc(ov_done, 1)

                head(0, False, True)
                with pe.Fori(1, N_DIFF - 1) as h:
                    head(h, True, True)
                head(N_DIFF - 1, True, False)
                mean_square(l * N_DIFF + N_DIFF - 1)
                pe.wait_ge(mix_step, N_MIX * (l + 1))
                for t in range(ST):
                    src = ybf[:, 2 * t:2 * t + 2, :].rearrange("p m e -> p (m e)")
                    last = pe.transpose(ps[7][:, t * P:(t + 1) * P], src, ident[:, :])
                last.then_inc(ybt_done, 1)

            def merge(l):
                with pe.Fori(0, KT // 2) as i:
                    for j in range(2):
                        pair = l * PAIRS_LAYER + PAIR_MERGE + 3 * i
                        b = 4 * j
                        pe.wait_ge(merged, l * KT + 2 * i + j + 1)
                        u = 3 * j
                        project(pair + u // 2, u % 2, ps[b][:, :], xn_hi, xn_lo)
                        u = 3 * j + 1
                        project(pair + u // 2, u % 2, ps[b + 1][:, :], xn_hi, xn_lo)
                        u = 3 * j + 2
                        s = u % 2
                        unit_arrived(pair + u // 2, s)
                        pe.wait_ge(yc_lo_done, (l + 1) * N_DIFF)
                        pe.wait_ge(yb_lo_done, l + 1)
                        three(ps[b + 2][:, :], w_hi[s][:, 4, :], w_lo[s][:, 4, :], yb_hi[:, 0, :], yb_lo[:, 0, :],
                              True, True)
                        for k in range(N_DIFF):
                            last = three(ps[b + 3][:, :], w_hi[s][:, k, :], w_lo[s][:, k, :],
                                         yc_hi[:, k, :], yc_lo[:, k, :], k == 0, k == N_DIFF - 1)
                        last.then_inc(unit_used, 1)

            def out_projection(l):
                with pe.Fori(0, KT // 2) as i:
                    pe.wait_ge(m_lo_done, (l + 1) * KT)
                    for j in range(2):
                        pe.wait_ge(x_ready, KT * (3 * l + 2) + 2 * i + j - 1)
                        project(l * PAIRS_LAYER + PAIR_OUT + i, j, ps[j][:, :], m_hi, m_lo)

            def single(out, w, rh, rl, first, last):
                pe.matmul(out, w, rh, start=first, stop=False)
                return pe.matmul(out, w, rl, start=False, stop=last)

            def s5():
                for c in range(UT):
                    project(PAIR_U + c // 2, c % 2, ps[c][:, :], xn_hi, xn_lo, norms=None if c else 3 * DEPTH + 1)
                with pe.Fori(0, UT) as c:
                    pe.wait_ge(u_lo_done, CREDIT + UT)
                    pe.wait_ge(yf_done, c + 1)
                    for s in range(4):
                        if s % 2 == 0:
                            unit_arrived(PAIR_S5 + c, s // 2)
                        for b in range(2):
                            w = 4 * (s % 2) + b
                            last = three(ps[bu_banks[s][b]][:, :], w_hi[s // 2][:, w, :], w_lo[s // 2][:, w, :],
                                         u_hi[:, c, :], u_lo[:, c, :], True, True)
                        last.then_inc(bu_mm, 1)
                    for s in range(4):
                        pe.wait_ge(st_lo_done, 4 * c + s + 1)
                        for b in range(2):
                            w = 4 * (s % 2) + 2 + b
                            last = three(ps[4][:, :], w_hi[s // 2][:, w, :], w_lo[s // 2][:, w, :],
                                         st_hi[s][:, b, :], st_lo[s][:, b, :],
                                         s == 0 and b == 0, s == 3 and b == 1)
                        if s % 2:
                            last.then_inc(unit_used, 1)
                with pe.Fori(0, UT // 2) as i:
                    for j in range(2):
                        pe.wait_ge(zb_done, 2 * i + j + 1)
                        project(PAIR_ZB + i, j, ps[2 * j][:, :], xn_hi, xn_lo)
                for c in range(UT):
                    if c % 2 == 0:
                        unit_arrived(PAIR_GLU, c // 2)
                    if c == 0:
                        pe.wait_ge(ge_lo_done, UT)
                    for k in range(UT):
                        w = UT * (c % 2) + k
                        last = three(ps[4 + c][:, :], w_hi[c // 2][:, w, :], w_lo[c // 2][:, w, :],
                                     ge_hi[:, k, :], ge_lo[:, k, :], k == 0, k == UT - 1)
                    if c % 2:
                        last.then_inc(unit_used, 1)

            def stick_breaking():
                def mean_square(h, j):
                    pe.wait_ge(sbq_done, 2 * (2 * h + j + 1))
                    pe.matmul(ps[j][:, :], ones[:, :], sbs[j][:, :], start=True, stop=True).then_inc(sbms_done, 1)

                def gate_argument(h, pair):
                    pe.wait_ge(sblog_done, 2 * h + 1)
                    project(pair + 1, 1, ps[0][:, :], xn_hi, xn_lo)

                def v_transposed(h):
                    pe.wait_ge(svf_done, h + 1)
                    for t in range(ST):
                        last = pe.transpose(ps[2][:, t * P:(t + 1) * P], svf[:, t * P:(t + 1) * P], ident[:, :])
                    last.then_inc(svt_done, 1)

                def logits(h, n):
                    b = ST - 1 - n
                    if n >= 2:
                        pe.wait_ge(lom_done, ST * h + n - 1)
                    three(ps[5 + n % 2][:, 0:S - b * P], sbn_hi[1][:, b * P:(b + 1) * P],
                          sbn_lo[1][:, b * P:(b + 1) * P], sbn_hi[0][:, b * P:S], sbn_lo[0][:, b * P:S],
                          True, True).then_inc(z_done, 1)

                def rest(h, n):
                    b = ST - 1 - n
                    pe.wait_ge(lom_lo_done, ST * h + n + 1)
                    if n >= 2:
                        pe.wait_ge(wlog_done, ST * h + n - 1)
                    out = ps[3 + n % 2]
                    last = single(out[:, 0:S - b * P], after_r[:, :], lom_hi[:, b, b * P:S], lom_lo[:, b, b * P:S],
                                  True, b == ST - 1)
                    for e in range(b + 1, ST):
                        last = single(out[:, (e - b) * P:S - b * P], ones_r[:, :], lom_hi[:, e, e * P:S],
                                      lom_lo[:, e, e * P:S], False, e == ST - 1)
                    last.then_inc(rest_done, 1)

                def head(h, has_next):
                    pair = PAIR_SB + 2 * h + 2
                    pe.wait_ge(sb_lo_done, 3 * h + 2)
                    logits(h, 0)
                    logits(h, 1)
                    if has_next:
                        pe.wait_ge(sz_done, h + 1)
                        project(pair, 0, ps[0][:, :], xn_hi, xn_lo)
                    rest(h, 0)
                    logits(h, 2)
                    if has_next:
                        project(pair, 1, ps[1][:, :], xn_hi, xn_lo)
                    rest(h, 1)
                    logits(h, 3)
                    pe.wait_ge(sb_lo_done, 3 * h + 3)
                    if has_next:
                        mean_square(h + 1, 0)
                        project(pair + 1, 0, ps[2][:, :], xn_hi, xn_lo)
                    rest(h, 2)
                    if has_next:
                        mean_square(h + 1, 1)
                    rest(h, 3)
                    if has_next:
                        gate_argument(h + 1, pair)
                    pe.wait_ge(wt_lo_done, ST * (h + 1))
                    for b in range(ST):
                        last = three(ps[7][:, b * P:S], sv_hi[:, b, :], sv_lo[:, b, :],
                                     w_hi_t[:, b, b * P:S], w_lo_t[:, b, b * P:S], b == 0, b == ST - 1)
                    last.then_inc(sbo_done, 1)
                    if has_next:
                        v_transposed(h + 1)

                pe.wait_ge(zb_done, CREDIT + UT)
                for j in range(2):
                    project(PAIR_SB, j, ps[j][:, :], xn_hi, xn_lo)
                for j in range(2):
                    mean_square(0, j)
                project(PAIR_SB + 1, 0, ps[2][:, :], xn_hi, xn_lo)
                gate_argument(0, PAIR_SB)
                v_transposed(0)
                with pe.Fori(0, SB_HEADS - 1) as h:
                    head(h, True)
                head(SB_HEADS - 1, False)
                with pe.Fori(0, KT // 2) as i:
                    for j in range(2):
                        pe.wait_ge(x_ready, KT * (3 * DEPTH + 2) + 2 * i + j - 1)
                        for b in range(2):
                            unit_arrived(PAIR_EOUT + 2 * i + j, b)
                            for k in range(6):
                                if 6 * b + k < SB_HEADS:
                                    pe.wait_ge(gated_lo, CREDIT + 6 * b + k + 1)
                                last = three(ps[j][:, :], w_hi[b][:, k, :], w_lo[b][:, k, :], eo_hi[:, 6 * b + k, :],
                                             eo_lo[:, 6 * b + k, :], b == 0 and k == 0, b == 1 and k == 5)
                            last.then_inc(unit_used, 1)

            def gla():
                project(PAIR_R, 0, ps[0][:, :], xn_hi, xn_lo, norms=3 * DEPTH + 2)
                unit_arrived(PAIR_R, 1)
                pe.wait_ge(r_lo_done, 1)
                for h in range(GLA_HEADS):
                    last = three(ps[4 + h][:, :], w_hi[1][:, h, :], w_lo[1][:, h, :], r_hi[:, :], r_lo[:, :],
                                 True, True)
                last.then_inc(unit_used, 1)
                with pe.Fori(0, GLA_HEADS) as h:
                    pair = PAIR_GLA + 3 * h
                    project(pair, 0, ps[0][:, :], xn_hi, xn_lo)
                    project(pair, 1, ps[1][:, :], xn_hi, xn_lo)
                    pe.wait_ge(r_lo_done, 1)
                    pe.wait_ge(raw_done, SB_HEADS + 2 * h)
                    for j in range(2):
                        project(pair + 1, j, ps[2 + j][:, :], xn_hi, xn_lo)
                    pe.wait_ge(gq_done, 3 * h + 3)
                    for t in range(ST):
                        last = pe.transpose(ps[0][:, t * P:(t + 1) * P], gq[2][:, t * P:(t + 1) * P], ident[:, :])
                    last.then_inc(kdt_done, 1)
                    pe.wait_ge(gq_lo_done, 2 * h + 2)
                    for t in range(ST):
                        r = slice(t * P, (t + 1) * P)
                        last = three(ps[1][:, r], gq_hi[1][:, r], gq_lo[1][:, r], gq_hi[0][:, r], gq_lo[0][:, r],
                                     True, True)
                    last.then_inc(sc_mm, 1)
                    for j in range(2):
                        pe.wait_ge(gvf_done, 2 * h + j + 1)
                        for t in range(ST):
                            last = pe.transpose(ps[2 + j][:, t * P:(t + 1) * P], gvf[j][:, t * P:(t + 1) * P],
                                                ident[:, :])
                        last.then_inc(gvt_done, 1)
                    pe.wait_ge(kd_lo_done, h + 1)
                    pe.wait_ge(gv_lo_done, 2 * h + 2)
                    for c in range(NCH - 1):
                        r = slice(CH * (c % 2), CH * (c % 2) + CH)
                        last = three(kv_bank(c),
                                     kd_hi[r, c // 2, :], kd_lo[r, c // 2, :], gv_hi[r, c // 2, :], gv_lo[r, c // 2, :],
                                     True, True)
                    last.then_inc(kv_done, 1)
                    for j in range(2):
                        project(pair + 2, j, ps[j][:, :], xn_hi, xn_lo)
                    pe.wait_ge(score_lo_done, h + 1)
                    for d in range(2):
                        for t in range(ST):
                            three(ps[2 + d][:, t * P:(t + 1) * P], gv_hi[:, t, d * P:(d + 1) * P],
                                  gv_lo[:, t, d * P:(d + 1) * P], score_hi[:, t, :], score_lo[:, t, :],
                                  t == 0, False)
                    for c in range(1, NCH):
                        pe.wait_ge(state_lo_done, (NCH - 1) * h + c)
                        for d in range(2):
                            last = three(ps[2 + d][:, CH * c:CH * c + CH], state_hi[c][:, d * P:(d + 1) * P],
                                         state_lo[c][:, d * P:(d + 1) * P], gq_hi[0][:, CH * c:CH * c + CH],
                                         gq_lo[0][:, CH * c:CH * c + CH], False, c == NCH - 1)
                    last.then_inc(go_mm, 1)
                    pe.wait_ge(gz_done, 2 * h + 2)
                    pe.wait_ge(gsq_done, 2 * h + 2)
                    pe.matmul(ps[4][:, :], ones[:, :], gsq[0][:, :], start=True, stop=False)
                    pe.matmul(ps[4][:, :], ones[:, :], gsq[1][:, :], start=False, stop=True).then_inc(gms_done, 1)
                with pe.Fori(0, KT // 2) as i:
                    for j in range(2):
                        pe.wait_ge(x_ready, KT * (3 * DEPTH + 3) + 2 * i + j - 1)
                        project(PAIR_OOUT + i, j, ps[j][:, :], go_hi, go_lo,
                                arrived=lambda k: pe.wait_ge(gated_lo, CREDIT + SB_HEADS + k + 1))

            pe.wait_ge(consts_ready, 1)
            pe.wait_ge(small_in, 16 * SMALL)
            for c, w in ((0, 512), (512, REL - 512)):
                last = pe.matmul(ps[c // 512][0:N_MAPS, 0:w], relt[:, :], onehot[:, c:c + w], start=True, stop=True)
            last.then_inc(table_ready, 1)
            with pe.Fori(0, DEPTH) as l:
                norm(3 * l, 0)
                ffn_up(2 * l, l * PAIRS_LAYER + PAIR_FFN1, 3 * l)
                ffn_down(2 * l, l * PAIRS_LAYER + PAIR_DOWN1)
                norm(3 * l + 1, 0)
                fourier(l)
                branch_a(l)
                first_head(l)
                dilated(l)
                diff(l)
                merge(l)
                out_projection(l)
                norm(3 * l + 2, 7)
                ffn_up(2 * l + 1, l * PAIRS_LAYER + PAIR_FFN2, 3 * l + 2)
                ffn_down(2 * l + 1, l * PAIRS_LAYER + PAIR_DOWN2)
            norm(3 * DEPTH, 0)
            norm(3 * DEPTH + 1, 0)
            s5()
            stick_breaking()
            norm(3 * DEPTH + 2, 7)
            gla()

        @block.scalar
        def _(act):
            def split(pair, j):
                act.wait_ge(unit_loaded[j], 16 * (pair + 1))
                act.wait_ge(unit_used, 2 * pair + j + 1)
                act.activation(w_hi[j][:, :, :], w_raw[j][:, :].rearrange("p (k m) -> p k m", k=8), ACT.Copy)\
                   .then_inc(unit_hi, 1)

            def used(pair, j):
                act.wait_ge(unit_used, CREDIT + 2 * pair + j + 1)

            def norm(n, r, bank, final=False, next_pair=None, dft=False):
                act.preload_act_table_set(LN_EXP)
                with act.Fori(0, KT) as k:
                    act.wait_ge(x_ready, KT * n + k + 1)
                    act.activation(sq[:, k, :], x[:, k, :], ACT.Square).then_inc(sq_done, 1)
                if dft:
                    load_dft()
                if next_pair is not None:
                    split(next_pair, 1)
                act.wait_ge(ms_done, n + 1)
                act.activation(rlog[:, :], ps[bank][:, :], ACT.Ln, bias=eps[:, 0:1], scale=1.0 / D).then_inc(rlog_done, 1)
                act.wait_ge(rlog_done, n + 1)
                act.activation(rstd[:, :], rlog[:, :], ACT.Exp, scale=-0.5).then_inc(rstd_done, 1)
                if final:
                    return
                with act.Fori(0, KT) as k:
                    act.wait_ge(xf_done, KT * r + k + 1)
                    act.activation(xn_hi[:, k, :], xf[:, k, :], ACT.Copy).then_inc(xh_done, 1)

            def ffn_up(r, pair0):
                act.preload_act_table(ACT.Silu)
                with act.Fori(0, FT // 2) as i:
                    for j in range(2):
                        f = r * FT + 2 * i + j
                        pair = pair0 + 2 * i + j
                        used(pair, 0)
                        act.wait_ge(prod_done, f + 1)
                        act.activation(gated[j][:, :], ps[2 * j][:, :], ACT.Silu).then_inc(gate_done, 1)
                        split(pair + 1, 0)
                        split(pair + 1, 1)
                        act.wait_ge(prod_done, CREDIT + f + 1)
                        act.activation(h_hi[:, 2 * i + j, :], prod[j][:, :], ACT.Copy).then_inc(hid_hi, 1)

            def split_ahead(pair0, pairs, last=False):
                with act.Fori(1, pairs) as i:
                    split(pair0 + i, 0)
                    split(pair0 + i, 1)
                if not last:
                    split(pair0 + pairs, 0)

            def load_dft():
                for half in range(2):
                    w = 4 * S + P
                    act.dma_start(dft_raw[:, half * w:(half + 1) * w], a["dft"][:, half * w:(half + 1) * w])\
                       .then_inc(dft_in, 16)

            def fourier(l):
                act.wait_ge(dft_in, 32 * (l + 1))
                act.activation(dft_hi[:, :], dft_raw[:, :], ACT.Copy).then_inc(dft_hi_done, 1)
                with act.Fori(0, GROUPS // 2) as i:
                    g0 = l * GROUPS + 2 * i
                    pair = l * PAIRS_LAYER + PAIR_FOUR + i
                    for j in range(2):
                        used(pair, j)
                        act.activation(fa_hi[j][:, :], ps[j][:, :], ACT.Copy).then_inc(fa_hi_done, 1)
                        split(pair + 1, j)
                    for j in range(2):
                        act.wait_ge(fp_mm, g0 + j + 1)
                        for b in range(2):
                            act.activation(fp_hi[j][:, 2 * b:2 * b + 2, :],
                                           ps[2 + 2 * j + b][:, :].rearrange("p (t c) -> p t c", t=2), ACT.Copy)\
                               .then_inc(fp_hi_done, 1)
                    for j in range(2):
                        act.wait_ge(fy_mm, g0 + j + 1)
                        act.activation(ya_hi[:, 2 * i + j, :], ps[j][:, :], ACT.Copy).then_inc(fy_hi_done, 1)

            def branch_a(l):
                act.preload_act_table(ACT.Sigmoid)
                with act.Fori(0, KT // 2) as i:
                    for j in range(2):
                        c = 2 * i + j
                        pair = l * PAIRS_LAYER + PAIR_BR_A + c
                        used(pair, 0)
                        split(pair + 1, 0)
                        act.wait_ge(mga_done, l * KT + c + 1)
                        act.activation(sig[j][:, :], ps[2 * j][:, :], ACT.Sigmoid,
                                       bias=gate_bias[:, bass.ds(l * 3 * KT + c, 1)]).then_inc(siga_done, 1)
                        split(pair + 1, 1)

            def load_bias(m, n):
                act.dma_start(bias[:, m, 0:BW], a["toeplitz"](n)).then_inc(bias_in[m], 16)

            def queries_keys(pair):
                used(pair, 0)
                act.activation(q_hi[:, :], ps[0][:, :], ACT.Copy).then_inc(qkv_hi, 1)
                used(pair + 1, 0)
                act.activation(k_hi[:, :], ps[1][:, :], ACT.Copy).then_inc(qkv_hi, 1)

            def values_as_made(pair):
                used(pair + 1, 1)
                act.activation(vf[:, :], ps[2][:, :], ACT.Copy).then_inc(vf_done, 1)

            def values(q):
                act.wait_ge(vt_done, q + 1)
                act.activation(v_hi[:, :, :], ps[2][:, :].rearrange("p (t m) -> p t m", t=ST), ACT.Copy)\
                   .then_inc(qkv_hi, 1)

            def first_head(l):
                pair = l * PAIRS_LAYER + PAIR_HEADS
                act.wait_ge(table_out, 16)
                for m in range(2):
                    load_bias(m, m)
                split(pair + 1, 0)
                split(pair + 1, 1)
                split(pair + 2, 0)
                queries_keys(pair)
                values_as_made(pair)

            def double_head(q, stat, transposed, next_pair, next_map=None, last_head=None):
                if next_pair is not None:
                    split(next_pair, 1)
                for step in range(STEPS):
                    if next_pair is not None and step in (4, 6, 10):
                        split(next_pair + (2 if step == 10 else 1), int(step == 6))
                    if step < 8:
                        act.wait_ge(nmax_done, 8 * q + step + 1)
                        act.activation(prob[:, step, :], logit[step % 2][:, :], ACT.Exp,
                                       bias=nmax[:, stat, step:step + 1],
                                       accum_out=rsum[:, stat, step:step + 1]).then_inc(exp_done, 1)
                    if next_pair is not None:
                        if next_map is not None and step in (4, 8):
                            load_bias(step // 8, next_map + step // 8)
                        if step == 10:
                            act.wait_ge(s_done, 8 * q + 8)
                            queries_keys(next_pair)
                    if step == 1:
                        values(q)
                    if last_head and step in (1, 3):
                        last_head(step)
                    transposed(step)

            def dilated(l):
                act.preload_act_table_set(LN_EXP)
                with act.Fori(0, N_DIL) as g:
                    q = l * N_DH + g
                    tq = l * N_T + 8 * g

                    def transposed(step):
                        i = step - 3
                        if not 0 <= i < 8:
                            return
                        m, t = divmod(i, ST)
                        act.wait_ge(t_done, tq + i + 1)
                        act.activation(pt_hi[m][:, :, t * P:(t + 1) * P],
                                       ps[5 + i % 2][:, :].rearrange("p (b q) -> p b q", b=ST), ACT.Copy)\
                           .then_inc(pt_hi_done, 1)

                    double_head(q, g, transposed, l * PAIRS_LAYER + PAIR_HEADS + 2 * g + 2, 2 * g + 2)
                    values_as_made(l * PAIRS_LAYER + PAIR_HEADS + 2 * g + 2)
                    act.wait_ge(o_done, l * N_DIL + g + 1)
                    act.activation(of[0:HD, :], ps[7][0:HD, :], ACT.Copy).then_inc(og_done, 1)
                    act.activation(of[HD:P, :], ps[3][HD:P, :], ACT.Copy).then_inc(og_done, 1)
                    act.wait_ge(ot_done, l * N_DIL + g + 1)
                    act.activation(og[:, g, :, :].rearrange("p (m t) e -> p t m e", m=2),
                                   ps[7][:, :].rearrange("p (t m e) -> p t m e", t=ST, m=2), ACT.Copy)\
                       .then_inc(og_done, 1)
                act.wait_ge(mix_step, N_MIX * l + 3)
                act.activation(mixw[:, 1:4, :], mixw[:, 1:4, :], ACT.Exp).then_inc(mix_exp, 1)

            def diff(l):
                def finish(step, h):
                    dq = l * N_DIFF + h
                    if step == 1:
                        act.wait_ge(oms_done, dq + 1)
                        act.activation(olog[:, :], ps[5][:, :], ACT.Ln, bias=eps[:, 1:2], scale=1.0 / P)\
                           .then_inc(olog_done, 1)
                        act.wait_ge(olog_done, dq + 1)
                        act.activation(orstd[:, :], olog[:, :], ACT.Exp, scale=-0.5).then_inc(orstd_done, 1)
                    else:
                        act.wait_ge(onorm_done, dq + 1)
                        act.activation(yc_hi[:, h, :], onorm[:, :], ACT.Copy).then_inc(yc_hi_done, 1)

                def head(h, has_last, has_next):
                    q = l * N_DH + N_DIL + h
                    dq = l * N_DIFF + h
                    tq = l * N_T + 8 * N_DIL + 4 * h

                    def transposed(step):
                        t, odd = divmod(step - 3, 2)
                        if not odd and 0 <= t < ST:
                            act.wait_ge(amap_step, 3 * (4 * dq + t) + 1)
                            act.activation(amap0[:, :], prob[:, 2 * t, :], ACT.Copy, scale=rinv[:, t, 0:1])\
                               .then_inc(amap0_done, 1)
                        t, odd = divmod(step - 6, 2)
                        if not odd and 0 <= t < ST:
                            act.wait_ge(t_done, tq + t + 1)
                            act.activation(pt_hi[0][:, :, t * P:(t + 1) * P],
                                           ps[5 + t % 2][:, :].rearrange("p (b q) -> p b q", b=ST), ACT.Copy)\
                               .then_inc(pt_hi_done, 1)

                    pair = l * PAIRS_LAYER + PAIR_HEADS + 2 * N_DIL + 2 * h + 2
                    double_head(q, N_DIL, transposed, pair if has_next else None,
                                last_head=(lambda step: finish(step, h - 1)) if has_last else None)
                    if has_next:
                        values_as_made(pair)
                    act.wait_ge(ov_done, dq + 1)
                    act.activation(of[:, :], ps[7][:, :], ACT.Copy)
                    act.activation(osq[:, :], ps[7][:, :], ACT.Square).then_inc(osq_done, 1)

                for h in range(2, N_DIFF):
                    act.dma_start(bias[:, h, 0:BW], a["toeplitz"](2 * N_DIL + h)).then_inc(head_bias_in, 16)
                head(0, False, True)
                with act.Fori(1, N_DIFF - 1) as h:
                    head(h, True, True)
                head(N_DIFF - 1, True, False)
                for step in (1, 3):
                    finish(step, N_DIFF - 1)
                act.wait_ge(ybt_done, l + 1)
                act.activation(yb_hi[:, 0, :], ps[7][:, :], ACT.Copy).then_inc(yb_hi_done, 1)

            def merge(l):
                act.preload_act_table(ACT.Sigmoid)
                split(l * PAIRS_LAYER + PAIR_MERGE, 1)
                with act.Fori(0, KT // 2) as i:
                    for j in range(2):
                        c = 2 * i + j
                        pair = l * PAIRS_LAYER + PAIR_MERGE + 3 * i
                        u = 3 * j
                        used(pair + u // 2, u % 2)
                        split(pair + (u + 2) // 2, (u + 2) % 2)
                        act.wait_ge(merged, l * KT + c + 1)
                        act.activation(sigb[j][:, :], ps[4 * j][:, :], ACT.Sigmoid,
                                       bias=gate_bias[:, bass.ds(l * 3 * KT + KT + c, 1)]).then_inc(sigbc_done, 1)
                        used(pair + (u + 1) // 2, (u + 1) % 2)
                        split(pair + (u + 3) // 2, (u + 3) % 2)
                        act.activation(sigc[j][:, :], ps[4 * j + 1][:, :], ACT.Sigmoid,
                                       bias=gate_bias[:, bass.ds(l * 3 * KT + 2 * KT + c, 1)]).then_inc(sigbc_done, 1)
                        split(pair + (u + 4) // 2, (u + 4) % 2)
                        act.wait_ge(merged, CREDIT + l * KT + c + 1)
                        act.activation(m_hi[:, c, :], mg[:, c, :], ACT.Copy).then_inc(m_hi_done, 1)

            def s5():
                s5_setup()
                act.preload_act_table(ACT.Gelu_apprx_tanh)
                for c in range(UT):
                    used(PAIR_U + c // 2, c % 2)
                    act.activation(uf[:, c, :], ps[c][:, :], ACT.Copy)
                    act.activation(u_hi[:, c, :], ps[c][:, :], ACT.Copy).then_inc(u_hi_done, 1)
                    split(PAIR_U + c // 2 + 1, c % 2)
                with act.Fori(0, UT) as c:
                    for s in range(4):
                        act.wait_ge(bu_mm, 4 * c + s + 1)
                        if s >= 2:
                            act.wait_ge(scan_step, N_SCAN * c + 2 * (s - 1))
                        for b in range(2):
                            act.activation(bx[s % 2][:, b, :], ps[bu_banks[s][b]][:, :], ACT.Copy,
                                           scale=s5_coef[:, 0, bass.ds(4 * c + s, 1)]).then_inc(bx_done, 1)
                    for s in range(4):
                        act.wait_ge(scan_step, N_SCAN * (c + 1) - 2 * (3 - s))
                        act.activation(st_hi[s][:, 0, :], sc[s][:, 0, :], ACT.Copy).then_inc(st_hi_done, 1)
                        act.activation(st_hi[s][:, 1, :], sc[s][:, 1, :], ACT.Copy, scale=-1.0)\
                           .then_inc(st_hi_done, 1)
                    for j in range(2):
                        split(PAIR_S5 + c + 1, j)
                    act.wait_ge(yf_done, c + 2)
                    act.activation(ge[:, c, :], yf[0][:, :], ACT.Gelu_apprx_tanh).then_inc(ge_done, 1)
                    act.wait_ge(ge_done, c + 1)
                    act.activation(ge_hi[:, c, :], ge[:, c, :], ACT.Copy).then_inc(ge_hi_done, 1)
                act.preload_act_table(ACT.Silu)
                with act.Fori(0, UT // 2) as i:
                    for j in range(2):
                        used(PAIR_ZB + i, j)
                        act.activation(zb[:, 2 * i + j, :], ps[2 * j][:, :], ACT.Silu).then_inc(zb_done, 1)
                        split(PAIR_ZB + i + 1, j)
                for c in range(UT):
                    if c % 2 == 0:
                        used(PAIR_GLU, c // 2)
                        if c == 0:
                            split(PAIR_SB, 0)
                    if c >= 2:
                        act.wait_ge(ob_step, 2 * (c - 1))
                    act.activation(glu[c % 2][:, :], ps[4 + c][:, :], ACT.Sigmoid, bias=s5_cols[:, 1, c:c + 1])\
                       .then_inc(glu_done, 1)
                for c in range(UT):
                    act.wait_ge(ob_step, 2 * (c + 1))
                    act.activation(eo_hi[:, SB_HEADS + c, :], ob_f[c % 2][:, :], ACT.Copy).then_inc(ob_hi_done, 1)

            def stick_breaking():
                def query_key(h, pair, j):
                    used(pair, j)
                    act.activation(sbq[j][:, :], ps[j][:, :], ACT.Copy).then_inc(sbq_done, 1)
                    act.activation(sbs[j][:, :], ps[j][:, :], ACT.Square).then_inc(sbq_done, 1)

                def log_mean(h, j):
                    act.wait_ge(sbms_done, 2 * h + j + 1)
                    act.activation(sbl[j][:, :], ps[j][:, :], ACT.Ln, bias=eps[:, 0:1], scale=1.0 / P)\
                       .then_inc(sblog_done, 1)

                def root(h, j):
                    act.wait_ge(sblog_done, 2 * h + j + 1)
                    act.activation(sbs[j][:, :], sbl[j][:, :], ACT.Exp, scale=-0.5).then_inc(sbr_done, 1)

                def value(pair):
                    used(pair + 1, 0)
                    act.activation(svf[:, :], ps[2][:, :], ACT.Copy).then_inc(svf_done, 1)
                    split(pair + 2, 0)

                def finish(h, pair):
                    used(pair + 1, 1)
                    act.activation(ez[:, h, :], ps[0][:, :], ACT.Copy).then_inc(sz_done, 1)
                    for j in range(2):
                        act.wait_ge(sbn_done, 2 * h + j + 1)
                        act.activation(sbn_hi[j][:, :], sbq[j][:, :], ACT.Copy).then_inc(sb_hi_done, 1)
                    act.wait_ge(svt_done, h + 1)
                    act.activation(sv_hi[:, :, :], ps[2][:, :].rearrange("p (t m) -> p t m", t=ST), ACT.Copy)\
                       .then_inc(sb_hi_done, 1)

                def log_rest(h, n):
                    b = ST - 1 - n
                    w = S - b * P
                    k = ST * h + n
                    act.wait_ge(z_done, k + 1)
                    act.activation(za[n % 2][:, 0:w], ps[5 + n % 2][:, 0:w], ACT.Abs, scale=P ** -0.5)\
                       .then_inc(za_done, 1)
                    act.wait_ge(za_done, k + 1)
                    act.activation(ze[n % 2][:, 0:w], za[n % 2][:, 0:w], ACT.Exp, scale=-1.0).then_inc(ze_done, 1)
                    act.wait_ge(ze_done, k + 1)
                    act.activation(za[n % 2][:, 0:w], ze[n % 2][:, 0:w], ACT.Ln, bias=ones[:, 0:1])\
                       .then_inc(zl_done, 1)
                    act.wait_ge(lom_done, k + 1)
                    act.activation(lom_hi[:, b, b * P:S], lom[n % 2][:, 0:w], ACT.Copy).then_inc(lom_hi_done, 1)

                def weights(h, n):
                    b = ST - 1 - n
                    w = S - b * P
                    k = ST * h + n
                    act.wait_ge(wlog_done, k + 1)
                    act.activation(ww[n % 2][:, 0:w], zm[n % 2][:, 0:w], ACT.Exp).then_inc(w_exp_done, 1)
                    act.wait_ge(w_masked, k + 1)
                    act.activation(w_hi_t[:, b, b * P:S], ww[n % 2][:, 0:w], ACT.Copy).then_inc(wt_hi_done, 1)

                def head(h, has_next):
                    pair = PAIR_SB + 2 * h + 2
                    if has_next:
                        split(pair, 1)
                    log_rest(h, 0)
                    log_rest(h, 1)
                    if has_next:
                        split(pair + 1, 0)
                        query_key(h + 1, pair, 0)
                    weights(h, 0)
                    log_rest(h, 2)
                    if has_next:
                        split(pair + 1, 1)
                        query_key(h + 1, pair, 1)
                    weights(h, 1)
                    log_rest(h, 3)
                    if has_next:
                        log_mean(h + 1, 0)
                        value(pair)
                    weights(h, 2)
                    if has_next:
                        log_mean(h + 1, 1)
                        for j in range(2):
                            root(h + 1, j)
                    weights(h, 3)
                    if has_next:
                        finish(h + 1, pair)

                act.preload_act_table_set(LN_EXP)
                split(PAIR_SB, 1)
                for j in range(2):
                    query_key(0, PAIR_SB, j)
                    split(PAIR_SB + 1, j)
                log_mean(0, 0)
                value(PAIR_SB)
                log_mean(0, 1)
                for j in range(2):
                    root(0, j)
                finish(0, PAIR_SB)
                with act.Fori(0, SB_HEADS - 1) as h:
                    head(h, True)
                head(SB_HEADS - 1, False)
                split(PAIR_EOUT, 1)
                gate_outputs(0, eo_hi, ez)
                split_ahead(PAIR_EOUT, KT)

            def gate_outputs(n0, out_hi, z):
                act.preload_act_table(ACT.Silu)
                with act.Fori(0, GATED // 2) as i:
                    for j in range(3):
                        n = n0 + 2 * i + j
                        if j < 2:
                            act.wait_ge(raw_done, n0 + GATED)
                            act.wait_ge(gated_f, n + 1)
                            act.activation(gate[j][:, :], z[:, 2 * i + j, :], ACT.Silu).then_inc(gate_made, 1)
                        if j:
                            act.wait_ge(gated_f, CREDIT + n)
                            act.activation(out_hi[:, 2 * i + j - 1, :], gated_o[j - 1][:, :], ACT.Copy)\
                               .then_inc(gated_hi, 1)

            def gla():
                act.preload_act_table_set(LN_EXP)
                used(PAIR_R, 0)
                act.activation(r_hi[:, :], ps[0][:, :], ACT.Copy).then_inc(r_hi_done, 1)
                for j in range(2):
                    split(PAIR_GLA, j)
                for h in range(GLA_HEADS):
                    act.wait_ge(gx_step, h + 1)
                    act.activation(ga[h % 2][:, :], gx[h % 2][:, :], ACT.Abs).then_inc(ga_step, 1)
                    act.wait_ge(ga_step, 3 * h + 1)
                    act.activation(ga[h % 2][:, :], ga[h % 2][:, :], ACT.Exp, scale=-1.0).then_inc(ga_step, 1)
                    act.wait_ge(ga_step, 3 * h + 2)
                    if h >= 2:
                        act.wait_ge(gcum_done, h - 1)
                    act.activation(gl[h % 2][:, :], ga[h % 2][:, :], ACT.Ln, bias=ones[:, 0:1]).then_inc(ga_step, 1)
                with act.Fori(0, GLA_HEADS) as h:
                    pair = PAIR_GLA + 3 * h
                    for j in range(2):
                        split(pair + 1, j)
                    act.wait_ge(gd_done, h + 1)
                    for n, (src, scale) in enumerate(((gcum[:, h, :], 1 / TAU), (gcum[:, h, :], -1 / TAU),
                                                      (gdiff[:, :], 1 / TAU))):
                        act.activation(gexp[n][:, :], src, ACT.Exp, scale=scale).then_inc(gexp_done, 1)
                    act.activation(gend[:, :], gcum[:, h, CH - 1::CH], ACT.Exp, scale=1 / TAU).then_inc(gexp_done, 1)
                    for j in range(2):
                        act.wait_ge(gq_done, 3 * h + j + 1)
                        act.activation(gq_hi[j][:, :], gq[j][:, :], ACT.Copy).then_inc(gq_hi_done, 1)
                    for j in range(2):
                        used(pair + 1, j)
                        act.activation(gvf[j][:, :], ps[2 + j][:, :], ACT.Copy).then_inc(gvf_done, 1)
                        split(pair + 2, j)
                    act.wait_ge(kdt_done, h + 1)
                    act.activation(kd_hi[:, :, :], ps[0][:, :].rearrange("p (t m) -> p t m", t=ST), ACT.Copy)\
                       .then_inc(kd_hi_done, 1)
                    act.wait_ge(score_done, h + 2)
                    act.activation(score_hi[:, :, :], score[:, :, :], ACT.Copy).then_inc(score_hi_done, 1)
                    for j in range(2):
                        act.wait_ge(gvt_done, 2 * h + j + 1)
                        act.activation(gv_hi[:, :, j * P:(j + 1) * P], ps[2 + j][:, :].rearrange("p (t m) -> p t m", t=ST),
                                       ACT.Copy).then_inc(gv_hi_done, 1)
                    for c in range(1, NCH):
                        act.wait_ge(state_done, (NCH - 1) * h + c)
                        act.activation(state_hi[c][:, :], state[c % 2][:, :], ACT.Copy).then_inc(state_hi_done, 1)
                    act.wait_ge(go_mm, h + 1)
                    for d in range(2):
                        act.activation(gsq[d][:, :], ps[2 + d][:, :], ACT.Square).then_inc(gsq_done, 1)
                    for d in range(2):
                        used(pair + 2, d)
                        act.activation(gz[:, 2 * h + d, :], ps[d][:, :], ACT.Copy).then_inc(gz_done, 1)
                        split(pair + 3, d)
                    act.wait_ge(gms_done, h + 1)
                    act.activation(grs[0][:, :], ps[4][:, :], ACT.Ln, bias=eps[:, 0:1], scale=0.5 / P).then_inc(grs_step, 1)
                    act.wait_ge(grs_step, 2 * h + 1)
                    act.activation(grs[1][:, :], grs[0][:, :], ACT.Exp, scale=-0.5).then_inc(grs_step, 1)
                gate_outputs(SB_HEADS, go_hi, gz)
                split_ahead(PAIR_OOUT, KT // 2, last=True)

            def s5_setup():
                lre, lim, ldt = (s5_in[:, n, :] for n in range(3))
                act.activation(s5_t[:, 0, :], ldt, ACT.Exp).then_inc(s5_tables, 1)
                act.wait_ge(s5_step, 2)
                act.activation(s5_t[:, 3, :], s5_t[:, 1, :], ACT.Exp).then_inc(s5_tables, 1)
                act.wait_ge(s5_step, 12)
                act.activation(s5_t[:, 5, :], s5_t[:, 5, :], ACT.Sin).then_inc(s5_tables, 1)
                act.activation(s5_t[:, 6, :], s5_t[:, 6, :], ACT.Sin).then_inc(s5_tables, 1)

            act.wait_ge(consts_ready, 1)
            act.wait_ge(small_in, 16 * SMALL)
            act.activation(after_r[:, :], after[:, 0:P], ACT.Copy).then_inc(masks_r, 1)
            act.activation(ones_r[:, :], ones[:, :], ACT.Copy).then_inc(masks_r, 1)
            act.wait_ge(setup_step, 2)
            act.activation(lame[:, :], lams[:, :], ACT.Exp).then_inc(masks_r, 1)
            act.wait_ge(table_copied, 2)
            act.dma_start(a["table"], table[:, :].unsqueeze(1).to_broadcast([N_MAPS, P, REL])).then_inc(table_out, 16)
            split(0, 0)
            with act.Fori(0, DEPTH) as l:
                norm(3 * l, 3 * l, 0, next_pair=l * PAIRS_LAYER + PAIR_FFN1)
                ffn_up(2 * l, l * PAIRS_LAYER + PAIR_FFN1)
                split_ahead(l * PAIRS_LAYER + PAIR_DOWN1, FT // 2)
                norm(3 * l + 1, 3 * l + 1, 0, next_pair=l * PAIRS_LAYER + PAIR_FOUR, dft=True)
                fourier(l)
                branch_a(l)
                first_head(l)
                dilated(l)
                diff(l)
                merge(l)
                split_ahead(l * PAIRS_LAYER + PAIR_OUT, KT // 2)
                norm(3 * l + 2, 3 * l + 2, 7, next_pair=l * PAIRS_LAYER + PAIR_FFN2)
                ffn_up(2 * l + 1, l * PAIRS_LAYER + PAIR_FFN2)
                split_ahead(l * PAIRS_LAYER + PAIR_DOWN2, FT // 2)
            norm(3 * DEPTH, 0, 0, final=True)
            norm(3 * DEPTH + 1, 3 * DEPTH, 0, next_pair=PAIR_U)
            s5()
            stick_breaking()
            norm(3 * DEPTH + 2, 3 * DEPTH + 1, 7, next_pair=PAIR_R)
            gla()

        @block.vector
        def _(dve):
            def used(pair, j):
                dve.wait_ge(unit_used, CREDIT + 2 * pair + j + 1)

            def low(out, full, hi):
                return dve.tensor_tensor(out, full, hi.bitcast(F32), ALU.subtract)

            def norm(n, r, final=False):
                dve.wait_ge(rstd_done, n + 1)
                for k in range(KT):
                    g = gains[:, bass.ds(n * KT + k, 1)]
                    if final:
                        dve.scalar_tensor_tensor(x[:, k, :], x[:, k, :], g, rstd[:, :], ALU.mult, ALU.mult)\
                           .then_inc(x_ready, 1)
                        continue
                    dve.scalar_tensor_tensor(xf[:, k, :], x[:, k, :], g, rstd[:, :], ALU.mult, ALU.mult)\
                       .then_inc(xf_done, 1)
                    if k:
                        dve.wait_ge(xh_done, KT * r + k)
                        low(xn_lo[:, k - 1, :], xf[:, k - 1, :], xn_hi[:, k - 1, :]).then_inc(xn_done, 1)
                if not final:
                    dve.wait_ge(xh_done, KT * r + KT)
                    low(xn_lo[:, KT - 1, :], xf[:, KT - 1, :], xn_hi[:, KT - 1, :]).then_inc(xn_done, 1)

            def ffn_up(r, pair0):
                with dve.Fori(0, FT // 2) as i:
                    for j in range(2):
                        f = r * FT + 2 * i + j
                        dve.wait_ge(gate_done, f + 1)
                        used(pair0 + 2 * i + j, 1)
                        dve.wait_ge(hid_lo, f + 1)
                        dve.tensor_tensor(prod[j][:, :], gated[j][:, :], ps[2 * j + 1][:, :], ALU.mult)\
                           .then_inc(prod_done, 1)
                        dve.wait_ge(hid_hi, f + 1)
                        low(h_lo[:, 2 * i + j, :], prod[j][:, :], h_hi[:, 2 * i + j, :]).then_inc(hid_lo, 1)

            def ffn_down(pair0):
                used(pair0 + FT // 2 - 1, 1)
                for m in range(KT):
                    dve.scalar_tensor_tensor(x[:, m, :], ps[m][:, :], 0.5, x[:, m, :], ALU.mult, ALU.add)\
                       .then_inc(x_ready, 1)

            def fourier(l):
                dve.wait_ge(dft_hi_done, l + 1)
                low(dft_lo[:, :], dft_raw[:, :], dft_hi[:, :]).then_inc(dft_lo_done, 1)
                with dve.Fori(0, GROUPS // 2) as i:
                    g0 = l * GROUPS + 2 * i
                    for j in range(2):
                        dve.wait_ge(fa_hi_done, g0 + j + 1)
                        low(fa_lo[j][:, :], ps[j][:, :], fa_hi[j][:, :]).then_inc(fa_lo_done, 1)
                    for j in range(2):
                        for b in range(2):
                            dve.wait_ge(fp_hi_done, 2 * (g0 + j) + b + 1)
                            low(fp_lo[j][:, 2 * b:2 * b + 2, :], ps[2 + 2 * j + b][:, :].rearrange("p (t c) -> p t c", t=2),
                                fp_hi[j][:, 2 * b:2 * b + 2, :]).then_inc(fp_lo_done, 1)
                    for j in range(2):
                        dve.wait_ge(fy_hi_done, g0 + j + 1)
                        low(ya_lo[:, 2 * i + j, :], ps[j][:, :], ya_hi[:, 2 * i + j, :]).then_inc(fy_lo_done, 1)

            def branch_a(l):
                with dve.Fori(0, KT // 2) as i:
                    for j in range(2):
                        c = 2 * i + j
                        dve.wait_ge(siga_done, l * KT + c + 1)
                        used(l * PAIRS_LAYER + PAIR_BR_A + c, 1)
                        dve.tensor_tensor(mg[:, c, :], sig[j][:, :], ps[2 * j + 1][:, :], ALU.mult).then_inc(mga_done, 1)

            def queries_keys(q):
                for n, (hi, lo) in enumerate(((q_hi, q_lo), (k_hi, k_lo))):
                    dve.wait_ge(qkv_hi, 3 * q + n + 1)
                    low(lo[:, :], ps[n][:, :], hi[:, :]).then_inc(qkv_lo, 1)

            def values(q):
                dve.wait_ge(qkv_hi, 3 * q + 3)
                low(v_lo[:, :, :], ps[2][:, :].rearrange("p (t m) -> p t m", t=ST), v_hi[:, :, :]).then_inc(qkv_lo, 1)

            def first_head(l):
                queries_keys(l * N_DH)

            def double_head(q, stat, tile_of, bias_of, bias_there, transposed, has_next, last_head=None):
                for step in range(STEPS):
                    if last_head and step in (2, 4):
                        last_head(step)
                    transposed(step)
                    if step < 8:
                        m, t = tile_of(step)
                        dve.wait_ge(s_done, 8 * q + step + 1)
                        dve.wait_ge(exp_done, 8 * q + step + 1)
                        if t == 0:
                            bias_there(m)
                        o = P * (ST - 1 - t)
                        dve.scalar_tensor_tensor(logit[step % 2][:, :], ps[3 + step % 2][:, :], HD ** -0.5,
                                                 bias_of(m, o), ALU.mult, ALU.add).then_inc(logit_done, 1)
                        dve.wait_ge(logit_done, CREDIT + 8 * q + step + 1)
                        dve.tensor_reduce(nmax[:, stat, step:step + 1], logit[step % 2][:, :], AX.X, ALU.max,
                                          negate=True).then_inc(nmax_done, 1)
                    if step == 1:
                        values(q)
                    if step == 10 and has_next:
                        queries_keys(q + 1)

            def transposed_low(n, m, t, bank):
                dve.wait_ge(pt_hi_done, n + 1)
                low(pt_lo[m][:, :, t * P:(t + 1) * P], ps[bank][:, :].rearrange("p (b q) -> p b q", b=ST),
                    pt_hi[m][:, :, t * P:(t + 1) * P]).then_inc(pt_lo_done, 1)

            def dilated(l):
                with dve.Fori(0, N_DIL) as g:
                    tq = l * N_T + 8 * g

                    def transposed(step):
                        i = step - 4
                        if 0 <= i < 8:
                            transposed_low(tq + i, i // ST, i % ST, 5 + i % 2)

                    q = l * N_DH + g
                    double_head(q, g, lambda s: divmod(s, ST), lambda m, o: bias[:, m, o:o + S],
                                lambda m: dve.wait_ge(bias_in[m], l * BIAS_LOADS + 16 * (g + 1)), transposed, True)
                step = [0]

                def link(ins):
                    step[0] += 1
                    ins.then_inc(mix_step, 1)
                    if step[0] < N_MIX:
                        dve.wait_ge(mix_step, N_MIX * l + step[0])

                def wide(w):
                    return w.unsqueeze(2).to_broadcast([P, 8, HD])

                dve.wait_ge(og_done, 3 * (l + 1) * N_DIL)
                link(dve.tensor_tensor(mixw[:, 0, :], nmax[:, 0, :], nmax[:, 1, :], ALU.min))
                link(dve.tensor_tensor(mixw[:, 0, :], mixw[:, 0, :], nmax[:, 2, :], ALU.min))
                link(dve.tensor_tensor(mixw[:, 1:4, :], mixw[:, 0:1, :].to_broadcast([P, N_DIL, 8]), nmax[:, 0:N_DIL, :],
                                       ALU.subtract))
                dve.wait_ge(mix_exp, l + 1)
                link(dve.tensor_tensor(mixr[:, :, :], mixw[:, 1:4, :], rsum[:, 0:N_DIL, :], ALU.mult))
                link(dve.tensor_tensor(mixw[:, 4, :], mixr[:, 0, :], mixr[:, 1, :], ALU.add))
                link(dve.tensor_tensor(mixw[:, 4, :], mixw[:, 4, :], mixr[:, 2, :], ALU.add))
                link(dve.reciprocal(mixw[:, 0, :], mixw[:, 4, :]))
                link(dve.tensor_tensor(mixr[:, :, :], mixw[:, 1:4, :], mixw[:, 0:1, :].to_broadcast([P, N_DIL, 8]),
                                       ALU.mult))
                out = ybf[:, :, :].rearrange("p (t m) e -> p m t e", m=2)
                tmp = ybt[:, :, :].rearrange("p (m t) e -> p m t e", m=2)

                def part(g):
                    return (og[:, g, :, :].rearrange("p (m t) e -> p m t e", m=2),
                            wide(mixr[:, g, :]).rearrange("p (m t) e -> p m t e", m=2))

                link(dve.tensor_tensor(out, *part(0), ALU.mult))
                link(dve.tensor_tensor(tmp, *part(1), ALU.mult))
                link(dve.tensor_tensor(out, out, tmp, ALU.add))
                link(dve.tensor_tensor(tmp, *part(2), ALU.mult))
                link(dve.tensor_tensor(out, out, tmp, ALU.add))

            def diff(l):
                def finish(step, h):
                    dq = l * N_DIFF + h
                    if step == 2:
                        dve.wait_ge(orstd_done, dq + 1)
                        dve.scalar_tensor_tensor(onorm[:, :], of[:, :], sub_gain[:, bass.ds(l, 1)], orstd[:, :],
                                                 ALU.mult, ALU.mult).then_inc(onorm_done, 1)
                    else:
                        dve.wait_ge(yc_hi_done, dq + 1)
                        low(yc_lo[:, h, :], onorm[:, :], yc_hi[:, h, :]).then_inc(yc_lo_done, 1)

                def head(h, has_last, has_next):
                    q = l * N_DH + N_DIL + h
                    dq = l * N_DIFF + h
                    tq = l * N_T + 8 * N_DIL + 4 * h

                    def transposed(step):
                        t, odd = divmod(step - 7, 2)
                        if not odd and 0 <= t < ST:
                            transposed_low(tq + t, 0, t, 5 + t % 2)
                        t, odd = divmod(step - 3, 2)
                        if not odd and 0 <= t < ST:
                            n = 3 * (4 * dq + t)
                            dve.wait_ge(exp_done, CREDIT + 8 * q + 2 * t + 2)
                            if t:
                                dve.wait_ge(amap_step, n)
                            dve.reciprocal(rinv[:, t, :], rsum[:, N_DIL, 2 * t:2 * t + 2]).then_inc(amap_step, 1)
                            dve.wait_ge(amap_step, n + 1)
                            dve.tensor_scalar(rinv[:, t, 1:2], rinv[:, t, 1:2], lam_neg[:, bass.ds(l, 1)], None,
                                              ALU.mult).then_inc(amap_step, 1)
                        t, odd = divmod(step - 4, 2)
                        if not odd and 0 <= t < ST:
                            n = 3 * (4 * dq + t)
                            dve.wait_ge(amap_step, n + 2)
                            dve.wait_ge(amap0_done, 4 * dq + t + 1)
                            dve.wait_ge(t_done, tq + t - 1)
                            dve.scalar_tensor_tensor(amap[t % 2][:, :], prob[:, 2 * t + 1, :], rinv[:, t, 1:2],
                                                     amap0[:, :], ALU.mult, ALU.add).then_inc(amap_step, 1)

                    if has_last:
                        dve.wait_ge(head_bias_in, 16 * (N_DIFF - 2) * (l + 1))
                    double_head(q, N_DIL, lambda s: (s % 2, s // 2),
                                lambda m, o: bias[:, bass.ds(h, 1), o:o + S].rearrange("p a s -> p (a s)"),
                                lambda m: dve.wait_ge(bias_in[m], (l + 1) * BIAS_LOADS), transposed, has_next,
                                (lambda step: finish(step, h - 1)) if has_last else None)

                head(0, False, True)
                with dve.Fori(1, N_DIFF - 1) as h:
                    head(h, True, True)
                head(N_DIFF - 1, True, False)
                for step in (2, 4):
                    finish(step, N_DIFF - 1)
                dve.wait_ge(yb_hi_done, l + 1)
                low(yb_lo[:, 0, :], ps[7][:, :], yb_hi[:, 0, :]).then_inc(yb_lo_done, 1)

            def merge(l):
                with dve.Fori(0, KT // 2) as i:
                    for j in range(2):
                        c = 2 * i + j
                        n = l * KT + c
                        u = 3 * j + 2
                        used(l * PAIRS_LAYER + PAIR_MERGE + 3 * i + u // 2, u % 2)
                        dve.wait_ge(sigbc_done, 2 * (n + 1))
                        dve.tensor_tensor(tmpb[j][:, :], sigb[j][:, :], ps[4 * j + 2][:, :], ALU.mult)\
                           .then_inc(merge_step, 1)
                        dve.tensor_tensor(tmpc[j][:, :], sigc[j][:, :], ps[4 * j + 3][:, :], ALU.mult)\
                           .then_inc(merge_step, 1)
                        dve.wait_ge(merge_step, 3 * n + 1)
                        dve.tensor_tensor(mg[:, c, :], mg[:, c, :], tmpb[j][:, :], ALU.add).then_inc(merge_step, 1)
                        dve.wait_ge(merge_step, 3 * n + 3)
                        dve.tensor_tensor(mg[:, c, :], mg[:, c, :], tmpc[j][:, :], ALU.add).then_inc(merged, 1)
                        dve.wait_ge(m_hi_done, n + 1)
                        low(m_lo[:, c, :], mg[:, c, :], m_hi[:, c, :]).then_inc(m_lo_done, 1)

            def out_projection(l):
                with dve.Fori(0, KT // 2) as i:
                    for j in range(2):
                        used(l * PAIRS_LAYER + PAIR_OUT + i, j)
                        dve.tensor_tensor(x[:, 2 * i + j, :], x[:, 2 * i + j, :], ps[j][:, :], ALU.add)\
                           .then_inc(x_ready, 1)

            def s5_setup():
                count = [0]

                def link(ins):
                    count[0] += 1
                    ins.then_inc(s5_step, 1)
                    dve.wait_ge(s5_step, count[0])

                def tt(out, x0, x1, op):
                    link(dve.tensor_tensor(out, x0, x1, op))

                def stt(out, x0, c, x1, op0=ALU.mult, op1=ALU.add):
                    link(dve.scalar_tensor_tensor(out, x0, c, x1, op0, op1))

                def ts(out, x0, c0, c1, op0, op1):
                    link(dve.tensor_scalar(out, x0, c0, c1, op0, op1))

                t = [s5_t[:, n, :] for n in range(12)]
                lre, lim = s5_in[:, 0, :], s5_in[:, 1, :]
                dve.wait_ge(s5_tables, 1)
                tt(t[1], lre, t[0], ALU.mult)
                tt(t[2], lim, t[0], ALU.mult)
                big = 1.5 * 2.0 ** 23
                ts(t[4], t[2], 1 / (2 * math.pi), big, ALU.mult, ALU.add)
                ts(t[4], t[4], -big, None, ALU.add, ALU.bypass)
                c1, c2 = 6.28125, 0.0019350051879882812
                stt(t[5], t[4], -c1, t[2])
                stt(t[5], t[4], -c2, t[5])
                stt(t[5], t[4], -(2 * math.pi - c1 - c2), t[5])
                limit = 3.1415925
                ts(t[6], t[5], math.pi / 2, None, ALU.add, ALU.bypass)
                ts(t[7], t[6], math.pi, -2 * math.pi, ALU.is_gt, ALU.mult)
                tt(t[6], t[6], t[7], ALU.add)
                ts(t[6], t[6], limit, -limit, ALU.min, ALU.max)
                ts(t[5], t[5], limit, -limit, ALU.min, ALU.max)
                assert count[0] == 12, count
                dve.wait_ge(s5_tables, 4)
                re, im, neg = (s5_pow[:, n, :, :] for n in range(3))
                tt(re[:, 0, :], t[3], t[6], ALU.mult)
                tt(im[:, 0, :], t[3], t[5], ALU.mult)
                ts(t[4], re[:, 0, :], -1.0, None, ALU.add, ALU.bypass)
                tt(t[7], lre, lre, ALU.mult)
                tt(t[8], lim, lim, ALU.mult)
                tt(t[7], t[7], t[8], ALU.add)
                link(dve.reciprocal(t[7], t[7]))
                tt(t[8], t[4], lre, ALU.mult)
                tt(t[9], im[:, 0, :], lim, ALU.mult)
                tt(t[8], t[8], t[9], ALU.add)
                tt(s5_coef[:, 0, :], t[8], t[7], ALU.mult)
                tt(t[9], im[:, 0, :], lre, ALU.mult)
                tt(t[10], t[4], lim, ALU.mult)
                tt(t[9], t[9], t[10], ALU.subtract)
                tt(s5_coef[:, 1, :], t[9], t[7], ALU.mult)
                ts(s5_coef[:, 2, :], s5_coef[:, 1, :], -1.0, None, ALU.mult, ALU.bypass)
                for n in range(LEVELS):
                    ts(neg[:, n, :], im[:, n, :], -1.0, None, ALU.mult, ALU.bypass)
                    if n + 1 < LEVELS:
                        tt(t[8], re[:, n, :], re[:, n, :], ALU.mult)
                        tt(t[9], im[:, n, :], im[:, n, :], ALU.mult)
                        tt(re[:, n + 1, :], t[8], t[9], ALU.subtract)
                        stt(im[:, n + 1, :], re[:, n, :], 2.0, im[:, n, :], ALU.mult, ALU.mult)

            def s5():
                s5_setup()
                for c in range(UT):
                    dve.wait_ge(u_hi_done, c + 1)
                    low(u_lo[:, c, :], ps[c][:, :], u_hi[:, c, :]).then_inc(u_lo_done, 1)
                with dve.Fori(0, UT) as c:
                    base = N_SCAN * c
                    dve.tensor_copy(s5_now[:, :, :, :], s5_pow[:, :, :, bass.ds(4 * c, 4)]).then_inc(s5_now_set, 1)
                    for s in range(4):
                        coef = [s5_coef[:, n, bass.ds(4 * c + s, 1)] for n in range(3)]
                        dve.wait_ge(bx_done, 2 * (4 * c + s) + 2)
                        re, im = (ps[b][:, :] for b in bu_banks[s])
                        dve.scalar_tensor_tensor(sc[s][:, 0, :], im, coef[2], bx[s % 2][:, 0, :], ALU.mult, ALU.add)\
                           .then_inc(scan_step, 1)
                        dve.scalar_tensor_tensor(sc[s][:, 1, :], re, coef[1], bx[s % 2][:, 1, :], ALU.mult, ALU.add)\
                           .then_inc(scan_step, 1)
                    steps = [(n, 2 * (1 << n) - 1) for n in range(LEVELS)]
                    steps += [(n, 3 * (1 << n) - 1) for n in reversed(range(LEVELS - 1))]
                    dve.wait_ge(s5_now_set, c + 1)
                    for m, (n, first) in enumerate(steps):
                        to, fro = slice(first, S, 2 << n), slice(first - (1 << n), S - (1 << n), 2 << n)
                        start = base + 8 + 12 * m
                        p_re, p_im, p_neg = ([s5_now[:, part, n, s:s + 1] for s in range(4)] for part in range(3))
                        for s in range(4):
                            dve.wait_ge(scan_step, start - 6 + 2 * s if m else base + 2 * (s + 1))
                            dve.scalar_tensor_tensor(sc[s][:, :, to], sc[s][:, :, fro], p_re[s], sc[s][:, :, to],
                                                     ALU.mult, ALU.add).then_inc(scan_step, 1)
                        for s in range(4):
                            dve.wait_ge(scan_step, start + s + 1)
                            dve.scalar_tensor_tensor(sc[s][:, 0, to], sc[s][:, 1, fro], p_neg[s], sc[s][:, 0, to],
                                                     ALU.mult, ALU.add).then_inc(scan_step, 1)
                            dve.scalar_tensor_tensor(sc[s][:, 1, to], sc[s][:, 0, fro], p_im[s], sc[s][:, 1, to],
                                                     ALU.mult, ALU.add).then_inc(scan_step, 1)
                    for s in range(4):
                        dve.wait_ge(st_hi_done, 2 * (4 * c + s) + 2)
                        low(st_lo[s][:, 0, :], sc[s][:, 0, :], st_hi[s][:, 0, :])
                        dve.scalar_tensor_tensor(st_lo[s][:, 1, :], sc[s][:, 1, :], -1.0,
                                                 st_hi[s][:, 1, :].bitcast(F32), ALU.mult, ALU.subtract)\
                           .then_inc(st_lo_done, 1)
                    dve.wait_ge(unit_used, CREDIT + 2 * (PAIR_S5 + c) + 2)
                    dve.scalar_tensor_tensor(yf[0][:, :], uf[:, c, :], s5_cols[:, 0, bass.ds(c, 1)], ps[4][:, :],
                                             ALU.mult, ALU.add).then_inc(yf_done, 1)
                    dve.wait_ge(ge_hi_done, c + 1)
                    low(ge_lo[:, c, :], ge[:, c, :], ge_hi[:, c, :]).then_inc(ge_lo_done, 1)
                for c in range(UT):
                    dve.wait_ge(glu_done, c + 1)
                    if c >= 2:
                        dve.wait_ge(ob_lo_done, c - 1)
                    if c == 0:
                        dve.wait_ge(zb_done, CREDIT + UT)
                    dve.tensor_tensor(ob_f[c % 2][:, :], glu[c % 2][:, :], ge[:, c, :], ALU.mult).then_inc(ob_step, 1)
                    dve.wait_ge(ob_step, 2 * c + 1)
                    dve.tensor_tensor(ob_f[c % 2][:, :], ob_f[c % 2][:, :], zb[:, c, :], ALU.mult).then_inc(ob_step, 1)
                    if c >= 1:
                        dve.wait_ge(ob_hi_done, c)
                        low(eo_lo[:, SB_HEADS + c - 1, :], ob_f[(c - 1) % 2][:, :], eo_hi[:, SB_HEADS + c - 1, :])\
                            .then_inc(ob_lo_done, 1)
                dve.wait_ge(ob_hi_done, UT)
                low(eo_lo[:, SB_HEADS + UT - 1, :], ob_f[(UT - 1) % 2][:, :], eo_hi[:, SB_HEADS + UT - 1, :])\
                    .then_inc(ob_lo_done, 1)

            def stick_breaking():
                scale = P ** -0.5

                def normed(h):
                    for j in range(2):
                        dve.wait_ge(sbr_done, 2 * h + j + 1)
                        dve.scalar_tensor_tensor(sbq[j][:, :], sbq[j][:, :], tail_cols[:, j:j + 1], sbs[j][:, :],
                                                 ALU.mult, ALU.mult).then_inc(sbn_done, 1)

                def normed_low(h):
                    for j in range(2):
                        dve.wait_ge(sb_hi_done, 3 * h + 1 + j)
                        low(sbn_lo[j][:, :], sbq[j][:, :], sbn_hi[j][:, :]).then_inc(sb_lo_done, 1)

                def value_low(h):
                    dve.wait_ge(sb_hi_done, 3 * h + 3)
                    low(sv_lo[:, :, :], ps[2][:, :].rearrange("p (t m) -> p t m", t=ST), sv_hi[:, :, :])\
                        .then_inc(sb_lo_done, 1)

                def log_rest(h, n):
                    b = ST - 1 - n
                    w = S - b * P
                    k = ST * h + n
                    z = ps[5 + n % 2][:, 0:w]
                    dve.wait_ge(za_done, k + 1)
                    if n >= 2:
                        dve.wait_ge(w_exp_done, k - 1)
                    dve.tensor_scalar(zm[n % 2][:, 0:w], z, scale, 0.0, ALU.mult, ALU.min).then_inc(zm_step, 1)
                    dve.wait_ge(zl_done, k + 1)
                    dve.wait_ge(zm_step, 3 * k + 1)
                    dve.tensor_tensor(zm[n % 2][:, 0:w], zm[n % 2][:, 0:w], za[n % 2][:, 0:w], ALU.subtract)\
                       .then_inc(zm_step, 1)
                    dve.wait_ge(zm_step, 3 * k + 2)
                    dve.scalar_tensor_tensor(lom[n % 2][:, 0:w], z, -scale, zm[n % 2][:, 0:w], ALU.mult, ALU.add)\
                       .then_inc(zm_step, 1)
                    dve.wait_ge(zm_step, 3 * k + 3)
                    dve.tensor_tensor(lom[n % 2][:, 0:P], lom[n % 2][:, 0:P], after[:, P:2 * P], ALU.mult)\
                       .then_inc(lom_done, 1)
                    dve.wait_ge(lom_hi_done, k + 1)
                    low(lom_lo[:, b, b * P:S], lom[n % 2][:, 0:w], lom_hi[:, b, b * P:S]).then_inc(lom_lo_done, 1)

                def weights(h, n):
                    m = n % 2
                    b = ST - 1 - n
                    w = S - b * P
                    k = ST * h + n
                    dve.wait_ge(rest_done, k + 1)
                    dve.tensor_tensor(zm[m][:, 0:w], zm[m][:, 0:w], ps[3 + m][:, 0:w], ALU.add).then_inc(wlog_done, 1)
                    dve.wait_ge(w_exp_done, k + 1)
                    dve.tensor_tensor(ww[m][:, 0:P], ww[m][:, 0:P], after[:, P:2 * P], ALU.mult).then_inc(w_masked, 1)
                    dve.wait_ge(wt_hi_done, k + 1)
                    low(w_lo_t[:, b, b * P:S], ww[m][:, 0:w], w_hi_t[:, b, b * P:S]).then_inc(wt_lo_done, 1)

                def head(h, has_next):
                    log_rest(h, 0)
                    for n in range(1, ST):
                        log_rest(h, n)
                        weights(h, n - 1)
                    if has_next:
                        normed(h + 1)
                    weights(h, 3)
                    if has_next:
                        normed_low(h + 1)
                    dve.wait_ge(sbo_done, h + 1)
                    dve.tensor_copy(eo[:, h, :], ps[7][:, :]).then_inc(raw_done, 1)
                    if has_next:
                        value_low(h + 1)

                dve.wait_ge(masks_r, 2)
                normed(0)
                normed_low(0)
                value_low(0)
                with dve.Fori(0, SB_HEADS - 1) as h:
                    head(h, True)
                head(SB_HEADS - 1, False)
                gate_outputs(0, eo, eo_hi, eo_lo)
                with dve.Fori(0, KT // 2) as i:
                    for j in range(2):
                        used(PAIR_EOUT + 2 * i + j, 1)
                        dve.tensor_tensor(x[:, 2 * i + j, :], x[:, 2 * i + j, :], ps[j][:, :], ALU.add)\
                           .then_inc(x_ready, 1)

            def gate_outputs(n0, raw, out_hi, out_lo):
                with dve.Fori(0, GATED // 2) as i:
                    for j in range(3):
                        n = n0 + 2 * i + j
                        if j < 2:
                            dve.wait_ge(gate_made, n + 1)
                            dve.wait_ge(gated_lo, n + 1)
                            dve.tensor_tensor(gated_o[j][:, :], raw[:, 2 * i + j, :], gate[j][:, :], ALU.mult)\
                               .then_inc(gated_f, 1)
                        if j:
                            dve.wait_ge(gated_hi, n)
                            low(out_lo[:, 2 * i + j - 1, :], gated_o[j - 1][:, :], out_hi[:, 2 * i + j - 1, :])\
                                .then_inc(gated_lo, 1)

            def gla():
                dve.memset(restart[:, :], 1.0).then_inc(gcum_set, 1)
                dve.wait_ge(gcum_set, 1)
                dve.memset(restart[:, 0:S:CH], 0.0).then_inc(gcum_set, 1)
                dve.memset(score[:, :, :], 0.0).then_inc(score_done, 1)
                dve.wait_ge(r_hi_done, 1)
                low(r_lo[:, :], ps[0][:, :], r_hi[:, :]).then_inc(r_lo_done, 1)
                used(PAIR_R, 1)
                for h in range(GLA_HEADS):
                    j = h % 2
                    if h >= 2:
                        dve.wait_ge(gcum_set, h + 1)
                    dve.tensor_scalar(gx[j][:, :], ps[4 + h][:, :], tail_cols[:, 4 + h:5 + h], None, ALU.add)\
                       .then_inc(gx_step, 1)
                    dve.wait_ge(ga_step, 3 * h + 3)
                    dve.scalar_tensor_tensor(gl[j][:, :], gx[j][:, :], 0.0, gl[j][:, :], ALU.min, ALU.subtract)\
                       .then_inc(gcum_set, 1)
                    dve.wait_ge(gcum_set, h + 3)
                    dve.tensor_tensor_scan(gcum[:, h, :], restart[:, :], gl[j][:, :], 0.0, ALU.mult, ALU.add)\
                       .then_inc(gcum_done, 1)
                dve.wait_ge(gcum_done, GLA_HEADS)
                with dve.Fori(0, GLA_HEADS) as h:
                    pair = PAIR_GLA + 3 * h
                    g = gcum[:, h, :].rearrange("p (c t) -> p c t", t=CH)
                    dve.wait_ge(gcum_done, GLA_HEADS)
                    dve.tensor_tensor(gdiff[:, :].rearrange("p (c t) -> p c t", t=CH),
                                      g[:, :, CH - 1:CH].to_broadcast([P, NCH, CH]), g, ALU.subtract).then_inc(gd_done, 1)
                    dve.wait_ge(gexp_done, 4 * h + 4)
                    used(pair, 0)
                    dve.scalar_tensor_tensor(gq[0][:, :], ps[0][:, :], P ** -0.5, gexp[0][:, :], ALU.mult, ALU.mult)\
                       .then_inc(gq_done, 1)
                    used(pair, 1)
                    dve.tensor_tensor(gq[1][:, :], gexp[1][:, :], ps[1][:, :], ALU.mult).then_inc(gq_done, 1)
                    dve.tensor_tensor(gq[2][:, :], gexp[2][:, :], ps[1][:, :], ALU.mult).then_inc(gq_done, 1)
                    for j in range(2):
                        dve.wait_ge(gq_hi_done, 2 * h + j + 1)
                        low(gq_lo[j][:, :], gq[j][:, :], gq_hi[j][:, :]).then_inc(gq_lo_done, 1)
                    dve.wait_ge(kd_hi_done, h + 1)
                    low(kd_lo[:, :, :], ps[0][:, :].rearrange("p (t m) -> p t m", t=ST), kd_hi[:, :, :])\
                        .then_inc(kd_lo_done, 1)
                    dve.wait_ge(small_in, 16 * SMALL)
                    dve.wait_ge(sc_mm, h + 1)
                    dve.copy_predicated(score[:, :, :], keep[:, :].unsqueeze(1).to_broadcast([P, ST, P]),
                                        ps[1][:, :].rearrange("p (t m) -> p t m", t=ST)).then_inc(score_done, 1)
                    dve.wait_ge(score_hi_done, h + 1)
                    low(score_lo[:, :, :], score[:, :, :], score_hi[:, :, :]).then_inc(score_lo_done, 1)
                    for j in range(2):
                        dve.wait_ge(gv_hi_done, 2 * h + j + 1)
                        low(gv_lo[:, :, j * P:(j + 1) * P], ps[2 + j][:, :].rearrange("p (t m) -> p t m", t=ST),
                            gv_hi[:, :, j * P:(j + 1) * P]).then_inc(gv_lo_done, 1)
                    dve.wait_ge(kv_done, h + 1)
                    for c in range(NCH - 1):
                        n = (NCH - 1) * h + c
                        kv = kv_bank(c)
                        new, old = (c + 1) % 2, c % 2
                        if c == 0:
                            dve.tensor_copy(state[new][:, :], kv).then_inc(state_done, 1)
                        else:
                            dve.scalar_tensor_tensor(state[new][:, :], state[old][:, :], gend[:, c:c + 1], kv,
                                                     ALU.mult, ALU.add).then_inc(state_done, 1)
                        dve.wait_ge(state_hi_done, n + 1)
                        low(state_lo[c + 1][:, :], state[new][:, :], state_hi[c + 1][:, :]).then_inc(state_lo_done, 1)
                        dve.wait_ge(state_done, n + 1)
                    dve.wait_ge(grs_step, 2 * h + 2)
                    for d in range(2):
                        dve.scalar_tensor_tensor(go[:, 2 * h + d, :], ps[2 + d][:, :], tail_cols[:, 2 + d:3 + d],
                                                 grs[1][:, :], ALU.mult, ALU.mult).then_inc(raw_done, 1)
                gate_outputs(SB_HEADS, go, go_hi, go_lo)
                with dve.Fori(0, KT // 2) as i:
                    for j in range(2):
                        used(PAIR_OOUT + i, j)
                        dve.tensor_tensor(x[:, 2 * i + j, :], x[:, 2 * i + j, :], ps[j][:, :], ALU.add)\
                           .then_inc(x_ready, 1)

            for s in (unit_used, prod_done, hid_lo, fy_lo_done, mga_done, logit_done, exp_done, pt_lo_done, merged,
                      u_lo_done, zb_done, gated_f, gated_lo):
                dve.sem_inc(s, CREDIT)
            dve.sem_inc(yf_done, 1)
            dve.memset(eps[:, 0:1], EPS)
            dve.memset(eps[:, 1:2], SUB_EPS)
            dve.memset(ones[:, :], 1.0).then_inc(consts_ready, 1)
            dve.wait_ge(small_in, 16 * SMALL)
            dve.wait_ge(table_ready, 1)
            dve.tensor_copy(table[:, 0:512], ps[0][0:N_MAPS, :]).then_inc(table_copied, 1)
            dve.tensor_copy(table[:, 512:REL], ps[1][0:N_MAPS, 0:REL - 512]).then_inc(table_copied, 1)
            half = 2 * DEPTH * HD
            dve.tensor_tensor(lamp[:, :], lamv[:, 0:half], lamv[:, half:2 * half], ALU.mult).then_inc(setup_step, 1)
            dve.wait_ge(setup_step, 1)
            dve.tensor_reduce(lams[:, :], lamp[:, :].rearrange("p (n c) -> p n c", c=HD), AX.X, ALU.add)\
               .then_inc(setup_step, 1)
            for l in range(DEPTH):
                dve.tensor_scalar(sub_gain[:, l:l + 1], sub_gain[:, l:l + 1], 1.0 - LAM_INIT[l], None, ALU.mult)\
                   .then_inc(setup_step, 1)
            dve.wait_ge(masks_r, 3)
            dve.tensor_tensor(lamd[:, :], lame[:, DEPTH:2 * DEPTH], lame[:, 0:DEPTH], ALU.subtract)\
               .then_inc(setup_step, 1)
            dve.wait_ge(setup_step, 3 + DEPTH)
            for l in range(DEPTH):
                dve.tensor_scalar(lam_neg[:, l:l + 1], lamd[:, l:l + 1], -LAM_INIT[l], None, ALU.add)\
                   .then_inc(setup_step, 1)
            dve.wait_ge(setup_step, 3 + 2 * DEPTH)
            dve.wait_ge(x_in, 16)
            dve.sem_inc(x_ready, KT)
            with dve.Fori(0, DEPTH) as l:
                norm(3 * l, 3 * l)
                ffn_up(2 * l, l * PAIRS_LAYER + PAIR_FFN1)
                ffn_down(l * PAIRS_LAYER + PAIR_DOWN1)
                norm(3 * l + 1, 3 * l + 1)
                fourier(l)
                branch_a(l)
                first_head(l)
                dilated(l)
                diff(l)
                merge(l)
                out_projection(l)
                norm(3 * l + 2, 3 * l + 2)
                ffn_up(2 * l + 1, l * PAIRS_LAYER + PAIR_FFN2)
                ffn_down(l * PAIRS_LAYER + PAIR_DOWN2)
            norm(3 * DEPTH, 0, final=True)
            norm(3 * DEPTH + 1, 3 * DEPTH)
            s5()
            stick_breaking()
            norm(3 * DEPTH + 2, 3 * DEPTH + 1)
            gla()


def tiles(w, c0, c1, k0=0, k1=None):
    return w[128 * k0:None if k1 is None else 128 * k1, c0:c1].reshape(-1, P, c1 - c0).transpose(1, 0, 2)


def weight_units(inp):
    units = []

    def unit(*parts):
        u = np.zeros((P, 8, P), np.float32)
        k = 0
        for t in parts:
            u[:, k:k + t.shape[1], :t.shape[2]] = t
            k += t.shape[1]
        units.append(u.reshape(P, UNIT))

    def col(w, c):
        unit(tiles(w, P * c, P * c + P))

    def ffn(gate, up, down):
        for f in range(FT):
            col(gate, f)
            col(up, f)
        for f in range(FT):
            units.append(down[P * f:P * f + P])

    for l in range(DEPTH):
        w_in, w_gate = inp["w_in"][l], inp["w_gate"][l]
        ffn(inp["w_ffn1_gate"][l], inp["w_ffn1_up"][l], inp["w_ffn1_down"][l])
        for g in range(GROUPS):
            col(w_in, g)
        for c in range(KT):
            col(w_gate, c)
            col(inp["w_br_a"][l], c)
        for n in range(N_DH):
            q, k, v = ((GROUPS + n, GROUPS + N_DIL + n, GROUPS + 2 * N_DIL + n) if n < N_DIL else
                       (14 + n, 18 + n, 22 + n))
            for whole, half in ((q, 0), (k, KT // 2)):
                col(w_in, whole)
                unit(tiles(w_in, P * v, P * v + P, half, half + KT // 2))
        for c in range(KT):
            col(w_gate, KT + c)
            col(w_gate, 2 * KT + c)
            unit(tiles(inp["w_br_c"][l], P * c, P * c + P), tiles(inp["w_br_b"][l], P * c, P * c + P))
        for c in range(KT):
            col(inp["w_out"][l], c)
        ffn(inp["w_ffn2_gate"][l], inp["w_ffn2_up"][l], inp["w_ffn2_down"][l])
    even = inp["even_w_in_2"][0]
    q0, k0, v0, z0, u0, zb0 = (n // P for n in (0, D, 2 * D, 3 * D, 4 * D, 4 * D + S5_W))
    for c in range(UT):
        col(even, u0 + c)
    units += s5_tiles(inp)
    for c in range(UT):
        col(even, zb0 + c)
    glu = inp["s5_w_glu_2"][0]
    for c in range(0, UT, 2):
        unit(tiles(glu, P * c, P * c + P), tiles(glu, P * c + P, P * c + 2 * P))
    for h in range(SB_HEADS):
        for c in (q0, k0, v0, z0):
            col(even, c + h)
    for c in range(KT):
        for half in range(2):
            unit(tiles(inp["even_w_out_2"][0], P * c, P * c + P, 6 * half, 6 * half + 6))
    odd = inp["odd_w_in_2"][0]
    key = D // 2
    q0, k0, v0, z0, r0 = (n // P for n in (0, key, 2 * key, 2 * key + D, 2 * key + 2 * D))
    unit(tiles(odd, P * r0, odd.shape[1]))
    wg = np.zeros((P, 8, P), np.float32)
    w = inp["gla_w_gate_2"][0]
    wg[:w.shape[0], :GLA_HEADS] = w.reshape(w.shape[0], GLA_HEADS, P)
    units.append(wg.reshape(P, UNIT))
    for h in range(GLA_HEADS):
        for c in (q0 + h, k0 + h, v0 + 2 * h, v0 + 2 * h + 1, z0 + 2 * h, z0 + 2 * h + 1):
            col(odd, c)
    for c in range(KT):
        col(inp["odd_w_out_2"][0], c)
    return units


def s5_tiles(inp):
    b = [inp[k][0].transpose(0, 2, 1) for k in ("s5_b_re_2", "s5_b_im_2")]
    c = [inp[k][0].transpose(0, 2, 1) for k in ("s5_c_re_2", "s5_c_im_2")]
    out = []
    for i in range(0, NST, 2):
        u = np.zeros((P, 8, P), np.float32)
        for s in range(2):
            for g in range(2):
                group = 2 * (i + s) + g
                ch = slice(S5_GROUP * (group % 8), S5_GROUP * (group % 8) + S5_GROUP)
                st = slice(S5_STATE * g, S5_STATE * g + S5_STATE)
                for n in range(2):
                    u[ch, 4 * s + n, st] = b[n][group]
                    u[st, 4 * s + 2 + n, ch] = c[n][group]
        out.append(u.reshape(P, UNIT))
    return out


def rel_bucket(rel):
    half, exact = BUCKETS // 2, BUCKETS // 4
    n = np.abs(rel)
    large = exact + (np.log(np.maximum(n, 1) / exact) / math.log(1024 / exact) * (half - exact)).astype(int)
    return np.where(rel > 0, half, 0) + np.where(n < exact, n, np.minimum(large, half - 1))


def shape_constants():
    rel = np.arange(REL) - (S - 1)
    onehot = np.zeros((BUCKETS + N_DIL, REL), np.float32)
    onehot[rel_bucket(rel), np.arange(REL)] = 1.0
    flags = np.zeros((N_DIL, N_MAPS), np.float32)
    for g, (window, dil) in enumerate(DIL):
        onehot[BUCKETS + g] = (np.abs(rel) > window // 2) | (rel % dil != 0)
        flags[g, 2 * g:2 * g + 2] = NEG
    tok = 2 * np.pi * (np.outer(np.arange(S), np.arange(S)) % S) / S
    chan = 2 * np.pi * (np.outer(np.arange(P), np.arange(P)) % P) / P
    cols = [np.cos(tok).reshape(ST, P, S).transpose(1, 0, 2).reshape(P, -1),
            np.sin(tok).reshape(ST, P, S).transpose(1, 0, 2).reshape(P, -1), np.cos(chan), -np.sin(chan)]
    return onehot, flags, (np.concatenate(cols, axis=1) / 16).astype(np.float32)


def same_chunk():
    s, t = np.arange(P)[:, None], np.arange(P)[None]
    return ((s // CH == t // CH) & (s <= t)).astype(np.uint32)


def feature_columns(v):
    return np.ascontiguousarray(v.reshape(-1, P).T)


def kernel(**inputs):
    import concourse.bacc as bacc
    from concourse.bass_utils import run_bass_kernel_spmd

    inp = {k: np.asarray(v) for k, v in inputs.items()}
    units = weight_units(inp)
    assert len(units) == 2 * N_PAIRS, (len(units), N_PAIRS)
    onehot, flags, dft = shape_constants()
    gain_rows = [inp[k][l] for l in range(DEPTH) for k in ("g_ffn1", "g_mix", "g_ffn2")]
    gain_rows += [inp["g_final"], inp["even_norm_g_2"][0], inp["odd_norm_g_2"][0]]
    arrays = {
        "x": np.ascontiguousarray(inp["x"][0].T.reshape(KT, P, S).transpose(1, 0, 2)),
        "weights": np.stack(units),
        "gains": feature_columns(np.concatenate(gain_rows)),
        "gate_bias": feature_columns(inp["b_gate"]),
        "ident": np.eye(P, dtype=np.float32),
        "sub_gain": np.ascontiguousarray(inp["subln_g"].T),
        "onehot": onehot,
        "relt": np.concatenate([inp["rel_bias"], flags]),
        "lam": np.concatenate([inp[k].reshape(1, -1) for k in ("lam_q1", "lam_q2", "lam_k1", "lam_k2")], axis=1),
        "dft": dft,
        "s5_in": np.stack([inp["s5_lambda_re_2"][0].reshape(NST, P).T, inp["s5_lambda_im_2"][0].reshape(NST, P).T,
                           np.repeat(inp["s5_log_dt_2"][0], S5_STATE).reshape(NST, P).T], axis=1),
        "s5_cols": np.stack([inp["s5_d_2"][0].reshape(UT, P).T, inp["s5_b_glu_2"][0].reshape(UT, P).T], axis=1),
        "tail_cols": feature_columns(np.concatenate([inp[k][0] for k in (
            "sb_q_norm_g_2", "sb_k_norm_g_2", "gla_o_norm_g_2", "gla_b_gate_2")])),
        "after": np.concatenate([np.tril(np.ones((P, P)), -1), np.triu(np.ones((P, P)), 1)], axis=1).astype(np.float32),
        "keep": same_chunk(),
    }
    nc = bacc.Bacc("TRN2", target_bir_lowering=False, num_devices=1, dynamic_dma_scratch_size=1024)
    a = {n: nc.dram_tensor("in_" + n, v.shape, mybir.dt.from_np(v.dtype), kind="ExternalInput").ap() for n, v in arrays.items()}
    a["out"] = nc.dram_tensor("out", (P, KT, S), F32, kind="ExternalOutput").ap()
    table = nc.dram_tensor("bias_table", (N_MAPS, P, REL), F32, kind="Internal").ap()
    a["table"] = table
    a["toeplitz"] = lambda m: bass.AP(table.tensor, m * (P * REL) + P - 1, [[REL - 1, P], [1, BW]])
    build_program(nc, a)
    r = run_bass_kernel_spmd(nc, [{"in_" + n: v for n, v in arrays.items()}], core_ids=[0])
    out = r.results[0]["out"]
    return np.ascontiguousarray(out.transpose(1, 0, 2).reshape(D, S).T)[None]
```
